# Optimizing a Trainium2 kernel written in Bass

```python
import functools
import jax, jax.numpy as jnp
from jax import lax
import numpy as np

D_MODEL = 1024
BATCH = 1
SEQ = 1024
DEPTH = 1
DEC_BATCH = 8
DEC_SEQ = 16
PAST_LEN = 1024

CHUNK = 64
Q_BLOCK = 2 * CHUNK
N_HEADS = 16
HEAD_DIM = D_MODEL // N_HEADS
ATT_W = N_HEADS * HEAD_DIM
D_RNN = D_MODEL
RNN_BLOCKS = 16
RNN_BW = D_RNN // RNN_BLOCKS
CONV_W = 4
RG_C = 8.0
D_FF = ((8 * D_MODEL // 3 + 255) // 256) * 256
N_BRANCH = 2
N_MOD = 9
MACARON_W = 0.5
EPS = 1e-6
FGT_BIAS_INIT = 3.0
IN_COLS = 2 * D_RNN + 3 * ATT_W + N_HEADS + N_BRANCH * D_MODEL
IN_SPLITS = (D_RNN, 2 * D_RNN, 2 * D_RNN + ATT_W, 2 * D_RNN + 2 * ATT_W, 2 * D_RNN + 3 * ATT_W, 2 * D_RNN + 3 * ATT_W + N_HEADS, 2 * D_RNN + 3 * ATT_W + N_HEADS + D_MODEL)

kernel_name = 'hybrid_rglru_fox_macaron_stream_step'

def rms_norm(x, g):
    xf = x.astype(jnp.float32)
    inv = lax.rsqrt(jnp.mean(xf * xf, axis=-1, keepdims=True) + EPS)
    return (xf * inv).astype(x.dtype) * g

def modulate(h, shift, scale):
    return h * (1 + scale[:, None, :]) + shift[:, None, :]

def ada_mod(c, w, b, n):
    m = jax.nn.silu(c) @ w + b
    return m.reshape(c.shape[0], n, D_MODEL)

def swiglu(h, w1, w3, w2):
    return (jax.nn.silu(h @ w1) * (h @ w3)) @ w2

def ffn_sublayer(x, mod, base, g, w1, w3, w2):
    h = modulate(rms_norm(x, g), mod[:, base], mod[:, base + 1])
    gate = 1 + mod[:, base + 2][:, None, :]
    return x + MACARON_W * gate * swiglu(h, w1, w3, w2)

def causal_conv(x, buf, w, b):
    t = x.shape[1]
    xp = jnp.concatenate([buf.astype(x.dtype), x], axis=1)
    y = b + sum(xp[:, j:j + t] * w[j] for j in range(CONV_W))
    return y, xp[:, xp.shape[1] - (CONV_W - 1):]

def block_diag(x, w, b):
    bsz, t, _ = x.shape
    y = jnp.einsum('btni,nij->btnj', x.reshape(bsz, t, RNN_BLOCKS, RNN_BW), w)
    return y.reshape(bsz, t, D_RNN) + b

def rg_lru(x, h0, wa, ba, wx, bx, lam):
    f32 = jnp.float32
    r = jax.nn.sigmoid(block_diag(x, wa, ba).astype(f32))
    i = jax.nn.sigmoid(block_diag(x, wx, bx).astype(f32))
    log_a = -RG_C * r * jax.nn.softplus(-lam.astype(f32))
    a = jnp.exp(log_a)
    u = jnp.sqrt(-jnp.expm1(2.0 * log_a)) * (i * x.astype(f32))

    def step(h, au):
        a_t, u_t = au
        h = a_t * h + u_t
        return h, h

    h_last, hs = lax.scan(step, h0.astype(f32), (jnp.swapaxes(a, 0, 1), jnp.swapaxes(u, 0, 1)))
    return jnp.swapaxes(hs, 0, 1).astype(x.dtype), h_last

def fox_prompt(q, k, v, logf):
    s_len = q.shape[1]
    ft = jnp.swapaxes(jnp.cumsum(logf, axis=1), 1, 2)
    scale = HEAD_DIM ** -0.5
    outs = []
    for blk in range(s_len // Q_BLOCK):
        q0, q1 = blk * Q_BLOCK, (blk + 1) * Q_BLOCK
        s = jnp.einsum('bqhd,bkhd->bhqk', q[:, q0:q1], k[:, :q1]).astype(jnp.float32) * scale
        s = s + ft[:, :, q0:q1, None] - ft[:, :, None, :q1]
        mask = jnp.arange(q1)[None, :] <= jnp.arange(q0, q1)[:, None]
        p = jax.nn.softmax(jnp.where(mask, s, -jnp.inf), axis=-1)
        outs.append(jnp.einsum('bhqk,bkhd->bqhd', p.astype(v.dtype), v[:, :q1]))
    return jnp.concatenate(outs, axis=1)

def fox_sample(q, k, v, logf, cache_k, cache_v, cache_logf):
    past, t = cache_k.shape[1], q.shape[1]
    kk = jnp.concatenate([cache_k.astype(k.dtype), k], axis=1)
    vv = jnp.concatenate([cache_v.astype(v.dtype), v], axis=1)
    lf = jnp.concatenate([cache_logf.astype(jnp.float32), logf], axis=1)
    ft = jnp.swapaxes(jnp.cumsum(lf, axis=1), 1, 2)
    s = jnp.einsum('bqhd,bkhd->bhqk', q, kk).astype(jnp.float32) * (HEAD_DIM ** -0.5)
    s = s + ft[:, :, past:, None] - ft[:, :, None, :]
    mask = jnp.arange(past + t)[None, :] <= (past + jnp.arange(t))[:, None]
    p = jax.nn.softmax(jnp.where(mask, s, -jnp.inf), axis=-1)
    return jnp.einsum('bhqk,bkhd->bqhd', p.astype(vv.dtype), vv)

def mixer_sublayer(x, mod, p, conv_buf, h0, attend):
    bsz, t, _ = x.shape
    h = modulate(rms_norm(x, p['norm']), mod[:, 3], mod[:, 4])
    xr, gr, q, k, v, fl, ga, gb = jnp.split(h @ p['w_in'], IN_SPLITS, axis=-1)
    xc, new_buf = causal_conv(xr, conv_buf, p['conv_w'], p['conv_b'])
    y_rnn, h_last = rg_lru(xc, h0, p['rg_wa'], p['rg_ba'], p['rg_wx'], p['rg_bx'], p['rg_lam'])
    a_out = jax.nn.gelu(gr) * y_rnn
    logf = jax.nn.log_sigmoid(fl.astype(jnp.float32) + p['b_fgt'].astype(jnp.float32))
    heads = (bsz, t, N_HEADS, HEAD_DIM)
    k = k.reshape(heads)
    v = v.reshape(heads)
    att = attend(q.reshape(heads), k, v, logf).reshape(bsz, t, ATT_W)
    z = jax.nn.sigmoid(ga) * (a_out @ p['w_br_rnn']) + jax.nn.sigmoid(gb) * (att @ p['w_br_att'])
    x = x + (1 + mod[:, 5][:, None, :]) * (z @ p['w_out'])
    return x, k, v, logf, new_buf, h_last

def setup_inputs(seed: int = 0) -> dict:
    key = jax.random.key(seed)
    ks = iter(jax.random.split(key, 48))
    f32 = jnp.float32
    L = DEPTH

    def nrm(shape, s):
        return jax.random.normal(next(ks), shape, f32) * s

    x_prompt = nrm((BATCH, SEQ, D_MODEL), 1.0)
    x_sample = nrm((DEC_BATCH, DEC_SEQ, D_MODEL), 1.0)
    cache_k = nrm((L, DEC_BATCH, PAST_LEN, N_HEADS, HEAD_DIM), 1.0)
    cache_v = nrm((L, DEC_BATCH, PAST_LEN, N_HEADS, HEAD_DIM), 1.0)
    cache_logf = jax.nn.log_sigmoid(nrm((L, DEC_BATCH, PAST_LEN, N_HEADS), 1.0) + FGT_BIAS_INIT)
    state_conv = nrm((L, DEC_BATCH, CONV_W - 1, D_RNN), 1.0)
    state_rglru = nrm((L, DEC_BATCH, D_RNN), 0.5)
    c_prompt = nrm((BATCH, D_MODEL), 1.0)
    c_sample = nrm((DEC_BATCH, D_MODEL), 1.0)
    w_ada = nrm((L, D_MODEL, N_MOD * D_MODEL), 0.2 * D_MODEL ** -0.5)
    b_ada = nrm((L, N_MOD * D_MODEL), 0.01)
    ffn1_norm = 1.0 + nrm((L, D_MODEL), 0.02)
    ffn1_w1 = nrm((L, D_MODEL, D_FF), D_MODEL ** -0.5)
    ffn1_w3 = nrm((L, D_MODEL, D_FF), D_MODEL ** -0.5)
    ffn1_w2 = nrm((L, D_FF, D_MODEL), D_FF ** -0.5)
    mix_norm = 1.0 + nrm((L, D_MODEL), 0.02)
    w_in = nrm((L, D_MODEL, IN_COLS), D_MODEL ** -0.5)
    b_fgt = FGT_BIAS_INIT + nrm((L, N_HEADS), 1.0)
    conv_w = nrm((L, CONV_W, D_RNN), CONV_W ** -0.5)
    conv_b = nrm((L, D_RNN), 0.01)
    rg_wa = nrm((L, RNN_BLOCKS, RNN_BW, RNN_BW), RNN_BW ** -0.5)
    rg_ba = nrm((L, D_RNN), 0.01)
    rg_wx = nrm((L, RNN_BLOCKS, RNN_BW, RNN_BW), RNN_BW ** -0.5)
    rg_bx = nrm((L, D_RNN), 0.01)
    a0 = jax.random.uniform(next(ks), (L, D_RNN), f32, 0.9, 0.999)
    pa = a0 ** (1.0 / RG_C)
    rg_lam = jnp.log(pa) - jnp.log1p(-pa)
    w_br_rnn = nrm((L, D_RNN, D_MODEL), D_RNN ** -0.5)
    w_br_att = nrm((L, ATT_W, D_MODEL), ATT_W ** -0.5)
    w_out = nrm((L, D_MODEL, D_MODEL), D_MODEL ** -0.5)
    ffn2_norm = 1.0 + nrm((L, D_MODEL), 0.02)
    ffn2_w1 = nrm((L, D_MODEL, D_FF), D_MODEL ** -0.5)
    ffn2_w3 = nrm((L, D_MODEL, D_FF), D_MODEL ** -0.5)
    ffn2_w2 = nrm((L, D_FF, D_MODEL), D_FF ** -0.5)
    final_norm = 1.0 + nrm((D_MODEL,), 0.02)
    w_ada_f = nrm((D_MODEL, 2 * D_MODEL), 0.2 * D_MODEL ** -0.5)
    b_ada_f = nrm((2 * D_MODEL,), 0.01)
    return {'x_prompt': x_prompt, 'x_sample': x_sample, 'cache_k': cache_k, 'cache_v': cache_v,
            'cache_logf': cache_logf, 'state_conv': state_conv, 'state_rglru': state_rglru,
            'c_prompt': c_prompt, 'c_sample': c_sample, 'w_ada': w_ada, 'b_ada': b_ada,
            'ffn1_norm': ffn1_norm, 'ffn1_w1': ffn1_w1, 'ffn1_w3': ffn1_w3, 'ffn1_w2': ffn1_w2,
            'mix_norm': mix_norm, 'w_in': w_in, 'b_fgt': b_fgt, 'conv_w': conv_w, 'conv_b': conv_b,
            'rg_wa': rg_wa, 'rg_ba': rg_ba, 'rg_wx': rg_wx, 'rg_bx': rg_bx, 'rg_lam': rg_lam,
            'w_br_rnn': w_br_rnn, 'w_br_att': w_br_att, 'w_out': w_out,
            'ffn2_norm': ffn2_norm, 'ffn2_w1': ffn2_w1, 'ffn2_w3': ffn2_w3, 'ffn2_w2': ffn2_w2,
            'final_norm': final_norm, 'w_ada_f': w_ada_f, 'b_ada_f': b_ada_f}

def reference(x_prompt, x_sample, cache_k, cache_v, cache_logf, state_conv, state_rglru,
              c_prompt, c_sample, w_ada, b_ada, ffn1_norm, ffn1_w1, ffn1_w3, ffn1_w2,
              mix_norm, w_in, b_fgt, conv_w, conv_b, rg_wa, rg_ba, rg_wx, rg_bx, rg_lam,
              w_br_rnn, w_br_att, w_out, ffn2_norm, ffn2_w1, ffn2_w3, ffn2_w2,
              final_norm, w_ada_f, b_ada_f):
    xp, xs = x_prompt, x_sample
    bp = x_prompt.shape[0]
    kp_l, vp_l, lp_l, cp_l, hp_l = [], [], [], [], []
    ks_l, vs_l, ls_l, cs_l, hs_l = [], [], [], [], []
    for l in range(DEPTH):
        mp = ada_mod(c_prompt, w_ada[l], b_ada[l], N_MOD)
        ms = ada_mod(c_sample, w_ada[l], b_ada[l], N_MOD)
        xp = ffn_sublayer(xp, mp, 0, ffn1_norm[l], ffn1_w1[l], ffn1_w3[l], ffn1_w2[l])
        xs = ffn_sublayer(xs, ms, 0, ffn1_norm[l], ffn1_w1[l], ffn1_w3[l], ffn1_w2[l])
        p = {'norm': mix_norm[l], 'w_in': w_in[l], 'b_fgt': b_fgt[l], 'conv_w': conv_w[l],
             'conv_b': conv_b[l], 'rg_wa': rg_wa[l], 'rg_ba': rg_ba[l], 'rg_wx': rg_wx[l],
             'rg_bx': rg_bx[l], 'rg_lam': rg_lam[l], 'w_br_rnn': w_br_rnn[l],
             'w_br_att': w_br_att[l], 'w_out': w_out[l]}
        buf0 = jnp.zeros((bp, CONV_W - 1, D_RNN), xp.dtype)
        h00 = jnp.zeros((bp, D_RNN), jnp.float32)
        xp, kp, vp, lp, cp, hp = mixer_sublayer(xp, mp, p, buf0, h00, fox_prompt)
        attend_s = functools.partial(fox_sample, cache_k=cache_k[l], cache_v=cache_v[l],
                                     cache_logf=cache_logf[l])
        xs, ks_, vs_, ls_, cs_, hs_ = mixer_sublayer(xs, ms, p, state_conv[l], state_rglru[l], attend_s)
        xp = ffn_sublayer(xp, mp, 6, ffn2_norm[l], ffn2_w1[l], ffn2_w3[l], ffn2_w2[l])
        xs = ffn_sublayer(xs, ms, 6, ffn2_norm[l], ffn2_w1[l], ffn2_w3[l], ffn2_w2[l])
        kp_l.append(kp); vp_l.append(vp); lp_l.append(lp); cp_l.append(cp); hp_l.append(hp)
        ks_l.append(ks_); vs_l.append(vs_); ls_l.append(ls_); cs_l.append(cs_); hs_l.append(hs_)
    mfp = ada_mod(c_prompt, w_ada_f, b_ada_f, 2)
    mfs = ada_mod(c_sample, w_ada_f, b_ada_f, 2)
    y_prompt = modulate(rms_norm(xp, final_norm), mfp[:, 0], mfp[:, 1])
    y_sample = modulate(rms_norm(xs, final_norm), mfs[:, 0], mfs[:, 1])
    return (y_prompt, y_sample,
            jnp.stack(kp_l), jnp.stack(vp_l), jnp.stack(lp_l), jnp.stack(cp_l), jnp.stack(hp_l),
            jnp.stack(ks_l), jnp.stack(vs_l), jnp.stack(ls_l), jnp.stack(cs_l), jnp.stack(hs_l))


_drawn_inputs = setup_inputs


def setup_inputs(seed=0):
    import zlib

    import numpy as np

    out = dict(_drawn_inputs(seed))
    spreads = {}
    factors = {'cache_logf': 26.264,
     'ffn1_norm': 6.285,
     'mix_norm': 2.849,
     'rg_ba': 31.091,
     'rg_bx': 26.292,
     'ffn2_norm': 6.966,
     'final_norm': 7.543,
     'b_ada_f': 4.117,
     'cache_k': 3.607,
     'cache_v': 4.208,
     'conv_b': 2.909}
    for name, (base, spread) in spreads.items():
        noise = np.random.default_rng([zlib.crc32(name.encode()), seed]).standard_normal(out[name].shape)
        drawn = base * np.exp(spread * noise) if base else spread * noise
        out[name] = __import__('jax').numpy.asarray(drawn.astype(out[name].dtype))
    for name, factor in factors.items():
        out[name] = (out[name] * factor).astype(out[name].dtype)
    return out
```

```python
import numpy as np
from contextlib import ExitStack

import concourse.bass as bass
from concourse import mybir

F32 = mybir.dt.float32
F32R = mybir.dt.float32r
ALU = mybir.AluOpType
ACT = mybir.ActivationFunctionType
AX = mybir.AxisListType

D = 1024
TP, SB, ST = 1024, 8, 16
TS = SB * ST
T = TP + TS
PAST = 1024
H, HD = 16, 64
KT = D // 128
CH = 384
NC = T // CH
CP = TP - (NC - 1) * CH
DFF = 2816
FF_PAIRS = DFF // 256
NMOD = 11
NSEQ = 1 + SB
CONV_W = 4
EPS = 1e-6
MASKED = -float(2 ** 100)
CREDIT = 4
ds = bass.ds


def tokens_of(chunk):
    return slice(chunk * CH, (chunk + 1) * CH)


def build(nc, a, o):
    with ExitStack() as ctx:
        program(nc, ctx, a, o)


def program(nc, ctx, a, o):
    def sb(stack, name, shape, dt=F32):
        return stack.enter_context(nc.sbuf_tensor(name, shape, dt))

    S = {}

    def sem(name):
        if name not in S:
            S[name] = ctx.enter_context(nc.semaphore(name))
        return S[name]

    psum = ctx.enter_context(nc.psum_tensor("psum", [128, 8 * 512], F32))
    ps = [psum[:, 512 * n:512 * n + 512] for n in range(8)]

    acts_hi = sb(ctx, "acts_hi", [128, KT, T], F32R)
    acts_lo = sb(ctx, "acts_lo", [128, KT, T], F32R)
    w_raw = [sb(ctx, f"w_raw{n}", [128, 2048]) for n in range(2)]
    w_hi = [sb(ctx, f"w_hi{n}", [128, 2048], F32R) for n in range(2)]
    w_lo = [sb(ctx, f"w_lo{n}", [128, 2048], F32R) for n in range(2)]
    mods = sb(ctx, "mods", [128, NMOD, KT, NSEQ])
    params = sb(ctx, "params", [128, 88 + 96])
    ident = sb(ctx, "ident", [128, 128])
    ones = sb(ctx, "ones", [128, 128])
    sum_rows = sb(ctx, "sum_rows", [2 * NSEQ, NSEQ])
    eps_col = sb(ctx, "eps_col", [128, 1])
    conv_state = sb(ctx, "conv_state", [128, SB * 3 * KT])
    h0 = sb(ctx, "h0", [128, SB * KT])
    states = sb(ctx, "states", [128, KT, 36])
    sp4 = sb(ctx, "sp4", [128, KT])
    lam_t = [sb(ctx, f"lam_t{n}", [128, KT]) for n in range(4)]
    past_last = sb(ctx, "past_last", [128, 1])
    tiny_col = sb(ctx, "tiny_col", [128, 1])
    wait_mark = sb(ctx, "wait_mark", [1, 2])
    b_fgt_col = sb(ctx, "b_fgt_col", [H, 1])
    wfl_hi = sb(ctx, "wfl_hi", [128, KT, H], F32R)
    wfl_lo = sb(ctx, "wfl_lo", [128, KT, H], F32R)
    new_logf = sb(ctx, "new_logf", [128, ST])
    new_f = sb(ctx, "new_f", [128, ST])
    ident_r = sb(ctx, "ident_r", [128, 128], F32R)
    causal_r = sb(ctx, "causal_r", [128, 128], F32R)
    pick_r = sb(ctx, "pick_r", [ST, 128], F32R)
    G_FFN1, G_MIX, G_FFN2, G_FINAL, G_CONVW, G_CONVB, G_BA, G_BX, G_LAM = (
        88, 96, 104, 112, 120, 152, 160, 168, 176)

    set2 = ExitStack()
    w_hi.append(sb(set2, "w_hi2", [128, 2048], F32R))
    w_lo.append(sb(set2, "w_lo2", [128, 2048], F32R))
    xs = ExitStack()
    x = sb(xs, "x", [128, KT, T])

    setup = ExitStack()
    x_rows = [sb(setup, f"x_rows{n}", [128, D]) for n in range(2)]
    vec_rows = [sb(setup, "vec_rows0", [88, 128]), sb(setup, "vec_rows1", [96, 128])]
    c_rows = sb(setup, "c_rows", [NSEQ, D])
    cT = sb(setup, "cT", [128, KT, 2 * NSEQ], F32R)
    mod_rows = [sb(setup, f"mod_rows{n}", [2 * NSEQ, 256]) for n in range(2)]
    state_rows = [sb(setup, "h0_rows", [SB * KT, 128])] + [sb(setup, f"conv_rows{n}", [96, 128]) for n in range(2)]
    wfl_raw = sb(setup, "wfl_raw", [128, KT, H])
    mask_f = sb(setup, "mask_f", [128, 128])
    past_rows = sb(setup, "past_rows", [128, PAST // 128, SB * H])
    setup.close()

    normf = ExitStack()
    xn = [sb(normf, f"xn{n}", [128, KT, CH]) for n in range(2)]
    inv = sb(normf, "inv", [128, CH])
    normf.close()

    ffnf = ExitStack()
    u_hi = sb(ffnf, "u_hi", [128, 2, T], F32R)
    u_lo = sb(ffnf, "u_lo", [128, 2, T], F32R)
    gated = [sb(ffnf, f"gated{n}", [128, CH]) for n in range(2)]
    u_f = [sb(ffnf, f"u_f{n}", [128, CH]) for n in range(2)]
    s_tmp = [sb(ffnf, f"s_tmp{n}", [128, SB, ST]) for n in range(2)]
    ffnf.close()

    finalf = ExitStack()
    xf = sb(finalf, "xf", [128, KT, CH])
    inv_f = sb(finalf, "inv_f", [128, CH])
    y_rows = [sb(finalf, f"y_rows{n}", [128, D]) for n in range(2)]
    finalf.close()
    xs.close()

    projf = ExitStack()
    st = [sb(projf, f"st{n}", [128, T]) for n in range(2)]
    tok = [sb(projf, f"tok{n}", [128, 3, 128]) for n in range(2)]
    lft = sb(projf, "lft", [128, T // 128, H])
    rnnf = ExitStack()
    PAD = CONV_W - 1
    XP = PAD + TP
    xpad = [sb(rnnf, f"xpad{n}", [128, XP + SB * (PAD + ST)]) for n in range(2)]
    xc = [sb(rnnf, f"xc{n}", [128, T]) for n in range(2)]
    rt = [sb(rnnf, f"rt{n}", [128, T]) for n in range(2)]
    it = [sb(rnnf, f"it{n}", [128, T]) for n in range(2)]
    gl = [sb(rnnf, f"gl{n}", [128, T]) for n in range(2)]
    bd = sb(rnnf, "bd", [128, 4, 128])
    tmp8 = [sb(rnnf, f"tmp8_{n}", [128, SB]) for n in range(2)]
    gate_p = sb(rnnf, "gate_p", [128, 2, 3])
    rnnf.close()
    brrf = ExitStack()
    a_stage = sb(brrf, "a_stage", [128, KT, T])
    state_out = sb(brrf, "state_out", [36, D])
    lf16 = sb(brrf, "lf16", [ST, 128])
    brrf.close()
    projf.close()
    set2.close()

    patf = ExitStack()
    kf = sb(patf, "kf", [128, TP])
    qf = sb(patf, "qf", [128, TP])
    k_hi = [sb(patf, f"k_hi{n}", [128, TP], F32R) for n in range(2)]
    k_lo = [sb(patf, f"k_lo{n}", [128, TP], F32R) for n in range(2)]
    q_hl = [sb(patf, f"q_hl{n}", [128, TP], F32R) for n in range(2)]
    vh = [sb(patf, f"vh{n}", [128, TP // 128, HD]) for n in range(2)]
    kbias = [sb(patf, f"kbias{n}", [128, TP]) for n in range(2)]
    pr = [sb(patf, f"pr{n}", [128, TP]) for n in range(4)]
    pT = [sb(patf, f"pT{n}", [128, TP]) for n in range(2)]
    att = sb(patf, "att", [128, TP // 128, 128])
    stat = sb(patf, "stat", [128, 4, 4])
    patf.close()

    satf = ExitStack()
    NEWK = PAST // 128
    kc = [sb(satf, f"kc{n}", [128, NEWK, 512]) for n in range(2)]
    vc = sb(satf, "vc", [128, NEWK, 512])
    kTs = [sb(satf, f"kTs{n}", [128, PAST]) for n in range(2)]
    kn = [sb(satf, f"kn{n}", [128, 4, ST]) for n in range(2)]
    vn = [sb(satf, f"vn{n}", [ST, 512]) for n in range(2)]
    qd = [sb(satf, f"qd{n}", [128, 4, 2 * ST]) for n in range(2)]
    sp = [sb(satf, f"sp{n}", [128, PAST + ST]) for n in range(2)]
    spT = sb(satf, "spT", [128, NEWK + 1, 128])
    sstat = sb(satf, "sstat", [128, 2, 4])
    satf.close()

    zf = ExitStack()
    zt = [sb(zf, f"z{n}", [128, T]) for n in range(3)]
    gb_t = [sb(zf, "gb_t0", [128, CH])]
    zpad = sb(zf, "zpad", [128, 4096 - 3 * T - CH])
    x2 = sb(zf, "x_again", [128, KT, T])
    zt += [sb(zf, f"z{n}", [128, T]) for n in range(3, KT)]
    gb_t.append(sb(zf, "gb_t1", [128, CH]))
    zf.close()

    NORMS_BEFORE = 3
    N_ADA = 4 * NMOD
    B_FFN1 = N_ADA
    B_PROJ = B_FFN1 + 3 * FF_PAIRS
    N_PROJ = 28
    B_BRR = B_PROJ + N_PROJ
    B_BRA = B_BRR + 4
    B_OUT = B_BRA + 4
    B_FFN2 = B_OUT + 4
    ADA_SLOTS = [(0, 2, 0, 2), (1, 2, 1, 2)]
    FFN_SLOTS = [(0, 1, 2, 3), (1, 2, 0, 3), (0, 2, 1, 3)]
    PROJ_SLOTS = [(0, 1, 2, 3), (1, 2, 0, 2), (0, 2, 1, 3), (1, 2, 2, 3), (0, 2, 0, 3), (1, 2, 1, 3), (0, 2, 0, 2)]
    BRR_SLOTS = [(0, 1, 2, 3), (1, 2, 1, 3), (0, 2, 0, 3), (1, 2, 1, 2)]
    PAIR_SLOTS = [(0, 2, 0, 2), (1, 2, 1, 2)]

    ADA_RAWS = (0, 0)
    FFN1_RAWS = (N_ADA // 2, N_ADA // 2)
    PROJ_RAWS = (FFN1_RAWS[0] + 2 * FF_PAIRS, FFN1_RAWS[1] + FF_PAIRS)
    BRR_RAWS = (PROJ_RAWS[0] + 16, PROJ_RAWS[1] + 12)
    BRA_RAWS = (BRR_RAWS[0] + 2, BRR_RAWS[1] + 2)
    OUT_RAWS = (BRA_RAWS[0] + 2, BRA_RAWS[1] + 2)
    FFN2_RAWS = (OUT_RAWS[0] + 2, OUT_RAWS[1] + 2)

    def load_block(eng, block, slot, source):
        raw, ago, _, _ = slot
        eng.wait_ge(sem("w_lo_done"), block - ago + 1 + CREDIT)
        eng.dma_start(w_raw[raw][:].rearrange("p (k n) -> p k n", n=source.shape[-1]), source).then_inc(
            sem(f"w_raw_loaded{raw}"), 16)

    def split_hi(eng, block, slot, loads_before):
        raw, _, st, ago = slot
        eng.wait_ge(sem(f"w_raw_loaded{raw}"), 16 * (loads_before + 1))
        eng.wait_ge(sem("w_used"), block - ago + 1 + CREDIT)
        eng.activation(w_hi[st][:], w_raw[raw][:], ACT.Copy).then_inc(sem("w_hi_done"), 1)

    def split_lo(eng, block, slot):
        raw, _, st, _ = slot
        eng.wait_ge(sem("w_hi_done"), block + 1)
        eng.tensor_tensor(w_lo[st][:], w_raw[raw][:], w_hi[st][:].bitcast(F32), ALU.subtract).then_inc(
            sem("w_lo_done"), 1)

    def wait_block(eng, block):
        eng.wait_ge(sem("w_lo_done"), block + 1 + CREDIT)

    def mm3(eng, out, whi, wlo, ahi, alo, first, last, opens=None):
        pass1 = eng.matmul(out, whi, ahi, start=first, stop=False)
        if opens is not None:
            pass1.then_inc(opens, 1)
        eng.matmul(out, whi, alo, start=False, stop=False)
        return eng.matmul(out, wlo, ahi, start=False, stop=last)

    def wcols(st, tile):
        h = w_hi[st][:].rearrange("p (k n) -> p k n", n=256)
        l = w_lo[st][:].rearrange("p (k n) -> p k n", n=256)
        return [h[:, k, 128 * tile:128 * tile + 128] for k in range(KT)], [l[:, k, 128 * tile:128 * tile + 128] for k in range(KT)]

    def kview(w):
        return w.rearrange("(k p) n -> p k n", p=128)

    w_ada_v = kview(a["w_ada"][0])
    w_adaf_v = kview(a["w_ada_f"])

    def scratch(name, shape):
        return nc.dram_tensor(name, shape, F32, kind="Internal").ap()

    x_dram = scratch("x_spill", [128, KT * T])
    q_dram, k_dram, a_dram, ga_dram, gb_dram, z1_dram = (
        scratch(name, [D, T]) for name in ("q_t", "k_t", "a_t", "gate_a_t", "gate_b_t", "z1_t"))
    bias_dram = scratch("prompt_bias", [H, TP])
    past_dram = scratch("sample_bias", [SB * H, PAST + ST])
    COL_XR, COL_GR, COL_Q, COL_K, COL_V, COL_FL = (D * n for n in range(6))
    COL_GA, COL_GB = COL_FL + H, COL_FL + H + D

    def minus_sums(eng, out, logf, initial):
        return eng.tensor_tensor_scan(out, ones[0:out.shape[0], 0:1].to_broadcast(list(out.shape)), logf, initial,
                                      ALU.mult, ALU.subtract)

    LOG1P_STEPS = 8

    def log1p_scalar(eng, u, name):
        eng.wait_ge(sem(name + "_dve"), 2)
        eng.activation(u, u, ACT.Ln).then_inc(sem(name + "_act"), 1)

    def log1p_vector(eng, tiles, name, e_ready):
        e, u, d, flag = tiles
        dve, act = sem(name + "_dve"), sem(name + "_act")
        eng.wait_ge(act, e_ready)
        eng.tensor_scalar(u, e, 1.0, None, ALU.add).then_inc(dve, 1)
        eng.wait_ge(dve, 1)
        eng.tensor_scalar(d, u, -1.0, None, ALU.add).then_inc(dve, 1)
        eng.wait_ge(dve, 2)
        eng.tensor_scalar(flag, d, 0.0, None, ALU.is_equal).then_inc(dve, 1)
        eng.wait_ge(dve, 3)
        eng.tensor_tensor(d, d, flag, ALU.add).then_inc(dve, 1)
        eng.wait_ge(dve, 4)
        eng.reciprocal(d, d).then_inc(dve, 1)
        eng.wait_ge(act, e_ready + 1)
        eng.tensor_tensor(u, u, flag, ALU.add).then_inc(dve, 1)
        eng.wait_ge(dve, 6)
        eng.tensor_tensor(u, u, d, ALU.mult).then_inc(dve, 1)
        eng.wait_ge(dve, 7)
        eng.tensor_tensor(e, e, u, ALU.mult).then_inc(dve, 1)
        eng.wait_ge(dve, 8)

    def setup_sync(eng):
        for n in range(2):
            rows = (["b_ada", "b_ada_f"], ["ffn1_norm", "mix_norm", "ffn2_norm", "final_norm", "conv_w",
                                           "conv_b", "rg_ba", "rg_bx", "rg_lam"])[n]
            at = 0
            for name in rows:
                v = a[name]
                v = {1: lambda v: v.rearrange("(r c) -> r c", c=128),
                     2: lambda v: v.rearrange("l (r c) -> (l r) c", c=128),
                     3: lambda v: v.rearrange("l w (r c) -> (l w r) c", c=128)}[len(v.shape)](v)
                eng.dma_start(vec_rows[n][at:at + v.shape[0], :], v).then_inc(sem("vec_loaded"), 16)
                at += v.shape[0]
        eng.dma_start(c_rows[0:1, :], a["c_prompt"]).then_inc(sem("c_loaded"), 16)
        eng.dma_start(c_rows[1:NSEQ, :], a["c_sample"]).then_inc(sem("c_loaded"), 16)
        xp = a["x_prompt"][0].rearrange("(m p) d -> m p d", p=128)
        with eng.Fori(0, TP // 256) as i:
            for k in range(2):
                eng.wait_ge(sem("x_turned"), i * 4 + 2 * k - 2 + CREDIT)
                eng.dma_start(x_rows[k][:], xp[i * 2 + k]).then_inc(sem(f"x_rows_loaded{k}"), 16)
        eng.wait_ge(sem("x_turned"), 14 + CREDIT)
        eng.dma_start(x_rows[0][:], a["x_sample"].rearrange("s t d -> (s t) d")).then_inc(sem("x_rows_loaded0"), 16)
        eng.dma_start(state_rows[0][:], a["state_rglru"].rearrange("l s (r c) -> (l s r) c", c=128)).then_inc(sem("state_loaded"), 16)
        conv_src = a["state_conv"].rearrange("l s j (r c) -> (l s j r) c", c=128)
        for n in range(2):
            eng.dma_start(state_rows[1 + n][:], conv_src[96 * n:96 * n + 96, :]).then_inc(sem("state_loaded"), 16)
        eng.dma_start(wfl_raw[:], kview(a["w_in"][0])[:, :, COL_FL:COL_FL + H]).then_inc(sem("fl_loaded"), 16)
        eng.dma_start(b_fgt_col[:], a["b_fgt"].rearrange("l h -> h l")).then_inc(sem("fl_loaded"), 16)
        for b in range(SB):
            eng.dma_start(past_rows[:, :, H * b:H * b + H], a["cache_logf"][0, b].rearrange("(k p) h -> p k h", p=128)).then_inc(sem("past_loaded"), 16)
        eng.wait_ge(sem("bank7_moved"), 3)
        eng.dma_start(past_dram[:, 0:PAST], past_rows[:].rearrange("p k n -> p (k n)")).then_inc(sem("past_stored"), 16)
        def ada(mod0, n, view):
            with eng.Fori(0, n) as i:
                for q in range(4):
                    load_block(eng, (i + mod0) * 4 + q, ADA_SLOTS[q % 2],
                               view[:, :, ds(i * D + q * 256, 256)])
        ada(0, 9, w_ada_v)
        ada(9, 2, w_adaf_v)

    def setup_scalar(eng):
        eng.sem_inc(sem("proj_free"), 6)
        eng.sem_inc(sem("tok_moved"), 2)
        eng.sem_inc(sem("ri_moved"), 2)
        for n in range(2):
            eng.sem_inc(sem(f"tok_stored{n}"), 16)
            eng.sem_inc(sem(f"st_stored{n}"), 16)
            eng.sem_inc(sem(f"a_stored{n}"), 16)
        eng.wait_ge(sem("c_loaded"), 32)
        eng.activation(c_rows[:], c_rows[:], ACT.Silu).then_inc(sem("c_act"), 1)
        eng.wait_ge(sem("setup_turned"), 2)
        eng.activation(cT[:, :, 0:NSEQ], ps[4][:, 0:KT * NSEQ].rearrange("p (k s) -> p k s", k=KT),
                       ACT.Copy).then_inc(sem("c_act"), 1)
        eng.wait_ge(sem("const"), CONSTS)
        eng.activation(ident_r[:], ident[:], ACT.Copy).then_inc(sem("const_split"), 1)
        eng.wait_ge(sem("const"), CONSTS + 2)
        eng.activation(causal_r[:], mask_f[:], ACT.Copy).then_inc(sem("const_split"), 1)
        eng.wait_ge(sem("const"), CONSTS + 4)
        eng.activation(pick_r[:], mask_f[0:ST, :], ACT.Copy).then_inc(sem("const_split"), 1)
        eng.wait_ge(sem("fl_loaded"), 32)
        eng.activation(wfl_hi[:], wfl_raw[:], ACT.Copy).then_inc(sem("const_split"), 1)
        eng.wait_ge(sem("params_ready"), 1)
        eng.activation(lam_t[0][:], params[:, G_LAM:G_LAM + KT], ACT.Abs).then_inc(sem("lam_act"), 1)
        eng.wait_ge(sem("lam_act"), 1)
        eng.activation(lam_t[0][:], lam_t[0][:], ACT.Exp, scale=-1.0).then_inc(sem("lam_act"), 1)
        log1p_scalar(eng, lam_t[1][:], "lam")
        with eng.Fori(0, NMOD) as i:
            for q in range(4):
                split_hi(eng, i * 4 + q, ADA_SLOTS[q % 2], i * 2 + q // 2)

    def setup_gpsimd(eng):
        eng.sem_inc(sem("w_lo_done"), CREDIT)
        eng.memset(ident[:], 0.0).then_inc(sem("const"), 1)
        eng.memset(ones[:], 1.0).then_inc(sem("const"), 1)
        eng.memset(sum_rows[:], 0.0).then_inc(sem("const"), 1)
        eng.memset(eps_col[:], EPS).then_inc(sem("const"), 1)
        eng.wait_ge(sem("const"), 4)
        eng.affine_select(out=ident[:], in_=ident[:], compare_op=ALU.not_equal, fill=1.0, base=0,
                          pattern=[[-1, 128]], channel_multiplier=1).then_inc(sem("const"), 1)
        eng.affine_select(out=sum_rows[:], in_=sum_rows[:], compare_op=ALU.not_equal, fill=1.0, base=0,
                          pattern=[[-1, NSEQ]], channel_multiplier=1).then_inc(sem("const"), 1)
        eng.wait_ge(sem("const"), 6)
        eng.affine_select(out=sum_rows[:], in_=sum_rows[:], compare_op=ALU.not_equal, fill=1.0, base=-NSEQ,
                          pattern=[[-1, NSEQ]], channel_multiplier=1).then_inc(sem("const"), 1)
        eng.memset(mask_f[:], 0.0).then_inc(sem("const"), 1)
        eng.wait_ge(sem("const"), CONSTS + 1)
        eng.affine_select(out=mask_f[:], in_=mask_f[:], compare_op=ALU.is_ge, fill=MASKED, base=0,
                          pattern=[[-1, 128]], channel_multiplier=1).then_inc(sem("const"), 1)
        eng.wait_ge(sem("const_split"), 2)
        eng.memset(mask_f[0:ST, :], 0.0).then_inc(sem("const"), 1)
        eng.wait_ge(sem("const"), CONSTS + 3)
        eng.affine_select(out=mask_f[0:ST, :].rearrange("p (h q) -> p h q", q=ST),
                          in_=mask_f[0:ST, :].rearrange("p (h q) -> p h q", q=ST), compare_op=ALU.not_equal,
                          fill=1.0, base=0, pattern=[[0, 8], [-1, ST]], channel_multiplier=1).then_inc(sem("const"), 1)
        with eng.Fori(0, NMOD) as i:
            for q in range(4):
                split_lo(eng, i * 4 + q, ADA_SLOTS[q % 2])

    CONSTS = 7

    def setup_tensor(eng):
        eng.sem_inc(sem("w_used"), CREDIT - 1)
        eng.sem_inc(sem("x_turned"), CREDIT)
        eng.wait_ge(sem("const"), CONSTS)
        eng.wait_ge(sem("vec_loaded"), 16 * 11)
        eng.transpose(ps[6][:, 0:88], vec_rows[0][:], ident[0:88, 0:88])
        eng.transpose(ps[6][:, 88:184], vec_rows[1][:], ident[0:96, 0:96]).then_inc(sem("setup_turned"), 1)
        eng.wait_ge(sem("c_act"), 1)
        for k in range(KT):
            last = eng.transpose(ps[4][:, NSEQ * k:NSEQ * k + NSEQ], c_rows[:, 128 * k:128 * k + 128],
                                 ident[0:NSEQ, 0:NSEQ])
        last.then_inc(sem("setup_turned"), 1)

        def turn_x(slot, tile, loads):
            eng.wait_ge(sem(f"x_rows_loaded{slot}"), 16 * loads)
            for half in range(2):
                eng.wait_ge(sem("x_moved"), tile * 2 + half + 1)
                for k in range(4):
                    last = eng.transpose(ps[2 * slot + half][:, 128 * k:128 * k + 128],
                                         x_rows[slot][:, 512 * half + 128 * k:512 * half + 128 * k + 128], ident[:])
                last.then_inc(sem("x_turned"), 1)

        with eng.Fori(0, TP // 256) as i:
            for k in range(2):
                turn_x(k, i * 2 + k, i + 1)
        turn_x(0, TP // 128, TP // 256 + 1)
        eng.wait_ge(sem("state_loaded"), 48)
        eng.transpose(ps[7][:, 0:64], state_rows[0][:], ident[0:64, 0:64])
        for n in range(2):
            last = eng.transpose(ps[7][:, 64 + 96 * n:160 + 96 * n], state_rows[1 + n][:], ident[0:96, 0:96])
        last.then_inc(sem("states_turned"), 1)
        eng.wait_ge(sem("past_loaded"), 16 * SB)
        for half in range(2):
            eng.wait_ge(sem("bank7_moved"), half + 1)
            for k in range(4):
                last = eng.transpose(ps[7][:, 128 * k:128 * k + 128], past_rows[:, 4 * half + k, :], ident[:])
            last.then_inc(sem("states_turned"), 1)
        eng.wait_ge(sem("cT_lo"), 1)
        with eng.Fori(0, NMOD) as i:
            for q in range(4):
                bank, st = 4 + q % 2, q % 2
                wait_block(eng, i * 4 + q)
                hi = w_hi[st][:].rearrange("p (k n) -> p k n", n=256)
                lo = w_lo[st][:].rearrange("p (k n) -> p k n", n=256)
                for k in range(KT):
                    mm = eng.matmul(ps[bank][0:2 * NSEQ, 0:256], cT[:, k, :], hi[:, k, :], start=(k == 0), stop=False)
                    if k == 0:
                        mm.then_inc(sem("w_used"), 1)
                    last = eng.matmul(ps[bank][0:2 * NSEQ, 0:256], cT[:, k, :], lo[:, k, :], start=False, stop=(k == KT - 1))
                last.then_inc(sem("ada_full"), 1)
                eng.wait_ge(sem("mod_rows_ready"), i * 4 + q + 1)
                if q == 0:
                    eng.wait_ge(sem("mod_ready"), i + 1)
                for t in range(2):
                    col = (2 * q + t) * NSEQ
                    last = eng.matmul(ps[6][:, col:col + NSEQ], mod_rows[q % 2][:, 128 * t:128 * t + 128],
                                      sum_rows[:], start=True, stop=True)
                last.then_inc(sem("mod_turned"), 1)

    def setup_vector(eng):
        eng.sem_inc(sem("x_moved"), CREDIT)
        eng.sem_inc(sem("mod_ready"), 1)
        for name in ("u_free", "y_free"):
            eng.sem_inc(sem(name), CREDIT)
        eng.wait_ge(sem("setup_turned"), 1)
        eng.tensor_copy(params[:], ps[6][:, 0:184]).then_inc(sem("params_ready"), 1)
        eng.wait_ge(sem("c_act"), 2)
        eng.tensor_tensor(cT[:, :, NSEQ:2 * NSEQ], ps[4][:, 0:KT * NSEQ].rearrange("p (k s) -> p k s", k=KT),
                          cT[:, :, 0:NSEQ].bitcast(F32), ALU.subtract).then_inc(sem("cT_lo"), 1)

        def move_x(slot, tile):
            for half in range(2):
                eng.wait_ge(sem("x_turned"), tile * 2 + half + 1 + CREDIT)
                eng.tensor_copy(x[:, 4 * half:4 * half + 4, ds(tile * 128, 128)],
                                ps[2 * slot + half][:].rearrange("p (k n) -> p k n", k=4)).then_inc(sem("x_moved"), 1)

        with eng.Fori(0, TP // 256) as i:
            for k in range(2):
                move_x(k, i * 2 + k)
        move_x(0, TP // 128)
        eng.wait_ge(sem("states_turned"), 1)
        eng.tensor_copy(h0[:], ps[7][:, 0:64])
        eng.tensor_copy(conv_state[:], ps[7][:, 64:256]).then_inc(sem("bank7_moved"), 1)
        past_f = past_rows[:].rearrange("p k n -> p (k n)")
        for half in range(2):
            eng.wait_ge(sem("states_turned"), half + 2)
            eng.wait_ge(sem("bank7_moved"), half + 1)
            minus_sums(eng, past_f[:, 512 * half:512 * half + 512], ps[7], past_f[:, 511:512] if half else 0.0).then_inc(sem("bank7_moved"), 1)
        eng.wait_ge(sem("bank7_moved"), 3)
        eng.tensor_copy(past_last[:], past_rows[:, PAST // 128 - 1, 127:128])
        eng.memset(tiny_col[:], 2.0 ** -100)
        eng.wait_ge(sem("const_split"), 4)
        eng.tensor_tensor(wfl_lo[:], wfl_raw[:], wfl_hi[:].bitcast(F32), ALU.subtract).then_inc(sem("fl_w_lo"), 1)
        log1p_vector(eng, [t[:] for t in lam_t], "lam", 2)
        eng.tensor_scalar(lam_t[1][:], params[:, G_LAM:G_LAM + KT], -1.0, 0.0, ALU.mult, ALU.max).then_inc(sem("lam_dve"), 1)
        eng.wait_ge(sem("lam_dve"), LOG1P_STEPS + 1)
        eng.tensor_tensor(lam_t[0][:], lam_t[0][:], lam_t[1][:], ALU.add).then_inc(sem("lam_dve"), 1)
        eng.wait_ge(sem("lam_dve"), LOG1P_STEPS + 2)
        eng.tensor_scalar(sp4[:], lam_t[0][:], 4.0, None, ALU.mult).then_inc(sem("lam_dve"), 1)
        eng.wait_ge(sem("params_ready"), 1)
        with eng.Fori(0, NMOD) as i:
            for q in range(4):
                eng.wait_ge(sem("ada_full"), i * 4 + q + 1)
                eng.tensor_copy(mod_rows[q % 2][:], ps[4 + q % 2][0:2 * NSEQ, 0:256]).then_inc(sem("mod_rows_ready"), 1)
            eng.wait_ge(sem("mod_turned"), i * 4 + 4)
            eng.tensor_tensor(mods[:, i, :, :], ps[6][:, 0:KT * NSEQ].rearrange("p (k s) -> p k s", k=KT),
                              params[:, ds(i * KT, KT)].unsqueeze(2).to_broadcast([128, KT, NSEQ]),
                              ALU.add).then_inc(sem("mod_ready"), 1)
        eng.wait_ge(sem("mod_ready"), NMOD + 1)
        for m, g in ((1, G_FFN1), (4, G_MIX), (7, G_FFN2), (10, G_FINAL)):
            eng.scalar_tensor_tensor(mods[:, m], mods[:, m], 1.0,
                                     params[:, g:g + KT].unsqueeze(2).to_broadcast([128, KT, NSEQ]),
                                     ALU.add, ALU.mult).then_inc(sem("mod_final"), 1)
        for m, half in ((2, 0.5), (5, 1.0), (8, 0.5)):
            eng.tensor_scalar(mods[:, m], mods[:, m], 1.0, half, ALU.add, ALU.mult).then_inc(sem("mod_final"), 1)

    def seq_bc(mod, k0=0, k1=KT):
        return mods[:, mod, k0:k1, 1:NSEQ].unsqueeze(3).to_broadcast([128, k1 - k0, SB, ST])

    def norm_tensor(eng, n):
        for c in range(NC):
            g = NC * n + c
            eng.wait_ge(sem("sq_ready"), g + 1)
            if c >= 2:
                eng.wait_ge(sem("rms_ready"), g - 1)
            for k in range(KT):
                last = eng.matmul(ps[6 + c % 2][:, 0:CH], ones[:], xn[c % 2][:, k, :], start=(k == 0), stop=(k == KT - 1))
            last.then_inc(sem("ss_ready"), 1)

    def norm_scalar(eng, n, x_ready):
        for c in range(NC):
            g = NC * n + c
            if c == 0:
                x_ready(eng)
            if c >= 2:
                eng.wait_ge(sem("h_lo"), g - 1)
            eng.activation(xn[c % 2][:], x[:, :, tokens_of(c)], ACT.Square).then_inc(sem("sq_ready"), 1)
            if c >= 1:
                norm_hi(eng, g - 1, c - 1)
        norm_hi(eng, NC * n + NC - 1, NC - 1)

    def norm_hi(eng, g, c):
        eng.wait_ge(sem("ss_ready"), g + 1)
        if g >= 1:
            eng.wait_ge(sem("x_normed"), g)
        eng.activation(inv[:], ps[6 + c % 2][:, 0:CH], ACT.Sqrt, scale=1.0 / D, bias=eps_col[:]).then_inc(sem("rms_ready"), 1)
        eng.wait_ge(sem("h_ready"), g + 1)
        eng.activation(acts_hi[:, :, tokens_of(c)], xn[c % 2][:], ACT.Copy).then_inc(sem("h_hi"), 1)

    def norm_vector(eng, n):
        mod = (0, 3, 6)[n]
        if n == 0:
            eng.wait_ge(sem("mod_final"), 7)
        for c in range(NC):
            g = NC * n + c
            h = xn[c % 2]
            eng.wait_ge(sem("rms_ready"), g + 1)
            eng.reciprocal(inv[:], inv[:]).then_inc(sem("inv_ready"), 1)
            eng.wait_ge(sem("inv_ready"), g + 1)
            eng.tensor_tensor(h[:], x[:, :, tokens_of(c)], inv[:].unsqueeze(1).to_broadcast([128, KT, CH]),
                              ALU.mult).then_inc(sem("x_normed"), 1)
            eng.wait_ge(sem("x_normed"), g + 1)
            scale_shift(eng, h, c, mod, mod + 1, n)
            eng.wait_ge(sem("h_hi"), g + 1)
            eng.tensor_tensor(acts_lo[:, :, tokens_of(c)], h[:], acts_hi[:, :, tokens_of(c)].bitcast(F32),
                              ALU.subtract).then_inc(sem("h_lo"), 1)

    def scale_shift(eng, h, c, shift, scale, n):
        cp = CH if c < NC - 1 else CP
        if c == NC - 1:
            hs = h[:, :, CP:CH].rearrange("p k (s t) -> p k s t", s=SB)
            eng.tensor_tensor(hs, hs, seq_bc(scale), ALU.mult).then_inc(sem("mod_step"), 1)
            eng.wait_ge(sem("mod_step"), n + 1)
            eng.tensor_tensor(hs, hs, seq_bc(shift), ALU.add)
        for k in range(KT):
            last = eng.tensor_scalar(h[:, k, 0:cp], h[:, k, 0:cp], mods[:, scale, k, 0:1], mods[:, shift, k, 0:1],
                                     ALU.mult, ALU.add)
        last.then_inc(sem("h_ready"), 1)

    def ffn_sync(eng, f):
        w1, w3, w2 = (a[f"ffn{f + 1}_w{n}"][0] for n in (1, 3, 2))
        block0 = (B_FFN1, B_FFN2)[f]
        w1v, w3v = kview(w1), kview(w3)
        with eng.Fori(0, FF_PAIRS) as i:
            b = block0 + i * 3
            load_block(eng, b, FFN_SLOTS[0], w1v[:, :, ds(i * 256, 256)])
            load_block(eng, b + 1, FFN_SLOTS[1], w3v[:, :, ds(i * 256, 256)])
            load_block(eng, b + 2, FFN_SLOTS[2],
                       w2[ds(i * 256, 256), :].rearrange("(t p) n -> p t n", p=128))

    def ffn_tensor(eng, f):
        block0 = (B_FFN1, B_FFN2)[f]
        with eng.Fori(0, FF_PAIRS) as i:
            it = f * FF_PAIRS + i
            for c in range(NC):
                for t in range(2):
                    n = 2 * c + t
                    g = it * 6 + n
                    eng.wait_ge(sem("u_free"), g - 2 + 1 + CREDIT)
                    if t == 0:
                        eng.wait_ge(sem("h_lo"), NC * (0, 2)[f] + c + 1)
                    if n == 0:
                        wait_block(eng, block0 + i * 3 + 1)
                    for which, bank in ((0, 2 * (n % 2)), (1, 2 * (n % 2) + 1)):
                        whi, wlo = wcols(FFN_SLOTS[which][2], t)
                        for k in range(KT):
                            opens = sem("w_used") if (n, which, k) == (0, 0, 0) else None
                            last = mm3(eng, ps[bank][:, 0:CH], whi[k], wlo[k], acts_hi[:, k, tokens_of(c)],
                                       acts_lo[:, k, tokens_of(c)], k == 0, k == KT - 1, opens)
                        if (n, which) == (5, 0):
                            last.then_inc(sem("w_used"), 1)
                    last.then_inc(sem("a_full"), 1)
            wait_block(eng, block0 + i * 3 + 2)
            h2 = w_hi[FFN_SLOTS[2][2]][:].rearrange("p (t n) -> p t n", t=2)
            l2 = w_lo[FFN_SLOTS[2][2]][:].rearrange("p (t n) -> p t n", t=2)
            for c in range(NC):
                eng.wait_ge(sem("u_lo_done"), it * 6 + 2 * c + 2)
                for d in range(KT):
                    eng.wait_ge(sem("y_free"), it * 24 + c * 8 + d - 4 + 1 + CREDIT)
                    for t in range(2):
                        opens = sem("w_used") if (c, d, t) == (0, 0, 0) else None
                        last = mm3(eng, ps[4 + d % 4][:, 0:CH], h2[:, t, 128 * d:128 * d + 128],
                                   l2[:, t, 128 * d:128 * d + 128], u_hi[:, t, tokens_of(c)],
                                   u_lo[:, t, tokens_of(c)], t == 0, t == 1, opens)
                    last.then_inc(sem("b_full"), 1)

    def ffn_scalar(eng, f):
        block0, raws = ((B_FFN1, FFN1_RAWS), (B_FFN2, FFN2_RAWS))[f]
        eng.wait_ge(sem("h_lo"), NC * (0, 2)[f] + NC)
        with eng.Fori(0, FF_PAIRS) as i:
            it = f * FF_PAIRS + i
            split_hi(eng, block0 + i * 3, FFN_SLOTS[0], raws[0] + i * 2)
            split_hi(eng, block0 + i * 3 + 1, FFN_SLOTS[1], raws[1] + i)
            split_hi(eng, block0 + i * 3 + 2, FFN_SLOTS[2], raws[0] + i * 2 + 1)
            for n in range(6):
                c, t = n // 2, n % 2
                g = it * 6 + n
                eng.wait_ge(sem("a_full"), g + 1)
                eng.wait_ge(sem("u_free"), g - 2 + 1 + CREDIT)
                eng.activation(gated[n % 2][:], ps[2 * (n % 2)][:, 0:CH], ACT.Silu).then_inc(sem("gated_ready"), 1)
                eng.wait_ge(sem("u_free"), g + 1 + CREDIT)
                eng.activation(u_hi[:, t, tokens_of(c)], u_f[n % 2][:], ACT.Copy).then_inc(sem("u_hi_done"), 1)

    def ffn_gpsimd(eng, f):
        block0 = (B_FFN1, B_FFN2)[f]
        with eng.Fori(0, FF_PAIRS) as i:
            it = f * FF_PAIRS + i
            for j in range(3):
                split_lo(eng, block0 + i * 3 + j, FFN_SLOTS[j])
            for n in range(6):
                c, t = n // 2, n % 2
                eng.wait_ge(sem("u_hi_done"), it * 6 + n + 1)
                eng.tensor_tensor(u_lo[:, t, tokens_of(c)], u_f[n % 2][:], u_hi[:, t, tokens_of(c)].bitcast(F32),
                                  ALU.subtract).then_inc(sem("u_lo_done"), 1)

    def ffn_vector(eng, f):
        gate = (2, 8)[f]
        with eng.Fori(0, FF_PAIRS) as i:
            it = f * FF_PAIRS + i
            for n in range(6):
                g = it * 6 + n
                eng.wait_ge(sem("gated_ready"), g + 1)
                if n >= 2:
                    eng.wait_ge(sem("u_lo_done"), g - 1)
                eng.tensor_tensor(u_f[n % 2][:], ps[2 * (n % 2) + 1][:, 0:CH], gated[n % 2][:],
                                  ALU.mult).then_inc(sem("u_free"), 1)
            for c in range(NC):
                for d in range(KT):
                    b = it * 24 + c * 8 + d
                    eng.wait_ge(sem("b_full"), b + 1)
                    add_gated(eng, ps[4 + d % 4], x, d, c, gate, "y_free", it * 8 + d + f * KT)

    def add_gated(eng, bank, xt, d, c, gate, done, step):
        cp = CH if c < NC - 1 else CP
        t0 = c * CH
        if c == NC - 1:
            eng.tensor_tensor(s_tmp[d % 2][:], bank[:, CP:CH].rearrange("p (s t) -> p s t", s=SB),
                              mods[:, gate, d, 1:NSEQ].unsqueeze(2).to_broadcast([128, SB, ST]),
                              ALU.mult).then_inc(sem("s_gated"), 1)
        last = eng.scalar_tensor_tensor(xt[:, d, t0:t0 + cp], bank[:, 0:cp], mods[:, gate, d, 0:1],
                                        xt[:, d, t0:t0 + cp], ALU.mult, ALU.add)
        if c == NC - 1:
            eng.wait_ge(sem("s_gated"), step + 1)
            xs_ = xt[:, d, TP:T].rearrange("p (s t) -> p s t", s=SB)
            last = eng.tensor_tensor(xs_, xs_, s_tmp[d % 2][:], ALU.add)
        last.then_inc(sem(done), 1)

    def final_tensor(eng):
        for c in range(NC):
            g = NC * NORMS_BEFORE + c
            eng.wait_ge(sem("sq_ready"), g + 1)
            for k in range(KT):
                last = eng.matmul(ps[6][:, 0:CH], ones[:], xf[:, k, :], start=(k == 0), stop=(k == KT - 1))
            last.then_inc(sem("ss_ready"), 1)
            eng.wait_ge(sem("h_ready"), g + 1)
            for m in range(3):
                tile = 3 * c + m
                for half in range(2):
                    n = 2 * tile + half
                    if tile >= 2:
                        eng.wait_ge(sem(("y_even", "y_odd")[half]), tile - 1)
                    for k in range(4):
                        last = eng.transpose(ps[n % 4][:, 128 * k:128 * k + 128],
                                             xf[:, 4 * half + k, 128 * m:128 * m + 128], ident[:])
                    last.then_inc(sem("y_turned"), 1)

    def final_scalar(eng):
        for c in range(NC):
            g = NC * NORMS_BEFORE + c
            if c == 0:
                eng.wait_ge(sem("y_free"), 2 * FF_PAIRS * 24 + CREDIT)
            if c >= 1:
                eng.wait_ge(sem("y_turned"), 6 * c)
            eng.activation(xf[:], x[:, :, tokens_of(c)], ACT.Square).then_inc(sem("sq_ready"), 1)
            eng.wait_ge(sem("ss_ready"), g + 1)
            eng.activation(inv_f[:], ps[6][:, 0:CH], ACT.Sqrt, scale=1.0 / D, bias=eps_col[:]).then_inc(sem("rms_ready"), 1)
            for m in range(3):
                tile = 3 * c + m
                n = 2 * tile + 1
                eng.wait_ge(sem("y_turned"), n + 1)
                if tile >= 2:
                    eng.wait_ge(sem(f"y_stored{tile % 2}"), 16 * (tile // 2))
                eng.activation(y_rows[tile % 2][:, 512:1024], ps[n % 4][:], ACT.Copy).then_inc(sem("y_odd"), 1)

    def final_vector(eng):
        for c in range(NC):
            g = NC * NORMS_BEFORE + c
            eng.wait_ge(sem("rms_ready"), g + 1)
            eng.reciprocal(inv_f[:], inv_f[:]).then_inc(sem("inv_ready"), 1)
            eng.wait_ge(sem("inv_ready"), g + 1)
            eng.tensor_tensor(xf[:], x[:, :, tokens_of(c)], inv_f[:].unsqueeze(1).to_broadcast([128, KT, CH]),
                              ALU.mult).then_inc(sem("x_normed"), 1)
            eng.wait_ge(sem("x_normed"), g + 1)
            cp = CH if c < NC - 1 else CP
            if c == NC - 1:
                hs = xf[:, :, CP:CH].rearrange("p k (s t) -> p k s t", s=SB)
                eng.tensor_tensor(hs, hs, seq_bc(10), ALU.mult).then_inc(sem("mod_step"), 1)
                eng.wait_ge(sem("mod_step"), NORMS_BEFORE + 1)
                eng.tensor_tensor(hs, hs, seq_bc(9), ALU.add)
            for k in range(KT):
                last = eng.tensor_scalar(xf[:, k, 0:cp], xf[:, k, 0:cp], mods[:, 10, k, 0:1], mods[:, 9, k, 0:1],
                                         ALU.mult, ALU.add)
            last.then_inc(sem("h_ready"), 1)
            for m in range(3):
                tile = 3 * c + m
                n = 2 * tile
                eng.wait_ge(sem("y_turned"), n + 1)
                if tile >= 2:
                    eng.wait_ge(sem(f"y_stored{tile % 2}"), 16 * (tile // 2))
                last = eng.tensor_copy(y_rows[tile % 2][:, 0:512], ps[n % 4][:])
                last.then_inc(sem("y_even"), 1)

    def final_sync(eng):
        yp = o["y_prompt"][0].rearrange("(m p) d -> m p d", p=128)
        for tile in range(T // 128):
            eng.wait_ge(sem("y_even"), tile + 1)
            eng.wait_ge(sem("y_odd"), tile + 1)
            dst = yp[tile] if tile < TP // 128 else o["y_sample"].rearrange("s t d -> (s t) d")
            eng.dma_start(dst, y_rows[tile % 2][:]).then_inc(sem(f"y_stored{tile % 2}"), 16)
        eng.wait_ge(sem("y_stored0"), 16 * 5)
        eng.wait_ge(sem("y_stored1"), 16 * 4)

    N_IT = KT // 2
    COLS = (COL_XR, COL_GR, COL_Q, COL_K, COL_V, COL_GA, COL_GB)
    XR, GR, Q, K, V, GA, GB = range(7)
    ST_BEFORE = {Q: 0, K: 1, V: 2, GA: 2, GB: 3}
    TOK_BEFORE = (0, 0, 1, 1, 3, 2)
    FL_STEPS = LOG1P_STEPS + 5

    def x_samples(t):
        return xpad[t][:, XP:].rearrange("p (s j) -> p s j", s=SB)

    def proj_sync(eng):
        eng.wait_ge(sem("y_free"), FF_PAIRS * 24 + CREDIT)
        eng.dma_start(x_dram, x[:].rearrange("p k t -> p (k t)")).then_inc(sem("x_spilled"), 16)
        w_in_v = kview(a["w_in"][0])

        def body(i, first):
            for j in range(7):
                load_block(eng, B_PROJ + i * 7 + j, PROJ_SLOTS[j], w_in_v[:, :, ds(i * 256 + COLS[j], 256)])
                if j == 0:
                    if first:
                        eng.wait_ge(sem("bd_clear"), 1)
                    else:
                        eng.wait_ge(sem("ri_full"), i * 12)
                    for n, name in enumerate(("rg_wa", "rg_wx")):
                        for half in range(2):
                            src = a[name][0].rearrange("(n two) i j -> two i n j", two=2)[half]
                            eng.dma_start(bd[64 * half:64 * half + 64, 2 * n:2 * n + 2, 64 * half:64 * half + 64],
                                          src[:, ds(i * 2, 2), :]).then_inc(sem("bd_loaded"), 16)
        body(0, True)
        with eng.Fori(1, N_IT) as i:
            body(i, False)

    def proj_tensor(eng):
        eng.wait_ge(sem("fl_w_lo"), 1)
        for c in range(NC):
            eng.wait_ge(sem("h_lo"), NC + c + 1)
            for k in range(KT):
                last = mm3(eng, ps[3 + c][0:H, 0:CH], wfl_hi[:, k, :], wfl_lo[:, k, :], acts_hi[:, k, tokens_of(c)],
                           acts_lo[:, k, tokens_of(c)], k == 0, k == KT - 1)
            last.then_inc(sem("fl_full"), 1)

        def body(i, first):
            for j in range(7):
                for n in range(6):
                    t, c = n // 3, n % 3
                    g = i * 42 + j * 6 + n
                    eng.wait_ge(sem("proj_free"), g + 1)
                    if first and (j, n) == (XR, 3):
                        eng.wait_ge(sem("fl_z"), 3)
                    if j in (V, GA):
                        e = i * 12 + (j - V) * 6 + n
                        if (j, n) == (V, 0):
                            eng.wait_ge(sem("ri_moved"), i * 12 + 12 + 2)
                        eng.wait_ge(sem("tok_moved"), e + 1)
                        for m in range(3):
                            last = eng.transpose(ps[6 + n % 2][:, 128 * m:128 * m + 128],
                                                 st[t][:, CH * c + 128 * m:CH * c + 128 * m + 128], ident[:])
                        last.then_inc(sem("tok_turned"), 1)
                    if n == 0:
                        wait_block(eng, B_PROJ + i * 7 + j)
                    whi, wlo = wcols(PROJ_SLOTS[j][2], t)
                    for k in range(KT):
                        last = mm3(eng, ps[n][:, 0:CH], whi[k], wlo[k], acts_hi[:, k, tokens_of(c)],
                                   acts_lo[:, k, tokens_of(c)], k == 0, k == KT - 1,
                                   sem("w_used") if (n, k) == (0, 0) else None)
                    last.then_inc(sem("proj_full"), 1)
                    if j == GR and first and n == 5:
                        logf_turn(eng)
                    if j == Q:
                        if n == 0:
                            eng.wait_ge(sem("bd_loaded"), i * 64 + 64)
                            if first:
                                eng.wait_ge(sem("lft_ready"), 1)
                            eng.wait_ge(sem("tok_moved"), i * 12 + 2)
                        if c == 0:
                            eng.wait_ge(sem("conv_ready"), i * 2 + t + 1)
                        for kind in range(2):
                            eng.wait_ge(sem("ri_moved"), i * 12 + 2 * n + kind + 1)
                            eng.matmul(ps[6 + kind][:, 0:CH], bd[:, 2 * kind + t, :], xc[t][:, tokens_of(c)],
                                       start=True, stop=True).then_inc(sem("ri_full"), 1)
        body(0, True)
        with eng.Fori(1, N_IT) as i:
            body(i, False)

    def logf_turn(eng):
        eng.wait_ge(sem("fl_done"), 1)
        eng.wait_ge(sem("fl_z"), 3)
        for m in range(T // 128):
            last = eng.transpose(ps[7][:, H * m:H * m + H], it[1][0:H, 128 * m:128 * m + 128], ident[0:H, 0:H])
        last.then_inc(sem("lf_turned"), 1)

    def proj_scalar(eng):
        split_hi(eng, B_PROJ, PROJ_SLOTS[0], PROJ_RAWS[0])
        eng.wait_ge(sem("x_spilled"), 16)
        eng.wait_ge(sem("h_lo"), 2 * NC)
        for c in range(NC):
            eng.wait_ge(sem("fl_full"), c + 1)
            eng.activation(it[1][0:H, tokens_of(c)], ps[3 + c][0:H, 0:CH], ACT.Identity,
                           bias=b_fgt_col[:]).then_inc(sem("fl_z"), 1)
        eng.wait_ge(sem("fl_z"), 3)
        eng.activation(rt[0][0:H, :], it[1][0:H, :], ACT.Abs).then_inc(sem("fl_act"), 1)
        eng.wait_ge(sem("fl_act"), 1)
        eng.activation(rt[0][0:H, :], rt[0][0:H, :], ACT.Exp, scale=-1.0).then_inc(sem("fl_act"), 1)
        log1p_scalar(eng, rt[1][0:H, :], "fl")

        def body(i, first):
            for j in range(7):
                for n in range(6):
                    t, c = n // 3, n % 3
                    g = i * 42 + j * 6 + n
                    tile = i * 2 + t
                    if j in (V, GA):
                        move_tokens(eng, i, j, n)
                    eng.wait_ge(sem("proj_full"), g + 1)
                    bank = ps[n][:, 0:CH]
                    if j == XR:
                        if c == 0:
                            eng.wait_ge(sem("rnn_done"), i * 2 + t + 1)
                        if c < NC - 1:
                            eng.activation(xpad[t][:, PAD + CH * c:PAD + CH * c + CH], bank, ACT.Copy).then_inc(sem("proj_free"), 1)
                        else:
                            eng.activation(xpad[t][:, PAD + CH * c:XP], bank[:, 0:CP], ACT.Copy)
                            eng.activation(x_samples(t)[:, :, PAD:], bank[:, CP:CH].rearrange("p (s q) -> p s q", s=SB),
                                           ACT.Copy).then_inc(sem("proj_free"), 1)
                    elif j == GR:
                        if c == 0:
                            eng.wait_ge(sem(f"a_stored{t}"), i * 16 + 16)
                        eng.activation(gl[t][:, tokens_of(c)], bank, ACT.Gelu_apprx_tanh).then_inc(sem("proj_free"), 1)
                    else:
                        if c == 0:
                            eng.wait_ge(sem(f"st_stored{t}"), (i * 4 + ST_BEFORE[j] + 1) * 16)
                        func = ACT.Sigmoid if j in (GA, GB) else ACT.Copy
                        eng.activation(st[t][:, tokens_of(c)], bank, func,
                                       scale=HD ** -0.5 if j == Q else 1.0).then_inc(sem("proj_free"), 1)
                        if c == NC - 1 and j != V:
                            eng.wait_ge(sem("proj_free"), g + 1 + 6)
                            dst = {Q: q_dram, K: k_dram, GA: ga_dram, GB: gb_dram}[j]
                            eng.dma_start(dst[ds(tile * 128, 128), :], st[t][:]).then_inc(sem(f"st_stored{t}"), 16)
                    if j == Q:
                        gates(eng, i, n, first)
                    if n == 2:
                        nj = (j + 1) % 7
                        raw = PROJ_SLOTS[nj][0]
                        split_hi(eng, B_PROJ + i * 7 + j + 1, PROJ_SLOTS[nj],
                                 (i * (4, 3)[raw] if j < 6 else i * 4 + 4) + nj // 2 + PROJ_RAWS[raw])
                    if first and (j, n) == (GR, 5):
                        forget_out(eng)
                    if (j, n) == (GA, 0):
                        for u in range(2):
                            eng.wait_ge(sem("rnn_done"), i * 2 + u + 1 + 2)
                            eng.dma_start(a_dram[ds(i * 256 + u * 128, 128), :], gl[u][:]).then_inc(sem(f"a_stored{u}"), 16)
        body(0, True)
        with eng.Fori(1, N_IT) as i:
            body(i, False)

    def move_tokens(eng, i, j, n):
        t, c = n // 3, n % 3
        which = j - V
        e = i * 12 + which * 6 + n
        slot = n % 2
        eng.wait_ge(sem("tok_turned"), e + 1)
        eng.wait_ge(sem(f"tok_stored{slot}"), ((i * 2 + which) * 4 + TOK_BEFORE[n] + 1) * 16)
        eng.activation(tok[slot][:], ps[6 + slot][:, 0:CH].rearrange("p (m d) -> p m d", m=3), ACT.Copy).then_inc(sem("tok_moved"), 1)
        eng.wait_ge(sem("tok_moved"), e + 1 + 2)
        name = ("k", "v")[which]
        prompt = o[name + "_prompt"][0, 0].rearrange("(m p) h d -> p m (h d)", p=128)
        cols = ds(i * 256 + t * 128, 128)
        m1 = 3 if c < NC - 1 else 2
        eng.dma_start(prompt[:, 3 * c:3 * c + m1, cols], tok[slot][:, 0:m1, :]).then_inc(sem(f"tok_stored{slot}"), 16)
        if c == NC - 1:
            sample = o[name + "_sample"][0].rearrange("s t h d -> (s t) (h d)")
            eng.dma_start(sample[:, cols], tok[slot][:, 2, :]).then_inc(sem(f"tok_stored{slot}"), 16)

    def gates(eng, i, n, first):
        t, c = n // 3, n % 3
        if first and n == 0:
            eng.wait_ge(sem("bias_stored"), 16)
            eng.wait_ge(sem("lf_turned"), 1)
        for kind, buf in ((0, rt), (1, it)):
            eng.wait_ge(sem("ri_full"), i * 12 + 2 * n + kind + 1)
            eng.activation(buf[t][:, tokens_of(c)], ps[6 + kind][:, 0:CH], ACT.Sigmoid,
                           bias=gate_p[:, t, kind:kind + 1]).then_inc(sem("ri_moved"), 1)
        if c == NC - 1:
            eng.wait_ge(sem("ri_moved"), i * 12 + 2 * n + 2 + 2)
            eng.activation(rt[t][:], rt[t][:], ACT.Tanh, scale=gate_p[:, t, 2:3]).then_inc(sem("rnn_act"), 1)
            eng.wait_ge(sem("rnn_act"), i * 4 + 2 * t + 1)
            eng.activation(xpad[t][:, 0:T], rt[t][:], ACT.Sqrt, scale=4.0, bias=tiny_col[:]).then_inc(sem("rnn_act"), 1)

    def forget_out(eng):
        eng.wait_ge(sem("bias_ready"), 1)
        eng.dma_start(bias_dram, rt[0][0:H, 0:TP]).then_inc(sem("bias_stored"), 16)
        eng.wait_ge(sem("lft_ready"), 1)
        eng.dma_start(o["logf_prompt"][0, 0].rearrange("(m p) h -> p m h", p=128), lft[:, 0:TP // 128, :]).then_inc(sem("logf_stored"), 16)
        eng.dma_start(o["logf_sample"][0].rearrange("s t h -> (s t) h"), lft[:, TP // 128, :]).then_inc(sem("logf_stored"), 16)

    def proj_gpsimd(eng):
        split_lo(eng, B_PROJ, PROJ_SLOTS[0])
        with eng.Fori(0, N_IT) as i:
            for j in range(7):
                split_lo(eng, B_PROJ + i * 7 + j + 1, PROJ_SLOTS[(j + 1) % 7])

    class Steps:

        def __init__(self, eng, name, base):
            self.eng, self.sem, self.base, self.n = eng, sem(name), base, 0

        def done(self, instruction):
            instruction.then_inc(self.sem, 1)
            self.n += 1

        def settle(self):
            self.eng.wait_ge(self.sem, self.base + self.n)

    RNN_STEPS = 2 * 21

    def proj_vector(eng):
        eng.sem_inc(sem("rnn_done"), 2)
        eng.wait_ge(sem("x_spilled"), 16)
        eng.wait_ge(sem("h_lo"), 2 * NC)
        eng.memset(bd[:], 0.0).then_inc(sem("bd_clear"), 1)
        log1p_vector(eng, [rt[0][0:H, :], rt[1][0:H, :], it[0][0:H, :], xc[0][0:H, :]], "fl", 2)
        eng.tensor_scalar(it[1][0:H, :], it[1][0:H, :], 0.0, None, ALU.min).then_inc(sem("fl_dve"), 1)
        eng.wait_ge(sem("fl_dve"), LOG1P_STEPS + 1)
        eng.tensor_tensor(it[1][0:H, :], it[1][0:H, :], rt[0][0:H, :], ALU.subtract).then_inc(sem("fl_done"), 1)
        eng.wait_ge(sem("fl_done"), 1)
        minus_sums(eng, rt[0][0:H, 0:TP], it[1][0:H, 0:TP], 0.0).then_inc(sem("bias_ready"), 1)

        def body(i, first):
            s = Steps(eng, "rnn_dve", i * RNN_STEPS)

            def channel(vec, t):
                return params[:, ds(i * 2 + (vec + t), 1)]

            for t in range(2):
                tile = i * 2 + t
                xs_, out_s = x_samples(t), xc[t][:, TP:T].rearrange("p (s q) -> p s q", s=SB)
                eng.wait_ge(sem("proj_free"), i * 42 + 3 * t + 3 + 6)
                s.done(eng.memset(xpad[t][:, 0:PAD], 0.0))
                for n, src in enumerate((channel(G_BA, t), channel(G_BX, t), sp4[:, ds(tile, 1)])):
                    eng.tensor_copy(gate_p[:, t, n:n + 1], src)
                cs = conv_state[:].rearrange("p (s j n) -> p s j n", s=SB, j=PAD)
                s.done(eng.tensor_copy(xs_[:, :, 0:PAD], cs[:, :, :, ds(tile, 1)].rearrange("p s j n -> p s (j n)")))
                s.settle()
                for j in range(CONV_W):
                    w = channel(G_CONVW + KT * j, t)
                    for out, src in ((xc[t][:, 0:TP], xpad[t][:, j:j + TP]), (out_s, xs_[:, :, j:j + ST])):
                        if j == 0:
                            s.done(eng.tensor_scalar(out, src, w, channel(G_CONVB, t), ALU.mult, ALU.add))
                        else:
                            s.done(eng.scalar_tensor_tensor(out, src, w, out, ALU.mult, ALU.add))
                    s.settle()
                eng.tensor_copy(states[:, ds(tile, 1), 0:PAD], xpad[t][:, TP:XP].unsqueeze(1))
                eng.tensor_copy(states[:, ds(tile, 1), PAD:PAD + SB * PAD].rearrange("p o (s j) -> p (o s) j", s=SB),
                                xs_[:, :, ST:ST + PAD]).then_inc(sem("conv_ready"), 1)
                if first and t == 1:
                    eng.wait_ge(sem("lf_turned"), 1)
                    eng.tensor_copy(lft[:], ps[7][:, 0:H * (T // 128)].rearrange("p (m h) -> p m h", h=H)).then_inc(sem("lft_ready"), 1)
            for t in range(2):
                tile = i * 2 + t
                root = xpad[t][:, 0:T]
                eng.wait_ge(sem("rnn_act"), i * 4 + 2 * t + 2)
                s.done(eng.tensor_tensor(it[t][:], it[t][:], xc[t][:], ALU.mult))
                s.settle()
                s.done(eng.tensor_scalar(xc[t][:], rt[t][:], 1.0, None, ALU.add))
                s.settle()
                s.done(eng.reciprocal(xc[t][:], xc[t][:]))
                s.done(eng.tensor_scalar(rt[t][:], rt[t][:], -1.0, 1.0, ALU.mult, ALU.add))
                s.settle()
                s.done(eng.tensor_tensor(root, root, xc[t][:], ALU.mult))
                s.done(eng.tensor_tensor(rt[t][:], rt[t][:], xc[t][:], ALU.mult))
                s.settle()
                s.done(eng.tensor_tensor(it[t][:], it[t][:], root, ALU.mult))
                first_a, first_u = rt[t][:, TP:T:ST], it[t][:, TP:T:ST]
                s.done(eng.tensor_tensor(tmp8[t][:], first_a, h0[:].rearrange("p (s n) -> p s n", s=SB)[:, :, ds(tile, 1)].rearrange("p s n -> p (s n)"), ALU.mult))
                s.settle()
                s.done(eng.tensor_tensor(first_u, first_u, tmp8[t][:], ALU.add))
                s.done(eng.memset(first_a, 0.0))
                s.settle()
                s.done(eng.tensor_tensor_scan(xc[t][:], rt[t][:], it[t][:], 0.0, ALU.mult, ALU.add))
                s.settle()
                eng.tensor_copy(states[:, ds(tile, 1), 27:28], xc[t][:, TP - 1:TP].unsqueeze(1))
                eng.tensor_copy(states[:, ds(tile, 1), 28:36], xc[t][:, TP + ST - 1:T:ST].unsqueeze(1)).then_inc(sem("states_ready"), 1)
                eng.wait_ge(sem("proj_free"), i * 42 + 6 + 3 * t + 3 + 6)
                eng.tensor_tensor(gl[t][:], gl[t][:], xc[t][:], ALU.mult).then_inc(sem("rnn_done"), 1)
            assert s.n == RNN_STEPS, s.n
        body(0, True)
        with eng.Fori(1, N_IT) as i:
            body(i, False)

    G_BRR = 42 * N_IT

    def brr_sync(eng):
        for t in range(2):
            eng.wait_ge(sem(f"a_stored{t}"), (N_IT + 1) * 16)
        eng.dma_start(a_stage[:], kview(a_dram)).then_inc(sem("a_loaded"), 16)
        w = kview(a["w_br_rnn"][0])

        def gate_in(j, t):
            if j == 0:
                eng.wait_ge(sem(f"st_stored{t}"), (4 * N_IT + 1) * 16)
            else:
                eng.wait_ge(sem(f"z1_stored{t}"), 16 * j)
            eng.dma_start(st[t][:], ga_dram[256 * j + 128 * t:256 * j + 128 * t + 128, :]).then_inc(sem(f"ga_loaded{t}"), 16)

        def out(j, t):
            eng.wait_ge(sem("br_free"), 6 * j + 3 * t + 3)
            eng.dma_start(z1_dram[256 * j + 128 * t:256 * j + 128 * t + 128, :], st[t][:]).then_inc(sem(f"z1_stored{t}"), 16)

        load_block(eng, B_BRR, BRR_SLOTS[0], w[:, :, 0:256])
        gate_in(0, 0)
        gate_in(0, 1)
        load_block(eng, B_BRR + 1, BRR_SLOTS[1], w[:, :, 256:512])
        for j in range(4):
            if j < 2:
                load_block(eng, B_BRR + j + 2, BRR_SLOTS[j + 2], w[:, :, 256 * j + 512:256 * j + 768])
            if j == 0:
                eng.wait_ge(sem("logf_stored"), 32)
                eng.dma_start(lf16[:].rearrange("t (s h) -> t s h", s=SB), o["logf_sample"][0].rearrange("s t h -> t s h")).then_inc(sem("lf16_loaded"), 16)
            for t in range(2):
                out(j, t)
                if j < 3:
                    gate_in(j + 1, t)
        eng.wait_ge(sem("new_f_ready"), 1)
        eng.dma_start(past_dram[:, PAST:PAST + ST], new_f[:]).then_inc(sem("past_stored"), 16)
        eng.wait_ge(sem("state_out_ready"), 2)
        cp = o["conv_prompt"][0, 0]
        cs = o["conv_sample"][0].rearrange("s j d -> (s j) d")
        for dst, r0, r1 in ((cp, 0, 3), (cs, 3, 27), (o["rglru_prompt"][0], 27, 28), (o["rglru_sample"][0], 28, 36)):
            eng.dma_start(dst, state_out[r0:r1, :]).then_inc(sem("states_stored"), 16)

    def brr_tensor(eng):
        for j in range(4):
            for n in range(6):
                t, c = n // 3, n % 3
                q = 6 * j + n
                if j == 0:
                    eng.wait_ge(sem("proj_free"), G_BRR - 6 + n + 1 + 6)
                    if t == 0:
                        eng.wait_ge(sem("a_lo"), c + 1)
                else:
                    eng.wait_ge(sem("br_free"), q - 6 + 1)
                if n == 0:
                    wait_block(eng, B_BRR + j)
                whi, wlo = wcols(BRR_SLOTS[j][2], t)
                for k in range(KT):
                    last = mm3(eng, ps[n][:, 0:CH], whi[k], wlo[k], acts_hi[:, k, tokens_of(c)],
                               acts_lo[:, k, tokens_of(c)], k == 0, k == KT - 1,
                               sem("w_used") if (n, k) == (0, 0) else None)
                last.then_inc(sem("br_full"), 1)
            if j == 1:
                eng.wait_ge(sem("states_ready"), 2 * N_IT)
                eng.wait_ge(sem("tok_moved"), 12 * N_IT + 2)
                for half in range(2):
                    for k in range(4):
                        last = eng.transpose(ps[6 + half][0:36, 128 * k:128 * k + 128], states[:, 4 * half + k, :], ident[:])
                last.then_inc(sem("state_rows_turned"), 1)
            if j == 2:
                eng.wait_ge(sem("lf16_loaded"), 16)
                eng.wait_ge(sem("state_out_ready"), 2)
                eng.transpose(ps[6][:, 0:ST], lf16[:], ident[0:ST, 0:ST]).then_inc(sem("lf16_turned"), 1)

    def brr_scalar(eng):
        eng.wait_ge(sem("a_loaded"), 16)
        eng.wait_ge(sem("proj_full"), G_BRR)
        for c in range(NC):
            eng.activation(acts_hi[:, :, tokens_of(c)], a_stage[:, :, tokens_of(c)], ACT.Copy).then_inc(sem("a_hi"), 1)
        for j in range(1, 4):
            raw = BRR_SLOTS[j][0]
            split_hi(eng, B_BRR + j, BRR_SLOTS[j], BRR_RAWS[raw] + j // 2)
        eng.wait_ge(sem("state_rows_turned"), 1)
        for half in range(2):
            eng.activation(state_out[:, 512 * half:512 * half + 512], ps[6 + half][0:36, :], ACT.Copy).then_inc(sem("state_out_ready"), 1)

    def brr_gpsimd(eng):
        for j in range(1, 4):
            split_lo(eng, B_BRR + j, BRR_SLOTS[j])

    def brr_vector(eng):
        for c in range(NC):
            eng.wait_ge(sem("a_hi"), c + 1)
            eng.tensor_tensor(acts_lo[:, :, tokens_of(c)], a_stage[:, :, tokens_of(c)],
                              acts_hi[:, :, tokens_of(c)].bitcast(F32), ALU.subtract).then_inc(sem("a_lo"), 1)
        for j in range(4):
            for n in range(6):
                t, c = n // 3, n % 3
                eng.wait_ge(sem("br_full"), 6 * j + n + 1)
                if c == 0:
                    eng.wait_ge(sem(f"ga_loaded{t}"), 16 * (j + 1))
                eng.tensor_tensor(st[t][:, tokens_of(c)], ps[n][:, 0:CH], st[t][:, tokens_of(c)], ALU.mult).then_inc(sem("br_free"), 1)
            if j == 3:
                eng.wait_ge(sem("lf16_turned"), 1)
                eng.tensor_copy(new_logf[:], ps[6][:, 0:ST]).then_inc(sem("lf16_moved"), 1)
                eng.wait_ge(sem("lf16_moved"), 1)
                minus_sums(eng, new_f[:], new_logf[:], past_last[:]).then_inc(sem("new_f_ready"), 1)

    PAIRS = H // 2
    STEPS = 16

    def att_sync(eng):
        for t in range(2):
            eng.wait_ge(sem(f"z1_stored{t}"), 64)
            eng.wait_ge(sem(f"tok_stored{t}"), 16 * (8 * N_IT + 1))
        eng.wait_ge(sem("states_stored"), 64)
        eng.wait_ge(sem("past_stored"), 32)
        v_rows = o["v_prompt"][0, 0].rearrange("(m p) h d -> p m (h d)", p=128)
        with eng.Fori(0, PAIRS) as i:
            for hh in range(2):
                hd = i * 2 + hh
                eng.wait_ge(sem("pa_split"), hd + 1)
                for half in range(2):
                    rows = slice(64 * half, 64 * half + 64)
                    eng.dma_start(kf[rows, :], k_dram[ds(i * 128 + hh * 64, 64), 0:TP]).then_inc(sem("kq_loaded"), 16)
                    eng.dma_start(qf[rows, :], q_dram[ds(i * 128 + hh * 64, 64), 0:TP]).then_inc(sem("kq_loaded"), 16)
                eng.wait_ge(sem("pa_max"), i * 16 + 8 * hh + 8)
                eng.dma_start(kbias[hh][:], bias_dram[ds(hd, 1), :].to_broadcast([128, TP])).then_inc(sem(f"kbias_loaded{hh}"), 16)
                eng.wait_ge(sem("pa_pv"), i * 16 + 8 * hh + 8)
                eng.dma_start(vh[hh][:], v_rows[:, :, ds(hd * 64, 64)]).then_inc(sem(f"vh_loaded{hh}"), 16)

    def att_tensor(eng):
        eng.sem_inc(sem("pa_s"), 16)
        eng.sem_inc(sem("pa_pv"), 16)
        eng.wait_ge(sem("br_free"), 24)
        eng.wait_ge(sem("state_out_ready"), 2)
        eng.wait_ge(sem("lf16_moved"), 1)
        with eng.Fori(0, PAIRS) as i:
            def scores(k):
                hh, qi = k // 8, k % 8
                keys = 128 * (qi + 1)
                if qi == 0:
                    eng.wait_ge(sem("pa_split"), i * 2 + hh + 2)
                eng.wait_ge(sem("pa_max"), i * 16 + k - 2 + 1 + 16)
                lhs = q_hl[hh][:, 128 * qi:128 * qi + 128]
                for c0 in range(0, keys, 512):
                    c1 = min(c0 + 512, keys)
                    out = psum[:, 1024 * (k % 2) + c0:1024 * (k % 2) + c1]
                    eng.matmul(out, lhs, k_hi[hh][:, c0:c1], start=True, stop=False)
                    last = eng.matmul(out, lhs, k_lo[hh][:, c0:c1], start=False, stop=c1 < keys)
                last = eng.matmul(psum[:, 1024 * (k % 2) + keys - 128:1024 * (k % 2) + keys], ident_r[:], causal_r[:],
                                  start=False, stop=True)
                last.then_inc(sem("pa_s"), 1)

            def turn(k):
                hh, qi = k // 8, k % 8
                eng.wait_ge(sem("pa_exp"), i * 16 + k + 1)
                eng.wait_ge(sem("pa_c4"), i * 16 + k + 1)
                for kb in range(qi + 1):
                    if kb == 4:
                        eng.wait_ge(sem("pa_c5"), i * 8 + 4 * hh + qi - 4 + 1)
                    last = eng.transpose(ps[4 + kb // 4][:, 128 * (kb % 4):128 * (kb % 4) + 128],
                                         pr[k % 4][:, 128 * kb:128 * kb + 128], ident[:])
                    if kb == min(3, qi):
                        last.then_inc(sem("pa_t4"), 1)
                if qi >= 4:
                    last.then_inc(sem("pa_t5"), 1)

            def values(k):
                hh, qi = k // 8, k % 8
                if qi == 0:
                    eng.wait_ge(sem(f"vh_loaded{hh}"), i * 16 + 16)
                eng.wait_ge(sem("pa_out"), i * 16 + k + 1)
                eng.wait_ge(sem("pa_c4"), i * 16 + k + 2)
                for kb in range(qi + 1):
                    if kb == 4:
                        eng.wait_ge(sem("pa_c5"), i * 8 + 4 * hh + qi - 4 + 2)
                    last = eng.matmul(ps[6 + k % 2][:, 0:HD], pT[k % 2][:, 128 * kb:128 * kb + 128], vh[hh][:, kb, :],
                                      start=(kb == 0), stop=(kb == qi))
                last.then_inc(sem("pa_pv"), 1)

            scores(0)
            scores(1)
            eng.wait_ge(sem("pa_turned_in"), i * 2 + 1)
            for k in range(STEPS):
                if k + 2 < STEPS:
                    scores(k + 2)
                turn(k)
                if k >= 1:
                    values(k - 1)
            values(STEPS - 1)
            eng.wait_ge(sem("pa_out"), i * 16 + 16 + 2)
            eng.wait_ge(sem("pa_c4"), i * 16 + 16 + 1)
            eng.wait_ge(sem("pa_c5"), i * 8 + 8 + 1)
            for bk in range(2):
                for m in range(4):
                    last = eng.transpose(ps[4 + bk][:, 128 * m:128 * m + 128], att[:, 4 * bk + m, :], ident[:])
                last.then_inc(sem("pa_at"), 1)

    def split_head_hi(eng, i, hd, hh):
        eng.wait_ge(sem("kq_loaded"), hd * 64 + 64)
        eng.wait_ge(sem("pa_s"), hd * 8 + 8)
        eng.activation(k_hi[hh][:], kf[:], ACT.Copy)
        eng.activation(q_hl[hh][:], qf[:], ACT.Copy).then_inc(sem("pa_hi"), 1)

    def att_scalar(eng):
        eng.sem_inc(sem("pa_c4"), 1)
        split_head_hi(eng, 0, 0, 0)

        def body(i, last):
            def exp(k):
                keys = 128 * (k % 8 + 1)
                eng.wait_ge(sem("pa_neg"), i * 16 + k + 1)
                eng.activation(pr[k % 4][:, 0:keys], pr[k % 4][:, 0:keys], ACT.Exp, bias=stat[:, k % 4, 1:2],
                               accum_out=stat[:, k % 4, 2:3]).then_inc(sem("pa_exp"), 1)

            exp(0)
            for k in range(STEPS):
                if k + 1 < STEPS:
                    exp(k + 1)
                cols = 128 * min(4, k % 8 + 1)
                eng.wait_ge(sem("pa_t4"), i * 16 + k + 1)
                eng.wait_ge(sem("pa_pv"), i * 16 + k - 1 + 16)
                eng.activation(pT[k % 2][:, 0:cols], ps[4][:, 0:cols], ACT.Copy).then_inc(sem("pa_c4"), 1)
                if k == 1:
                    split_head_hi(eng, i, i * 2 + 1, 1)
                if k == 9 and not last:
                    split_head_hi(eng, i, i * 2 + 2, 0)
        with eng.Fori(0, PAIRS - 1) as i:
            body(i, False)
        body(PAIRS - 1, True)

    def att_gpsimd(eng):
        eng.sem_inc(sem("pa_split"), 1)

        def body(i, hh):
            hd = i * 2 + hh
            eng.wait_ge(sem("pa_hi"), hd + 1)
            eng.tensor_tensor(k_lo[hh][:], kf[:], k_hi[hh][:].bitcast(F32), ALU.subtract).then_inc(sem("pa_k_lo"), 1)
            eng.wait_ge(sem("pa_k_lo"), hd + 1)
            low = slice(64, 128)
            eng.tensor_tensor(q_hl[hh][low, :], qf[low, :], q_hl[hh][low, :].bitcast(F32), ALU.subtract).then_inc(sem("pa_split"), 1)
        with eng.Fori(0, PAIRS) as i:
            body(i, 0)
            body(i, 1)

    def att_vector(eng):
        eng.sem_inc(sem("pa_max"), 16)
        eng.sem_inc(sem("pa_c5"), 1)
        eng.sem_inc(sem("pa_out"), 2)
        eng.sem_inc(sem("pa_turned_in"), 1)
        with eng.Fori(0, PAIRS) as i:
            def maxima(k):
                hh, qi = k // 8, k % 8
                keys = 128 * (qi + 1)
                st_ = stat[:, k % 4, :]
                eng.wait_ge(sem("pa_s"), i * 16 + k + 1 + 16)
                if qi == 0:
                    eng.wait_ge(sem(f"kbias_loaded{hh}"), i * 16 + 16)
                eng.memset(wait_mark[:, 0:1], 0.0)
                eng.tensor_tensor_reduce(pr[k % 4][:, 0:keys], psum[:, 1024 * (k % 2):1024 * (k % 2) + keys],
                                         kbias[hh][:, 0:keys], 1.0, -3e38, ALU.add, ALU.max, st_[:, 0:1]).then_inc(sem("pa_max"), 1)
                eng.wait_ge(sem("pa_max"), i * 16 + k + 1 + 16)
                eng.tensor_scalar(st_[:, 1:2], st_[:, 0:1], -1.0, None, ALU.mult).then_inc(sem("pa_neg"), 1)

            def output(k):
                hh, qi = k // 8, k % 8
                st_ = stat[:, k % 4, :]
                eng.wait_ge(sem("pa_exp"), i * 16 + k + 1)
                eng.reciprocal(st_[:, 3:4], st_[:, 2:3]).then_inc(sem("pa_rec"), 1)
                eng.wait_ge(sem("pa_rec"), i * 16 + k + 1)
                eng.wait_ge(sem("pa_pv"), i * 16 + k + 1 + 16)
                eng.tensor_scalar(att[:, qi, HD * hh:HD * hh + HD], ps[6 + k % 2][:, 0:HD], st_[:, 3:4], None,
                                  ALU.mult).then_inc(sem("pa_out"), 1)

            maxima(0)
            maxima(1)
            for k in range(STEPS):
                hh, qi = k // 8, k % 8
                if k + 2 < STEPS:
                    maxima(k + 2)
                if qi >= 4:
                    cols = 128 * (qi - 3)
                    eng.wait_ge(sem("pa_t5"), i * 8 + 4 * hh + qi - 4 + 1)
                    eng.wait_ge(sem("pa_pv"), i * 16 + k - 1 + 16)
                    eng.tensor_copy(pT[k % 2][:, 512:512 + cols], ps[5][:, 0:cols]).then_inc(sem("pa_c5"), 1)
                if k >= 1:
                    output(k - 1)
            output(STEPS - 1)
            for bk in range(2):
                cols = slice(512 * bk, 512 * bk + 512)
                hi = acts_hi[:, ds(i, 1), cols].rearrange("p o t -> p (o t)")
                lo = acts_lo[:, ds(i, 1), cols].rearrange("p o t -> p (o t)")
                eng.wait_ge(sem("pa_at"), i * 2 + bk + 1)
                eng.tensor_scalar(hi, ps[4 + bk], 1.0, None, ALU.mult).then_inc(sem("pa_att_hi"), 1)
                eng.wait_ge(sem("pa_att_hi"), i * 2 + bk + 1)
                eng.tensor_tensor(lo, ps[4 + bk], hi.bitcast(F32), ALU.subtract).then_inc(sem("pa_turned_in"), 1)

    UNITS = 2 * SB

    def sat_sync(eng):
        eng.wait_ge(sem("pa_turned_in"), 2 * PAIRS + 1)
        eng.wait_ge(sem("qd_clear"), 1)
        k_rows = a["cache_k"][0].rearrange("b (m p) h d -> b p m (h d)", p=128)
        v_rows = a["cache_v"][0].rearrange("b (m p) h d -> p (b m) (h d)", p=128)

        def keys(b, g):
            u = b * 2 + g
            eng.wait_ge(sem("sa_sc"), u * 4 + 1)
            eng.dma_start(kc[g][:], k_rows[b][:, :, 512 * g:512 * g + 512]).then_inc(sem(f"kc_loaded{g}"), 16)
            toks = ds(b * ST + TP, ST)
            for half in range(2):
                src = q_dram[512 * g:512 * g + 512, :].rearrange("(p two d) t -> two d p t", two=2, d=HD)[half]
                eng.dma_start(qd[g][64 * half:64 * half + 64, :, ST * half:ST * half + ST], src[:, :, toks]).then_inc(sem(f"sa_small{g}"), 16)
            eng.dma_start(kn[g][:], k_dram[512 * g:512 * g + 512, :].rearrange("(p c) t -> c p t", c=128)[:, :, toks]).then_inc(sem(f"sa_small{g}"), 16)
            eng.wait_ge(sem("sa_pv"), u + 1)
            eng.dma_start(vn[g][:], o["v_sample"][0][b, :, 8 * g:8 * g + 8, :].rearrange("t h d -> t (h d)")).then_inc(sem(f"sa_small{g}"), 16)
            for h in range(8):
                eng.dma_start(sp[g][ST * h:ST * h + ST, :],
                              past_dram[ds(b * H + 8 * g + h, 1), :].to_broadcast([ST, PAST + ST])).then_inc(sem(f"sa_small{g}"), 16)

        def values(b, g):
            eng.wait_ge(sem("sa_pv"), b * 2 + g + 2)
            eng.dma_start(vc[:], v_rows[:, ds(b * 8, 8), 512 * g:512 * g + 512]).then_inc(sem("vc_loaded"), 16)

        keys(0, 0)
        with eng.Fori(0, SB - 1) as b:
            keys(b, 1)
            values(b, 0)
            keys(b + 1, 0)
            values(b, 1)
        keys(SB - 1, 1)
        values(SB - 1, 0)
        values(SB - 1, 1)


    def sat_tensor(eng):
        eng.sem_inc(sem("sa_sc"), 5)
        eng.sem_inc(sem("sa_pv"), 2)
        eng.wait_ge(sem("pa_turned_in"), 2 * PAIRS + 1)

        def scores(b, g):
            u = b * 2 + g
            base = 1536 * g

            def turn(p):
                for bk, name in enumerate(("sa_kev6", "sa_kev7")):
                    eng.wait_ge(sem(name), u * 4 + p + 1)
                    for m in range(4):
                        last = eng.transpose(ps[6 + bk][:, 128 * m:128 * m + 128],
                                             kc[g][:, 4 * bk + m, 128 * p:128 * p + 128], ident[:])
                    last.then_inc(sem(("sa_kt6", "sa_kt7")[bk]), 1)

            eng.wait_ge(sem(f"kc_loaded{g}"), b * 16 + 16)
            turn(0)
            eng.wait_ge(sem("sa_out"), u + 1)
            new = slice(base + PAST, base + PAST + ST)
            eng.matmul(psum[:, new], pick_r[:], causal_r[0:ST, 0:ST], start=True, stop=False, skip_group_check=True)
            for p in range(4):
                if p < 3:
                    turn(p + 1)
                if p == 0:
                    eng.wait_ge(sem(f"sa_small{g}"), b * 192 + 192)
                rows = slice(32 * p, 32 * p + 32)
                for bk, name in enumerate(("sa_kev6", "sa_kev7")):
                    eng.wait_ge(sem(name), u * 4 + p + 2)
                    eng.matmul(psum[rows, base + 512 * bk:base + 512 * bk + 512], qd[g][:, p, :],
                               kTs[p % 2][:, 512 * bk:512 * bk + 512], start=True, stop=True)
                eng.matmul(psum[rows, new], qd[g][:, p, :], kn[g][:, p, :], start=False, stop=True,
                           skip_group_check=True).then_inc(sem("sa_sc"), 1)

        def finish(b, g):
            u = b * 2 + g
            base = 1536 * g
            eng.wait_ge(sem("sa_norm"), u + 1)
            for kb in range(NEWK + 1):
                n = 128 if kb < NEWK else ST
                last = eng.transpose(psum[0:n, base + 128 * kb:base + 128 * kb + 128], sp[g][:, 128 * kb:128 * kb + n], ident[:])
                if kb in (3, 7, 8):
                    last.then_inc(sem(f"sa_pt{kb // 4}"), 1)
            eng.wait_ge(sem("sa_pe2"), u + 1)
            eng.wait_ge(sem("sa_pe1"), u + 1)
            eng.wait_ge(sem("vc_loaded"), u * 16 + 16)
            for p in range(4):
                out = psum[:, base + 1280 + 32 * p:base + 1280 + 32 * p + 32]
                for kb in range(NEWK):
                    eng.matmul(out, vc[:, kb, 128 * p:128 * p + 128], spT[:, kb, 32 * p:32 * p + 32], start=(kb == 0), stop=False)
                last = eng.matmul(out, vn[g][:, 128 * p:128 * p + 128], spT[0:ST, NEWK, 32 * p:32 * p + 32], start=False, stop=True)
            last.then_inc(sem("sa_pv"), 1)

        scores(0, 0)
        with eng.Fori(0, SB - 1) as b:
            scores(b, 1)
            finish(b, 0)
            scores(b + 1, 0)
            finish(b, 1)
        scores(SB - 1, 1)
        finish(SB - 1, 0)
        finish(SB - 1, 1)

    def sat_scalar(eng):
        eng.sem_inc(sem("sa_kev6"), 1)

        def stage(vb, vg, ub, ug):
            for p in range(4):
                if vb is not None:
                    v = vb * 2 + vg
                    eng.wait_ge(sem("sa_kt6"), v * 4 + p + 1)
                    eng.wait_ge(sem("sa_sc"), v * 4 + p + 4)
                    eng.activation(kTs[p % 2][:, 0:512], ps[6], ACT.Copy).then_inc(sem("sa_kev6"), 1)
                if p == 1 and ub is not None:
                    u = ub * 2 + ug
                    eng.wait_ge(sem("sa_neg"), u + 1)
                    eng.activation(sp[ug][:], sp[ug][:], ACT.Exp, bias=sstat[:, ug, 1:2],
                                   accum_out=sstat[:, ug, 2:3]).then_inc(sem("sa_exp"), 1)
            if ub is not None:
                u = ub * 2 + ug
                base = 1536 * ug
                eng.wait_ge(sem("sa_pt0"), u + 1)
                eng.wait_ge(sem("sa_pv"), u + 2)
                eng.activation(spT[:, 0:4, :], psum[:, base:base + 512].rearrange("p (k n) -> p k n", k=4), ACT.Copy)
                eng.wait_ge(sem("sa_pt2"), u + 1)
                eng.activation(spT[0:ST, NEWK, :], psum[0:ST, base + 1024:base + 1152], ACT.Copy).then_inc(sem("sa_pe2"), 1)

        stage(0, 0, None, None)
        with eng.Fori(0, SB - 1) as b:
            stage(b, 1, b, 0)
            stage(b + 1, 0, b, 1)
        stage(SB - 1, 1, SB - 1, 0)
        stage(None, None, SB - 1, 1)

    def sat_vector(eng):
        eng.sem_inc(sem("sa_kev7"), 1)
        eng.sem_inc(sem("sa_out"), 2)
        for g in range(2):
            last = eng.memset(qd[g][:], 0.0)
        last.then_inc(sem("qd_clear"), 1)

        def stage(vb, vg, ub, ug):
            for p in range(4):
                if vb is not None:
                    v = vb * 2 + vg
                    eng.wait_ge(sem("sa_kt7"), v * 4 + p + 1)
                    eng.wait_ge(sem("sa_sc"), v * 4 + p + 4)
                    eng.tensor_copy(kTs[p % 2][:, 512:1024], ps[7]).then_inc(sem("sa_kev7"), 1)
                if ub is None:
                    continue
                u = ub * 2 + ug
                s_ = sstat[:, ug, :]
                if p == 0:
                    eng.wait_ge(sem("sa_sc"), u * 4 + 4 + 5)
                    eng.memset(wait_mark[:, 1:2], 0.0)
                    eng.tensor_tensor_reduce(sp[ug][:], psum[:, 1536 * ug:1536 * ug + PAST + ST], sp[ug][:], 1.0, -3e38,
                                             ALU.add, ALU.max, s_[:, 0:1]).then_inc(sem("sa_max"), 1)
                    eng.wait_ge(sem("sa_max"), u + 1)
                    eng.tensor_scalar(s_[:, 1:2], s_[:, 0:1], -1.0, None, ALU.mult).then_inc(sem("sa_neg"), 1)
                if p == 2:
                    eng.wait_ge(sem("sa_exp"), u + 1)
                    eng.reciprocal(s_[:, 3:4], s_[:, 2:3]).then_inc(sem("sa_rec"), 1)
                    eng.wait_ge(sem("sa_rec"), u + 1)
                    eng.tensor_scalar(sp[ug][:], sp[ug][:], s_[:, 3:4], None, ALU.mult).then_inc(sem("sa_norm"), 1)
            if ub is not None:
                u = ub * 2 + ug
                base = 1536 * ug
                eng.wait_ge(sem("sa_pt1"), u + 1)
                eng.wait_ge(sem("sa_pv"), u + 2)
                eng.tensor_copy(spT[:, 4:8, :], psum[:, base + 512:base + 1024].rearrange("p (k n) -> p k n", k=4)).then_inc(sem("sa_pe1"), 1)
                eng.wait_ge(sem("sa_pv"), u + 1 + 2)
                out = psum[:, base + 1280:base + 1408].rearrange("p (k n) -> p k n", k=4)
                toks = ds(ub * ST + TP, ST)
                blocks = [(out[64 * half:64 * half + 64, :, ST * half:ST * half + ST],
                           acts_hi[64 * half:64 * half + 64, 4 * ug:4 * ug + 4, toks],
                           acts_lo[64 * half:64 * half + 64, 4 * ug:4 * ug + 4, toks]) for half in range(2)]
                for src, hi, lo in blocks:
                    last = eng.tensor_scalar(hi, src, 1.0, None, ALU.mult)
                last.then_inc(sem("sa_hi"), 1)
                eng.wait_ge(sem("sa_hi"), u + 1)
                for src, hi, lo in blocks:
                    last = eng.tensor_tensor(lo, src, hi.bitcast(F32), ALU.subtract)
                last.then_inc(sem("sa_out"), 1)

        stage(0, 0, None, None)
        with eng.Fori(0, SB - 1) as b:
            stage(b, 1, b, 0)
            stage(b + 1, 0, b, 1)
        stage(SB - 1, 1, SB - 1, 0)
        stage(None, None, SB - 1, 1)

    def pair_block(name):
        w = kview(a[name][0])
        return lambda j: w[:, :, 256 * j:256 * j + 256]

    def merge_loads_ahead(eng):
        for j in range(2):
            load_block(eng, B_BRA + j, PAIR_SLOTS[j], pair_block("w_br_att")(j))

    def merge_sync(eng):
        eng.wait_ge(sem("sa_out"), UNITS + 2)

        def gate(q):
            tile, c = q // 3, q % 3
            if q >= 2:
                eng.wait_ge(sem("m_free"), q - 1)
            eng.dma_start(gb_t[q % 2][:], gb_dram[128 * tile:128 * tile + 128, tokens_of(c)]).then_inc(sem(f"gb_loaded{q % 2}"), 16)
        gate(0)
        gate(1)
        for d in range(KT):
            eng.dma_start(zt[d][:], z1_dram[128 * d:128 * d + 128, :]).then_inc(sem("z1_loaded"), 16)
        load_block(eng, B_BRA + 2, PAIR_SLOTS[0], pair_block("w_br_att")(2))
        eng.dma_start(x[:].rearrange("p k t -> p (k t)"), x_dram).then_inc(sem("x_again"), 16)
        for q in range(2, 24):
            gate(q)
            if q == 6:
                load_block(eng, B_BRA + 3, PAIR_SLOTS[1], pair_block("w_br_att")(3))
            if q in (12, 18):
                j = q // 6 - 2
                load_block(eng, B_OUT + j, PAIR_SLOTS[j], pair_block("w_out")(j))
        for j in (2, 3):
            load_block(eng, B_OUT + j, PAIR_SLOTS[j % 2], pair_block("w_out")(j))

    def merge_tensor(eng):
        for block0, base, done in ((B_BRA, 0, "m_free"), (B_OUT, 24, "o_free")):
            for j in range(4):
                for n in range(6):
                    t, c = n // 3, n % 3
                    q = 6 * j + n
                    if block0 == B_OUT and j == 0:
                        eng.wait_ge(sem("m_free"), 24)
                        if t == 0:
                            eng.wait_ge(sem("z_lo"), 8 * c + 8)
                    elif j == 0:
                        eng.wait_ge(sem("sa_out"), UNITS + 2)
                    else:
                        eng.wait_ge(sem(done), q - 6 + 1)
                    if n == 0:
                        wait_block(eng, block0 + j)
                    whi, wlo = wcols(PAIR_SLOTS[j % 2][2], t)
                    for k in range(KT):
                        last = mm3(eng, ps[n][:, 0:CH], whi[k], wlo[k], acts_hi[:, k, tokens_of(c)],
                                   acts_lo[:, k, tokens_of(c)], k == 0, k == KT - 1,
                                   sem("w_used") if (n, k) == (0, 0) else None)
                    last.then_inc(sem("m_full"), 1)

    def pair_split(eng, block0, j):
        raw = PAIR_SLOTS[j % 2][0]
        split_hi(eng, block0 + j, PAIR_SLOTS[j % 2], {B_BRA: BRA_RAWS, B_OUT: OUT_RAWS}[block0][raw] + j // 2)

    def merge_scalar(eng):
        for j in range(1, 4):
            pair_split(eng, B_BRA, j)
        pair_split(eng, B_OUT, 0)
        eng.wait_ge(sem("m_free"), 24)
        eng.wait_ge(sem("m_full"), 24)
        for c in range(NC):
            for d in range(KT):
                eng.activation(acts_hi[:, d, tokens_of(c)], zt[d][:, tokens_of(c)], ACT.Copy).then_inc(sem("z_hi"), 1)
        for j in range(1, 4):
            pair_split(eng, B_OUT, j)

    def merge_gpsimd(eng):
        for j in range(1, 4):
            split_lo(eng, B_BRA + j, PAIR_SLOTS[j % 2])
        for j in range(4):
            split_lo(eng, B_OUT + j, PAIR_SLOTS[j % 2])

    def merge_vector(eng):
        for q in range(24):
            j, n = q // 6, q % 6
            tile, c = q // 3, q % 3
            eng.wait_ge(sem("m_full"), q + 1)
            eng.wait_ge(sem(f"gb_loaded{q % 2}"), 16 * (q // 2 + 1))
            if q == 0:
                eng.wait_ge(sem("z1_loaded"), 16 * KT)
            eng.tensor_tensor(gb_t[q % 2][:], ps[n][:, 0:CH], gb_t[q % 2][:], ALU.mult).then_inc(sem("m_step"), 1)
            eng.wait_ge(sem("m_step"), q + 1)
            z_ = zt[tile][:, tokens_of(c)]
            eng.tensor_tensor(z_, z_, gb_t[q % 2][:], ALU.add).then_inc(sem("m_free"), 1)
        for c in range(NC):
            for d in range(KT):
                eng.wait_ge(sem("z_hi"), 8 * c + d + 1)
                eng.tensor_tensor(acts_lo[:, d, tokens_of(c)], zt[d][:, tokens_of(c)],
                                  acts_hi[:, d, tokens_of(c)].bitcast(F32), ALU.subtract).then_inc(sem("z_lo"), 1)
        eng.wait_ge(sem("x_again"), 16)
        for q in range(24):
            d, c, n = q // 3, q % 3, q % 6
            eng.wait_ge(sem("m_full"), 24 + q + 1)
            add_gated(eng, ps[n], x, d, c, 5, "o_free", FF_PAIRS * KT + d)

    def x_set_up(eng):
        eng.wait_ge(sem("x_moved"), 2 * (T // 128) + CREDIT)
        eng.wait_ge(sem("mod_final"), 7)

    def x_after_ffn1(eng):
        eng.wait_ge(sem("y_free"), FF_PAIRS * 24 + CREDIT)

    def x_after_mixer(eng):
        eng.wait_ge(sem("o_free"), 24)

    block = ctx.enter_context(nc.Block())

    @block.sync
    def _(eng):
        setup_sync(eng)
        ffn_sync(eng, 0)
        proj_sync(eng)
        brr_sync(eng)
        merge_loads_ahead(eng)
        att_sync(eng)
        sat_sync(eng)
        merge_sync(eng)
        ffn_sync(eng, 1)
        final_sync(eng)

    @block.scalar
    def _(eng):
        setup_scalar(eng)
        norm_scalar(eng, 0, x_set_up)
        ffn_scalar(eng, 0)
        norm_scalar(eng, 1, x_after_ffn1)
        proj_scalar(eng)
        brr_scalar(eng)
        pair_split(eng, B_BRA, 0)
        att_scalar(eng)
        sat_scalar(eng)
        merge_scalar(eng)
        norm_scalar(eng, 2, x_after_mixer)
        ffn_scalar(eng, 1)
        final_scalar(eng)

    @block.gpsimd
    def _(eng):
        setup_gpsimd(eng)
        ffn_gpsimd(eng, 0)
        proj_gpsimd(eng)
        brr_gpsimd(eng)
        split_lo(eng, B_BRA, PAIR_SLOTS[0])
        att_gpsimd(eng)
        merge_gpsimd(eng)
        ffn_gpsimd(eng, 1)

    @block.tensor
    def _(eng):
        setup_tensor(eng)
        norm_tensor(eng, 0)
        ffn_tensor(eng, 0)
        norm_tensor(eng, 1)
        proj_tensor(eng)
        brr_tensor(eng)
        att_tensor(eng)
        sat_tensor(eng)
        merge_tensor(eng)
        norm_tensor(eng, 2)
        ffn_tensor(eng, 1)
        final_tensor(eng)

    @block.vector
    def _(eng):
        setup_vector(eng)
        norm_vector(eng, 0)
        ffn_vector(eng, 0)
        norm_vector(eng, 1)
        proj_vector(eng)
        brr_vector(eng)
        att_vector(eng)
        sat_vector(eng)
        merge_vector(eng)
        norm_vector(eng, 2)
        ffn_vector(eng, 1)
        final_vector(eng)


_INS = ['x_prompt', 'x_sample', 'cache_k', 'cache_v', 'cache_logf', 'state_conv', 'state_rglru', 'c_prompt',
        'c_sample', 'w_ada', 'b_ada', 'ffn1_norm', 'ffn1_w1', 'ffn1_w3', 'ffn1_w2', 'mix_norm', 'w_in', 'b_fgt',
        'conv_w', 'conv_b', 'rg_wa', 'rg_ba', 'rg_wx', 'rg_bx', 'rg_lam', 'w_br_rnn', 'w_br_att', 'w_out',
        'ffn2_norm', 'ffn2_w1', 'ffn2_w3', 'ffn2_w2', 'final_norm', 'w_ada_f', 'b_ada_f']
_OUTS = [('y_prompt', (1, TP, D)), ('y_sample', (SB, ST, D)),
         ('k_prompt', (1, 1, TP, H, HD)), ('v_prompt', (1, 1, TP, H, HD)), ('logf_prompt', (1, 1, TP, H)),
         ('conv_prompt', (1, 1, CONV_W - 1, D)), ('rglru_prompt', (1, 1, D)),
         ('k_sample', (1, SB, ST, H, HD)), ('v_sample', (1, SB, ST, H, HD)), ('logf_sample', (1, SB, ST, H)),
         ('conv_sample', (1, SB, CONV_W - 1, D)), ('rglru_sample', (1, SB, D))]


def kernel(**inputs):
    import concourse.bacc as bacc
    from concourse.bass_utils import run_bass_kernel_spmd

    nc = bacc.Bacc("TRN2", target_bir_lowering=False, num_devices=1)
    arrays, ins, outs = {}, {}, {}
    for name in _INS:
        arrays[f"in_{name}"] = np.ascontiguousarray(inputs[name])
        ins[name] = nc.dram_tensor(f"in_{name}", arrays[f"in_{name}"].shape, F32, kind="ExternalInput").ap()
    for name, shape in _OUTS:
        outs[name] = nc.dram_tensor(f"out_{name}", shape, F32, kind="ExternalOutput").ap()
    build(nc, ins, outs)
    got = run_bass_kernel_spmd(nc, [arrays], core_ids=[0]).results[0]
    return tuple(got[f"out_{name}"] for name, _ in _OUTS)
```

```python
import numpy as np
from contextlib import ExitStack

import concourse.bass as bass
from concourse import mybir

F32 = mybir.dt.float32
F32R = mybir.dt.float32r
ALU = mybir.AluOpType
ACT = mybir.ActivationFunctionType


D = 1024
TP, SB, ST = 1024, 8, 16
TS = SB * ST
T = TP + TS
PAST = 1024
H, HD = 16, 64
KT = D // 128
CH = 384
NC = T // CH
CP = TP - (NC - 1) * CH
DFF = 2816
FF_PAIRS = DFF // 256
NMOD = 11
NSEQ = 1 + SB
CONV_W = 4
EPS = 1e-6
MASKED = -float(2 ** 100)
CREDIT = 4
ds = bass.ds


def tokens_of(chunk):
    return slice(chunk * CH, (chunk + 1) * CH)


def build(nc, a, o):
    with ExitStack() as ctx:
        program(nc, ctx, a, o)


def program(nc, ctx, a, o):
    def sb(stack, name, shape, dt=F32):
        return stack.enter_context(nc.sbuf_tensor(name, shape, dt))

    S = {}

    def sem(name):
        if name not in S:
            S[name] = ctx.enter_context(nc.semaphore(name))
        return S[name]

    psum = ctx.enter_context(nc.psum_tensor("psum", [128, 8 * 512], F32))
    ps = [psum[:, 512 * n:512 * n + 512] for n in range(8)]

    adaf = ExitStack()
    ada_w = [sb(adaf, f"ada_w{n}", [128, KT, 512]) for n in range(4)]
    adaf.close()
    normf = ExitStack()
    sq = sb(normf, "sq", [128, KT, T])
    h_f = sb(normf, "h_f", [128, KT, T])
    normf.close()
    acts_hi = sb(ctx, "acts_hi", [128, KT, T], F32R)
    acts_lo = sb(ctx, "acts_lo", [128, KT, T], F32R)
    w_raw = [sb(ctx, f"w_raw{n}", [128, 2048]) for n in range(2)]
    w_hi = [sb(ctx, f"w_hi{n}", [128, 2048], F32R) for n in range(2)]
    w_lo = [sb(ctx, f"w_lo{n}", [128, 2048], F32R) for n in range(2)]
    mods = sb(ctx, "mods", [128, NMOD, KT, NSEQ])
    params = sb(ctx, "params", [128, 88 + 96])
    ident = sb(ctx, "ident", [128, 128])
    ones = sb(ctx, "ones", [128, 128])
    eps_col = sb(ctx, "eps_col", [128, 1])
    conv_state = sb(ctx, "conv_state", [128, SB * 3 * KT])
    h0 = sb(ctx, "h0", [128, SB * KT])
    states = sb(ctx, "states", [128, KT, 36])
    sp4 = sb(ctx, "sp4", [128, KT])
    lam_t = [sb(ctx, f"lam_t{n}", [128, KT]) for n in range(4)]
    past_last = sb(ctx, "past_last", [128, 1])
    tiny_col = sb(ctx, "tiny_col", [128, 1])
    wait_mark = sb(ctx, "wait_mark", [1, 2])
    b_fgt_col = sb(ctx, "b_fgt_col", [H, 1])
    wfl_hi = sb(ctx, "wfl_hi", [128, KT, H], F32R)
    wfl_lo = sb(ctx, "wfl_lo", [128, KT, H], F32R)
    new_logf = sb(ctx, "new_logf", [128, ST])
    new_f = sb(ctx, "new_f", [128, ST])
    ident_r = sb(ctx, "ident_r", [128, 128], F32R)
    causal_r = sb(ctx, "causal_r", [128, 128], F32R)
    pick_r = sb(ctx, "pick_r", [ST, 128], F32R)
    G_FFN1, G_MIX, G_FFN2, G_FINAL, G_CONVW, G_CONVB, G_BA, G_BX, G_LAM = (
        88, 96, 104, 112, 120, 152, 160, 168, 176)

    set2 = ExitStack()
    w_hi.append(sb(set2, "w_hi2", [128, 2048], F32R))
    w_lo.append(sb(set2, "w_lo2", [128, 2048], F32R))
    xs = ExitStack()
    x = sb(xs, "x", [128, KT, T])

    setup = ExitStack()
    x_rows = [sb(setup, f"x_rows{n}", [128, D]) for n in range(2)]
    vec_rows = [sb(setup, "vec_rows0", [88, 128]), sb(setup, "vec_rows1", [96, 128])]
    c_rows = sb(setup, "c_rows", [NSEQ, D])
    cT = sb(setup, "cT", [128, KT, NSEQ])
    mod_rows = [sb(setup, f"mod_rows{n}", [NSEQ, 512]) for n in range(2)]
    state_rows = [sb(setup, "h0_rows", [SB * KT, 128])] + [sb(setup, f"conv_rows{n}", [96, 128]) for n in range(2)]
    wfl_raw = sb(setup, "wfl_raw", [128, KT, H])
    mask_f = sb(setup, "mask_f", [128, 128])
    past_rows = sb(setup, "past_rows", [128, PAST // 128, SB * H])
    setup.close()

    ffnf = ExitStack()
    u_hi = sb(ffnf, "u_hi", [128, 2, T], F32R)
    u_lo = sb(ffnf, "u_lo", [128, 2, T], F32R)
    gated = [sb(ffnf, f"gated{n}", [128, CH]) for n in range(2)]
    u_f = [sb(ffnf, f"u_f{n}", [128, CH]) for n in range(2)]
    s_tmp = [sb(ffnf, f"s_tmp{n}", [128, SB, ST]) for n in range(2)]
    ffnf.close()

    finalf = ExitStack()
    y_rows = [sb(finalf, f"y_rows{n}", [128, D]) for n in range(2)]
    finalf.close()
    xs.close()

    projf = ExitStack()
    st = [sb(projf, f"st{n}", [128, T]) for n in range(2)]
    tok = [sb(projf, f"tok{n}", [128, 3, 128]) for n in range(2)]
    lft = sb(projf, "lft", [128, T // 128, H])
    rnnf = ExitStack()
    PAD = CONV_W - 1
    XP = PAD + TP
    xpad = [sb(rnnf, f"xpad{n}", [128, XP + SB * (PAD + ST)]) for n in range(2)]
    xc = [sb(rnnf, f"xc{n}", [128, T]) for n in range(2)]
    rt = [sb(rnnf, f"rt{n}", [128, T]) for n in range(2)]
    it = [sb(rnnf, f"it{n}", [128, T]) for n in range(2)]
    gl = [sb(rnnf, f"gl{n}", [128, T]) for n in range(2)]
    bd = sb(rnnf, "bd", [128, 4, 128])
    tmp8 = [sb(rnnf, f"tmp8_{n}", [128, SB]) for n in range(2)]
    gate_p = sb(rnnf, "gate_p", [128, 2, 3])
    rnnf.close()
    brrf = ExitStack()
    a_stage = sb(brrf, "a_stage", [128, KT, T])
    state_out = sb(brrf, "state_out", [36, D])
    lf16 = sb(brrf, "lf16", [ST, 128])
    brrf.close()
    projf.close()
    set2.close()

    patf = ExitStack()
    kf = sb(patf, "kf", [128, TP])
    qf = sb(patf, "qf", [128, TP])
    k_hi = [sb(patf, "k_hi0", [128, TP], F32R)]
    q_hl = [sb(patf, "q_hl0", [128, TP], F32R)]
    k_hi.append(sb(patf, "k_hi1", [128, TP], F32R))
    q_hl.append(sb(patf, "q_hl1", [128, TP], F32R))
    k_lo1 = sb(patf, "k_lo1", [128, TP], F32R)
    vh = [sb(patf, f"vh{n}", [128, TP // 128, HD]) for n in range(2)]
    kbias = [sb(patf, f"kbias{n}", [128, TP]) for n in range(2)]
    pr = [sb(patf, f"pr{n}", [128, TP]) for n in range(4)]
    pT = [sb(patf, f"pT{n}", [128, TP]) for n in range(2)]
    att = sb(patf, "att", [128, TP // 128, 128])
    stat = sb(patf, "stat", [128, 4, 4])
    before = 16 * TP + 2 * 8 * HD + 16
    brr_frame = 2 * 2048 + (2 + KT) * T + 2 * 3 * 128 + T // 128 * H + D + 128
    sb(patf, "patf_gap", [128, brr_frame - before])
    k_lo = [sb(patf, "k_lo0", [128, TP], F32R), k_lo1]
    patf.close()

    satf = ExitStack()
    NEWK = PAST // 128
    kc = [sb(satf, f"kc{n}", [128, NEWK, 512]) for n in range(2)]
    vc = sb(satf, "vc", [128, NEWK, 512])
    kTs = [sb(satf, f"kTs{n}", [128, PAST]) for n in range(2)]
    kn = [sb(satf, f"kn{n}", [128, 4, ST]) for n in range(2)]
    vn = [sb(satf, f"vn{n}", [ST, 512]) for n in range(2)]
    qd = [sb(satf, f"qd{n}", [128, 4, 2 * ST]) for n in range(2)]
    sp = [sb(satf, f"sp{n}", [128, PAST + ST]) for n in range(2)]
    spT = sb(satf, "spT", [128, NEWK + 1, 128])
    sstat = sb(satf, "sstat", [128, 2, 4])
    o_rows = sb(satf, "o_rows", [128, 128])
    satf.close()

    zf = ExitStack()
    zt = [sb(zf, f"z{n}", [128, T]) for n in range(3)]
    gb_t = [sb(zf, "gb_t0", [128, CH])]
    sb(zf, "z_gap", [128, 4096 - 3 * T - CH])
    sb(zf, "x_again", [128, KT, T])
    zt += [sb(zf, f"z{n}", [128, T]) for n in range(3, KT)]
    gb_t.append(sb(zf, "gb_t1", [128, CH]))
    zf.close()

    CONSTS = 4
    NORMS_BEFORE = 3
    B_FFN1 = 0
    B_PROJ = B_FFN1 + 3 * FF_PAIRS
    N_PROJ = 28
    B_BRR = B_PROJ + N_PROJ
    B_BRA = B_BRR + 4
    B_OUT = B_BRA + 4
    B_FFN2 = B_OUT + 4
    FFN_SLOTS = [(0, 1, 2, 3), (1, 2, 0, 3), (0, 2, 1, 3)]
    PROJ_SLOTS = [(0, 1, 2, 3), (1, 2, 0, 2), (0, 2, 1, 3), (1, 2, 2, 3), (0, 2, 0, 3), (1, 2, 1, 3), (0, 2, 0, 2)]
    BRR_SLOTS = [(0, 1, 2, 3), (1, 2, 1, 3), (0, 2, 0, 3), (1, 2, 1, 2)]
    PAIR_SLOTS = [(0, 2, 0, 2), (1, 2, 1, 2)]

    FFN1_RAWS = (0, 0)
    PROJ_RAWS = (FFN1_RAWS[0] + 2 * FF_PAIRS, FFN1_RAWS[1] + FF_PAIRS)
    BRR_RAWS = (PROJ_RAWS[0] + 16, PROJ_RAWS[1] + 12)
    BRA_RAWS = (BRR_RAWS[0] + 2, BRR_RAWS[1] + 2)
    OUT_RAWS = (BRA_RAWS[0] + 2, BRA_RAWS[1] + 2)
    FFN2_RAWS = (OUT_RAWS[0] + 2, OUT_RAWS[1] + 2)

    def load_block(eng, block, slot, source):
        raw, ago, _, _ = slot
        eng.wait_ge(sem("w_lo_done"), block - ago + 1 + CREDIT)
        eng.dma_start(w_raw[raw][:].rearrange("p (k n) -> p k n", n=source.shape[-1]), source).then_inc(
            sem(f"w_raw_loaded{raw}"), 16)

    def split_hi(eng, block, slot, loads_before):
        raw, _, st, ago = slot
        eng.wait_ge(sem(f"w_raw_loaded{raw}"), 16 * (loads_before + 1))
        eng.wait_ge(sem("w_used"), block - ago + 1 + CREDIT)
        eng.activation(w_hi[st][:], w_raw[raw][:], ACT.Copy).then_inc(sem("w_hi_done"), 1)

    def split_lo(eng, block, slot):
        raw, _, st, _ = slot
        eng.wait_ge(sem("w_hi_done"), block + 1)
        eng.tensor_tensor(w_lo[st][:], w_raw[raw][:], w_hi[st][:].bitcast(F32), ALU.subtract).then_inc(
            sem("w_lo_done"), 1)

    def wait_block(eng, block):
        eng.wait_ge(sem("w_lo_done"), block + 1 + CREDIT)

    def mm3(eng, out, whi, wlo, ahi, alo, first, last, opens=None):
        pass1 = eng.matmul(out, whi, ahi, start=first, stop=False)
        if opens is not None:
            pass1.then_inc(opens, 1)
        eng.matmul(out, whi, alo, start=False, stop=False)
        return eng.matmul(out, wlo, ahi, start=False, stop=last)

    def wcols(st, tile):
        h = w_hi[st][:].rearrange("p (k n) -> p k n", n=256)
        l = w_lo[st][:].rearrange("p (k n) -> p k n", n=256)
        return [h[:, k, 128 * tile:128 * tile + 128] for k in range(KT)], [l[:, k, 128 * tile:128 * tile + 128] for k in range(KT)]

    def kview(w):
        return w.rearrange("(k p) n -> p k n", p=128)

    ADA_HALVES = 2 * NMOD
    w_ada_v = kview(a["w_ada"][0])
    w_adaf_v = kview(a["w_ada_f"])

    def scratch(name, shape):
        return nc.dram_tensor(name, shape, F32, kind="Internal").ap()

    x_dram = scratch("x_spill", [128, KT * T])
    q_dram, k_dram, a_dram, ga_dram, gb_dram, z1_dram = (
        scratch(name, [D, T]) for name in ("q_t", "k_t", "a_t", "gate_a_t", "gate_b_t", "z1_t"))
    bias_dram = scratch("prompt_bias", [H, TP])
    past_dram = scratch("sample_bias", [SB * H, PAST + ST])
    COL_XR, COL_GR, COL_Q, COL_K, COL_V, COL_FL = (D * n for n in range(6))
    COL_GA, COL_GB = COL_FL + H, COL_FL + H + D

    def minus_sums(eng, out, logf, initial):
        return eng.tensor_tensor_scan(out, ones[0:out.shape[0], 0:1].to_broadcast(list(out.shape)), logf, initial,
                                      ALU.mult, ALU.subtract)

    LOG1P_STEPS = 8

    def log1p_scalar(eng, u, name):
        eng.wait_ge(sem(name + "_dve"), 2)
        eng.activation(u, u, ACT.Ln).then_inc(sem(name + "_act"), 1)

    def log1p_vector(eng, tiles, name, e_ready):
        e, u, d, flag = tiles
        dve, act = sem(name + "_dve"), sem(name + "_act")
        eng.wait_ge(act, e_ready)
        eng.tensor_scalar(u, e, 1.0, None, ALU.add).then_inc(dve, 1)
        eng.wait_ge(dve, 1)
        eng.tensor_scalar(d, u, -1.0, None, ALU.add).then_inc(dve, 1)
        eng.wait_ge(dve, 2)
        eng.tensor_scalar(flag, d, 0.0, None, ALU.is_equal).then_inc(dve, 1)
        eng.wait_ge(dve, 3)
        eng.tensor_tensor(d, d, flag, ALU.add).then_inc(dve, 1)
        eng.wait_ge(dve, 4)
        eng.reciprocal(d, d).then_inc(dve, 1)
        eng.wait_ge(act, e_ready + 1)
        eng.tensor_tensor(u, u, flag, ALU.add).then_inc(dve, 1)
        eng.wait_ge(dve, 6)
        eng.tensor_tensor(u, u, d, ALU.mult).then_inc(dve, 1)
        eng.wait_ge(dve, 7)
        eng.tensor_tensor(e, e, u, ALU.mult).then_inc(dve, 1)
        eng.wait_ge(dve, 8)

    def setup_sync(eng):
        for n in range(2):
            rows = (["b_ada", "b_ada_f"], ["ffn1_norm", "mix_norm", "ffn2_norm", "final_norm", "conv_w",
                                           "conv_b", "rg_ba", "rg_bx", "rg_lam"])[n]
            at = 0
            for name in rows:
                v = a[name]
                v = {1: lambda v: v.rearrange("(r c) -> r c", c=128),
                     2: lambda v: v.rearrange("l (r c) -> (l r) c", c=128),
                     3: lambda v: v.rearrange("l w (r c) -> (l w r) c", c=128)}[len(v.shape)](v)
                eng.dma_start(vec_rows[n][at:at + v.shape[0], :], v).then_inc(sem("vec_loaded"), 16)
                at += v.shape[0]
        eng.dma_start(c_rows[0:1, :], a["c_prompt"]).then_inc(sem("c_loaded"), 16)
        eng.dma_start(c_rows[1:NSEQ, :], a["c_sample"]).then_inc(sem("c_loaded"), 16)
        xp = a["x_prompt"][0].rearrange("(m p) d -> m p d", p=128)

        def load_ada(h, slot, source):
            eng.wait_ge(sem("ada_full"), h + 1)
            eng.dma_start(ada_w[slot][:], source).then_inc(sem(f"ada_loaded{slot}"), 16)

        def load_x(slot, tile, source):
            eng.wait_ge(sem("x_turned"), tile * 2 - 2 + CREDIT)
            eng.dma_start(x_rows[slot][:], source).then_inc(sem(f"x_rows_loaded{slot}"), 16)

        with eng.Fori(0, 4) as i:
            for k in range(4):
                load_ada(i * 4 + k, k, w_ada_v[:, :, ds((i * 4 + k) * 512, 512)])
                if k % 2 == 1:
                    load_x(k // 2, i * 2 + k // 2, xp[i * 2 + k // 2])
        load_x(0, TP // 128, a["x_sample"].rearrange("s t d -> (s t) d"))
        eng.dma_start(state_rows[0][:], a["state_rglru"].rearrange("l s (r c) -> (l s r) c", c=128)).then_inc(sem("state_loaded"), 16)
        conv_src = a["state_conv"].rearrange("l s j (r c) -> (l s j r) c", c=128)
        for n in range(2):
            eng.dma_start(state_rows[1 + n][:], conv_src[96 * n:96 * n + 96, :]).then_inc(sem("state_loaded"), 16)
        eng.dma_start(wfl_raw[:], kview(a["w_in"][0])[:, :, COL_FL:COL_FL + H]).then_inc(sem("fl_loaded"), 16)
        eng.dma_start(b_fgt_col[:], a["b_fgt"].rearrange("l h -> h l")).then_inc(sem("fl_loaded"), 16)
        for b in range(SB):
            eng.dma_start(past_rows[:, :, H * b:H * b + H], a["cache_logf"][0, b].rearrange("(k p) h -> p k h", p=128)).then_inc(sem("past_loaded"), 16)
        for h in range(16, ADA_HALVES):
            view, at = (w_ada_v, h) if h < 18 else (w_adaf_v, h - 18)
            load_ada(h, h % 4, view[:, :, 512 * at:512 * at + 512])
        eng.wait_ge(sem("bank7_moved"), 3)
        eng.dma_start(past_dram[:, 0:PAST], past_rows[:].rearrange("p k n -> p (k n)")).then_inc(sem("past_stored"), 16)

    def setup_scalar(eng):
        eng.sem_inc(sem("proj_free"), 6)
        eng.sem_inc(sem("tok_moved"), 2)
        eng.sem_inc(sem("ri_moved"), 2)
        for n in range(2):
            eng.sem_inc(sem(f"tok_stored{n}"), 16)
            eng.sem_inc(sem(f"st_stored{n}"), 16)
            eng.sem_inc(sem(f"a_stored{n}"), 16)
        eng.wait_ge(sem("c_loaded"), 32)
        eng.activation(c_rows[:], c_rows[:], ACT.Silu).then_inc(sem("c_act"), 1)
        eng.wait_ge(sem("setup_turned"), 2)
        eng.activation(cT[:], ps[4][:, 0:KT * NSEQ].rearrange("p (k s) -> p k s", k=KT),
                       ACT.Copy).then_inc(sem("c_act"), 1)
        eng.wait_ge(sem("const"), CONSTS)
        eng.activation(ident_r[:], ident[:], ACT.Copy).then_inc(sem("const_split"), 1)
        eng.wait_ge(sem("const"), CONSTS + 2)
        eng.activation(causal_r[:], mask_f[:], ACT.Copy).then_inc(sem("const_split"), 1)
        eng.wait_ge(sem("const"), CONSTS + 4)
        eng.activation(pick_r[:], mask_f[0:ST, :], ACT.Copy).then_inc(sem("const_split"), 1)
        eng.wait_ge(sem("fl_loaded"), 32)
        eng.activation(wfl_hi[:], wfl_raw[:], ACT.Copy).then_inc(sem("const_split"), 1)
        eng.wait_ge(sem("params_ready"), 1)
        eng.activation(lam_t[0][:], params[:, G_LAM:G_LAM + KT], ACT.Abs).then_inc(sem("lam_act"), 1)
        eng.wait_ge(sem("lam_act"), 1)
        eng.activation(lam_t[0][:], lam_t[0][:], ACT.Exp, scale=-1.0).then_inc(sem("lam_act"), 1)
        log1p_scalar(eng, lam_t[1][:], "lam")

    def setup_gpsimd(eng):
        eng.sem_inc(sem("w_lo_done"), CREDIT)
        eng.memset(ident[:], 0.0).then_inc(sem("const"), 1)
        eng.memset(ones[:], 1.0).then_inc(sem("const"), 1)
        eng.memset(eps_col[:], EPS).then_inc(sem("const"), 1)
        eng.wait_ge(sem("const"), 3)
        eng.affine_select(out=ident[:], in_=ident[:], compare_op=ALU.not_equal, fill=1.0, base=0,
                          pattern=[[-1, 128]], channel_multiplier=1).then_inc(sem("const"), 1)
        eng.memset(mask_f[:], 0.0).then_inc(sem("const"), 1)
        eng.wait_ge(sem("const"), CONSTS + 1)
        eng.affine_select(out=mask_f[:], in_=mask_f[:], compare_op=ALU.is_ge, fill=MASKED, base=0,
                          pattern=[[-1, 128]], channel_multiplier=1).then_inc(sem("const"), 1)
        eng.wait_ge(sem("const_split"), 2)
        eng.memset(mask_f[0:ST, :], 0.0).then_inc(sem("const"), 1)
        eng.wait_ge(sem("const"), CONSTS + 3)
        eng.affine_select(out=mask_f[0:ST, :].rearrange("p (h q) -> p h q", q=ST),
                          in_=mask_f[0:ST, :].rearrange("p (h q) -> p h q", q=ST), compare_op=ALU.not_equal,
                          fill=1.0, base=0, pattern=[[0, 8], [-1, ST]], channel_multiplier=1).then_inc(sem("const"), 1)


    def setup_tensor(eng):
        eng.sem_inc(sem("w_used"), CREDIT - 1)
        eng.sem_inc(sem("x_turned"), CREDIT)
        eng.sem_inc(sem("ada_full"), CREDIT)
        eng.sem_inc(sem("pa_s"), 16)
        eng.sem_inc(sem("pa_pv"), 16)
        eng.sem_inc(sem("sa_sc"), 5)
        eng.wait_ge(sem("const"), CONSTS)
        eng.wait_ge(sem("vec_loaded"), 16 * 11)
        eng.transpose(ps[6][:, 0:88], vec_rows[0][:], ident[0:88, 0:88])
        eng.transpose(ps[6][:, 88:184], vec_rows[1][:], ident[0:96, 0:96]).then_inc(sem("setup_turned"), 1)
        eng.wait_ge(sem("c_act"), 1)
        for k in range(KT):
            last = eng.transpose(ps[4][:, NSEQ * k:NSEQ * k + NSEQ], c_rows[:, 128 * k:128 * k + 128],
                                 ident[0:NSEQ, 0:NSEQ])
        last.then_inc(sem("setup_turned"), 1)

        def turn_x(slot, tile, loads):
            eng.wait_ge(sem(f"x_rows_loaded{slot}"), 16 * loads)
            for half in range(2):
                eng.wait_ge(sem("x_moved"), tile * 2 + half + 1)
                for k in range(4):
                    last = eng.transpose(ps[2 * slot + half][:, 128 * k:128 * k + 128],
                                         x_rows[slot][:, 512 * half + 128 * k:512 * half + 128 * k + 128], ident[:])
                last.then_inc(sem("x_turned"), 1)

        def ada(h, slot, loads):
            eng.wait_ge(sem(f"ada_loaded{slot}"), 16 * loads)
            for k in range(KT):
                last = eng.matmul(ps[4 + slot % 2][0:NSEQ, :], cT[:, k, :], ada_w[slot][:, k, :],
                                  start=(k == 0), stop=(k == KT - 1))
            last.then_inc(sem("ada_full"), 1)

        def turn_rows(h, slot):
            eng.wait_ge(sem("mod_rows_ready"), h + 1)
            eng.wait_ge(sem("mod_ready"), h + 1)
            for t in range(4):
                last = eng.matmul(ps[6][:, NSEQ * t:NSEQ * t + NSEQ], mod_rows[slot % 2][:, 128 * t:128 * t + 128],
                                  ident[0:NSEQ, 0:NSEQ], start=True, stop=True)
            last.then_inc(sem("mod_turned"), 1)

        eng.wait_ge(sem("c_act"), 2)
        ada(0, 0, 1)
        with eng.Fori(0, 4) as i:
            for k in range(4):
                h = i * 4 + k
                ada(h + 1, (k + 1) % 4, i + 1 + (k + 1) // 4)
                turn_rows(h, k)
                if k % 2 == 1:
                    turn_x(k // 2, i * 2 + k // 2, i + 1)
        turn_x(0, TP // 128, TP // 256 + 1)
        eng.wait_ge(sem("state_loaded"), 48)
        eng.transpose(ps[7][:, 0:64], state_rows[0][:], ident[0:64, 0:64])
        for n in range(2):
            last = eng.transpose(ps[7][:, 64 + 96 * n:160 + 96 * n], state_rows[1 + n][:], ident[0:96, 0:96])
        last.then_inc(sem("states_turned"), 1)
        eng.wait_ge(sem("past_loaded"), 16 * SB)
        for half in range(2):
            eng.wait_ge(sem("bank7_moved"), half + 1)
            for k in range(4):
                last = eng.transpose(ps[7][:, 128 * k:128 * k + 128], past_rows[:, 4 * half + k, :], ident[:])
            last.then_inc(sem("states_turned"), 1)
        for h in range(16, ADA_HALVES):
            if h + 1 < ADA_HALVES:
                ada(h + 1, (h + 1) % 4, (h + 1) // 4 + 1)
            turn_rows(h, h % 4)

    def setup_vector(eng):
        eng.sem_inc(sem("x_moved"), CREDIT)
        eng.sem_inc(sem("mod_ready"), 1)
        for name in ("u_free", "y_free"):
            eng.sem_inc(sem(name), CREDIT)
        eng.wait_ge(sem("setup_turned"), 1)
        eng.tensor_copy(params[:], ps[6][:, 0:184]).then_inc(sem("params_ready"), 1)
        def move_x(slot, tile):
            for half in range(2):
                eng.wait_ge(sem("x_turned"), tile * 2 + half + 1 + CREDIT)
                eng.tensor_copy(x[:, 4 * half:4 * half + 4, ds(tile * 128, 128)],
                                ps[2 * slot + half][:].rearrange("p (k n) -> p k n", k=4)).then_inc(sem("x_moved"), 1)

        def copy_rows(h, slot):
            eng.wait_ge(sem("ada_full"), h + 1 + CREDIT)
            eng.tensor_copy(mod_rows[slot % 2][:], ps[4 + slot % 2][0:NSEQ, :]).then_inc(sem("mod_rows_ready"), 1)

        def add_bias(h, mod, half):
            eng.wait_ge(sem("mod_turned"), h + 1)
            eng.tensor_tensor(mods[:, mod, 4 * half:4 * half + 4, :],
                              ps[6][:, 0:4 * NSEQ].rearrange("p (k s) -> p k s", k=4),
                              params[:, ds(h * 4, 4)].unsqueeze(2).to_broadcast([128, 4, NSEQ]),
                              ALU.add).then_inc(sem("mod_ready"), 1)

        eng.wait_ge(sem("params_ready"), 1)
        copy_rows(0, 0)
        with eng.Fori(0, 4) as i:
            for k in range(4):
                copy_rows(i * 4 + k + 1, (k + 1) % 4)
                add_bias(i * 4 + k, i * 2 + k // 2, k % 2)
                if k % 2 == 1:
                    move_x(k // 2, i * 2 + k // 2)
        move_x(0, TP // 128)
        eng.wait_ge(sem("states_turned"), 1)
        eng.tensor_copy(h0[:], ps[7][:, 0:64])
        eng.tensor_copy(conv_state[:], ps[7][:, 64:256]).then_inc(sem("bank7_moved"), 1)
        past_f = past_rows[:].rearrange("p k n -> p (k n)")
        for half in range(2):
            eng.wait_ge(sem("states_turned"), half + 2)
            eng.wait_ge(sem("bank7_moved"), half + 1)
            minus_sums(eng, past_f[:, 512 * half:512 * half + 512], ps[7], past_f[:, 511:512] if half else 0.0).then_inc(sem("bank7_moved"), 1)
        eng.wait_ge(sem("bank7_moved"), 3)
        eng.tensor_copy(past_last[:], past_rows[:, PAST // 128 - 1, 127:128])
        eng.memset(tiny_col[:], 2.0 ** -100)
        eng.wait_ge(sem("const_split"), 4)
        eng.tensor_tensor(wfl_lo[:], wfl_raw[:], wfl_hi[:].bitcast(F32), ALU.subtract).then_inc(sem("fl_w_lo"), 1)
        log1p_vector(eng, [t[:] for t in lam_t], "lam", 2)
        eng.tensor_scalar(lam_t[1][:], params[:, G_LAM:G_LAM + KT], -1.0, 0.0, ALU.mult, ALU.max).then_inc(sem("lam_dve"), 1)
        eng.wait_ge(sem("lam_dve"), LOG1P_STEPS + 1)
        eng.tensor_tensor(lam_t[0][:], lam_t[0][:], lam_t[1][:], ALU.add).then_inc(sem("lam_dve"), 1)
        eng.wait_ge(sem("lam_dve"), LOG1P_STEPS + 2)
        eng.tensor_scalar(sp4[:], lam_t[0][:], 4.0, None, ALU.mult).then_inc(sem("lam_dve"), 1)
        for h in range(16, ADA_HALVES):
            if h + 1 < ADA_HALVES:
                copy_rows(h + 1, (h + 1) % 4)
            add_bias(h, h // 2, h % 2)
        eng.wait_ge(sem("mod_ready"), ADA_HALVES + 1)
        for m, g in ((1, G_FFN1), (4, G_MIX), (7, G_FFN2), (10, G_FINAL)):
            eng.scalar_tensor_tensor(mods[:, m], mods[:, m], 1.0,
                                     params[:, g:g + KT].unsqueeze(2).to_broadcast([128, KT, NSEQ]),
                                     ALU.add, ALU.mult).then_inc(sem("mod_final"), 1)
        for m, half in ((2, 0.5), (5, 1.0), (8, 0.5)):
            eng.tensor_scalar(mods[:, m], mods[:, m], 1.0, half, ALU.add, ALU.mult).then_inc(sem("mod_final"), 1)

    def seq_bc(mod, k0=0, k1=KT):
        return mods[:, mod, k0:k1, 1:NSEQ].unsqueeze(3).to_broadcast([128, k1 - k0, SB, ST])

    STAT_BANKS = [(6, 7, 4), (0, 1, 2), (6, 7, 4), (0, 1, 2)]

    NORM_MODS = [(0, 1), (3, 4), (6, 7), (9, 10)]
    K_ON_ACT = 5

    def stats(n, c):
        return ps[STAT_BANKS[n][c]][:, 0:CH]

    def norm_square(eng, n, c):
        eng.activation(sq[:, :, tokens_of(c)], x[:, :, tokens_of(c)], ACT.Square).then_inc(sem("sq_ready"), 1)

    def norm_sum(eng, n, c):
        eng.wait_ge(sem("sq_ready"), NC * n + c + 1)
        for k in range(KT):
            last = eng.matmul(stats(n, c), ones[:], sq[:, k, tokens_of(c)], start=(k == 0), stop=(k == KT - 1))
        last.then_inc(sem("ss_ready"), 1)

    def norm_root(eng, n, c):
        eng.wait_ge(sem("ss_ready"), NC * n + c + 1)
        eng.activation(stats(n, c), stats(n, c), ACT.Sqrt, scale=1.0 / D, bias=eps_col[:]).then_inc(sem("rms_ready"), 1)

    def norm_inverse(eng, n, c):
        eng.wait_ge(sem("rms_ready"), NC * n + c + 1)
        eng.reciprocal(stats(n, c), stats(n, c)).then_inc(sem("inv_ready"), 1)

    def norm_scale(eng, n, c):
        g = NC * n + c
        h = h_f[:, :, tokens_of(c)]
        shift, scale = NORM_MODS[n]
        eng.wait_ge(sem("inv_ready"), g + 1)
        eng.tensor_tensor(h, x[:, :, tokens_of(c)], stats(n, c).unsqueeze(1).to_broadcast([128, KT, CH]),
                          ALU.mult).then_inc(sem("x_normed"), 1)
        eng.wait_ge(sem("x_normed"), g + 1)
        cp = CH if c < NC - 1 else CP
        if c == NC - 1:
            hs = h_f[:, :, TP:T].rearrange("p k (s t) -> p k s t", s=SB)
            eng.tensor_tensor(hs, hs, seq_bc(scale), ALU.mult).then_inc(sem("mod_step"), 1)
            eng.wait_ge(sem("mod_step"), n + 1)
            eng.tensor_tensor(hs, hs, seq_bc(shift), ALU.add)
        for k in range(K_ON_ACT):
            hp = h_f[:, k, CH * c:CH * c + cp]
            last = eng.tensor_scalar(hp, hp, mods[:, scale, k, 0:1], mods[:, shift, k, 0:1], ALU.mult, ALU.add)
        last.then_inc(sem("h_ready"), 1)

    def norm_modulate(eng, n, c):
        cp = CH if c < NC - 1 else CP
        shift, scale = NORM_MODS[n]
        eng.wait_ge(sem("x_normed"), NC * n + c + 1)
        for k in range(K_ON_ACT, KT):
            hp = h_f[:, k, CH * c:CH * c + cp]
            last = eng.activation(hp, hp, ACT.Identity, scale=mods[:, scale, k, 0:1], bias=mods[:, shift, k, 0:1])
        last.then_inc(sem("h_modulated"), 1)

    def norm_hi(eng, n, c):
        norm_modulate(eng, n, c)
        eng.wait_ge(sem("h_modulated"), NC * n + c + 1)
        eng.wait_ge(sem("h_ready"), NC * n + c + 1)
        eng.activation(acts_hi[:, :, tokens_of(c)], h_f[:, :, tokens_of(c)], ACT.Copy).then_inc(sem("h_hi"), 1)

    def norm_lo(eng, n, c):
        eng.wait_ge(sem("h_hi"), NC * n + c + 1)
        eng.tensor_tensor(acts_lo[:, :, tokens_of(c)], h_f[:, :, tokens_of(c)],
                          acts_hi[:, :, tokens_of(c)].bitcast(F32), ALU.subtract).then_inc(sem("h_lo"), 1)

    def norm_scalar(eng, n, x_ready):
        for c in range(NC):
            x_ready(eng, c)
            norm_square(eng, n, c)
            if c >= 1:
                norm_root(eng, n, c - 1)
        if n < 3:
            norm_hi(eng, n, 0)
        else:
            norm_modulate(eng, n, 0)
        norm_root(eng, n, 2)
        if n < 3:
            norm_hi(eng, n, 1)
        else:
            norm_modulate(eng, n, 1)
        if n == 1:
            norm_hi(eng, n, 2)

    def norm_vector(eng, n):
        norm_inverse(eng, n, 0)
        norm_scale(eng, n, 0)
        norm_inverse(eng, n, 1)
        norm_lo(eng, n, 0)
        norm_scale(eng, n, 1)
        norm_inverse(eng, n, 2)
        norm_lo(eng, n, 1)
        if n == 1:
            norm_scale(eng, n, 2)
            norm_lo(eng, n, 2)

    def ffn_sync(eng, f):
        w1, w3, w2 = (a[f"ffn{f + 1}_w{n}"][0] for n in (1, 3, 2))
        block0 = (B_FFN1, B_FFN2)[f]
        w1v, w3v = kview(w1), kview(w3)
        with eng.Fori(0, FF_PAIRS) as i:
            b = block0 + i * 3
            load_block(eng, b, FFN_SLOTS[0], w1v[:, :, ds(i * 256, 256)])
            load_block(eng, b + 1, FFN_SLOTS[1], w3v[:, :, ds(i * 256, 256)])
            load_block(eng, b + 2, FFN_SLOTS[2],
                       w2[ds(i * 256, 256), :].rearrange("(t p) n -> p t n", p=128))

    def ffn_tensor(eng, f):
        block0 = (B_FFN1, B_FFN2)[f]

        def body(i, last_step):
            it = f * FF_PAIRS + i
            for c in range(NC):
                for t in range(2):
                    n = 2 * c + t
                    g = it * 6 + n
                    eng.wait_ge(sem("u_free"), g - 2 + 1 + CREDIT)
                    if t == 0:
                        eng.wait_ge(sem("h_lo"), NC * (0, 2)[f] + c + 1)
                    if n == 0:
                        wait_block(eng, block0 + i * 3 + 1)
                    for which, bank in ((0, 2 * (n % 2)), (1, 2 * (n % 2) + 1)):
                        whi, wlo = wcols(FFN_SLOTS[which][2], t)
                        for k in range(KT):
                            opens = sem("w_used") if (n, which, k) == (0, 0, 0) else None
                            last = mm3(eng, ps[bank][:, 0:CH], whi[k], wlo[k], acts_hi[:, k, tokens_of(c)],
                                       acts_lo[:, k, tokens_of(c)], k == 0, k == KT - 1, opens)
                        if (n, which) == (5, 0):
                            last.then_inc(sem("w_used"), 1)
                    last.then_inc(sem("a_full"), 1)
            wait_block(eng, block0 + i * 3 + 2)
            h2 = w_hi[FFN_SLOTS[2][2]][:].rearrange("p (t n) -> p t n", t=2)
            l2 = w_lo[FFN_SLOTS[2][2]][:].rearrange("p (t n) -> p t n", t=2)
            for c in range(NC):
                eng.wait_ge(sem("u_lo_done"), it * 6 + 2 * c + 2)
                for d in range(KT):
                    eng.wait_ge(sem("y_free"), it * 24 + c * 8 + d - 4 + 1 + CREDIT)
                    for t in range(2):
                        opens = sem("w_used") if (c, d, t) == (0, 0, 0) else None
                        last = mm3(eng, ps[4 + d % 4][:, 0:CH], h2[:, t, 128 * d:128 * d + 128],
                                   l2[:, t, 128 * d:128 * d + 128], u_hi[:, t, tokens_of(c)],
                                   u_lo[:, t, tokens_of(c)], t == 0, t == 1, opens)
                    last.then_inc(sem("b_full"), 1)
                if last_step and c >= 1:
                    if c == 1:
                        eng.wait_ge(sem("u_free"), it * 6 + 6 + CREDIT)
                    norm_sum(eng, 2 * f + 1, c - 1)

        with eng.Fori(0, FF_PAIRS - 1) as i:
            body(i, False)
        body(FF_PAIRS - 1, True)
        if f == 0:
            norm_sum(eng, 1, NC - 1)

    def ffn_split_hi(eng, f, i, j):
        block0, raws = ((B_FFN1, FFN1_RAWS), (B_FFN2, FFN2_RAWS))[f]
        split_hi(eng, block0 + i * 3 + j, FFN_SLOTS[j], (raws[0] + i * 2, raws[1] + i, raws[0] + i * 2 + 1)[j])

    def ffn_scalar(eng, f):
        def body(i, first_step=False, last_step=False):
            it = f * FF_PAIRS + i
            ffn_split_hi(eng, f, i, 2)
            for n in range(6):
                c, t = n // 2, n % 2
                g = it * 6 + n
                eng.wait_ge(sem("a_full"), g + 1)
                eng.wait_ge(sem("u_free"), g - 2 + 1 + CREDIT)
                eng.activation(gated[n % 2][:], ps[2 * (n % 2)][:, 0:CH], ACT.Silu).then_inc(sem("gated_ready"), 1)
                eng.wait_ge(sem("u_free"), g + 1 + CREDIT)
                eng.activation(u_hi[:, t, tokens_of(c)], u_f[n % 2][:], ACT.Copy).then_inc(sem("u_hi_done"), 1)
                if first_step and n == 1:
                    norm_hi(eng, 2 * f, 2)
            if not last_step:
                ffn_split_hi(eng, f, i + 1, 0)
                ffn_split_hi(eng, f, i + 1, 1)

        body(0, first_step=True)
        with eng.Fori(1, FF_PAIRS - 1) as i:
            body(i)
        body(FF_PAIRS - 1, last_step=True)

    def ffn_gpsimd(eng, f):
        block0 = (B_FFN1, B_FFN2)[f]

        def body(i, last_step):
            it = f * FF_PAIRS + i
            split_lo(eng, block0 + i * 3 + 2, FFN_SLOTS[2])
            for n in range(6):
                c, t = n // 2, n % 2
                eng.wait_ge(sem("u_hi_done"), it * 6 + n + 1)
                eng.tensor_tensor(u_lo[:, t, tokens_of(c)], u_f[n % 2][:], u_hi[:, t, tokens_of(c)].bitcast(F32),
                                  ALU.subtract).then_inc(sem("u_lo_done"), 1)
            if not last_step:
                for j in range(2):
                    split_lo(eng, block0 + (i + 1) * 3 + j, FFN_SLOTS[j])

        for j in range(2):
            split_lo(eng, block0 + j, FFN_SLOTS[j])
        with eng.Fori(0, FF_PAIRS - 1) as i:
            body(i, False)
        body(FF_PAIRS - 1, True)

    def ffn_vector(eng, f):
        gate = (2, 8)[f]

        def body(i, first_step):
            it = f * FF_PAIRS + i
            for n in range(6):
                g = it * 6 + n
                eng.wait_ge(sem("gated_ready"), g + 1)
                if n >= 2:
                    eng.wait_ge(sem("u_lo_done"), g - 1)
                eng.tensor_tensor(u_f[n % 2][:], ps[2 * (n % 2) + 1][:, 0:CH], gated[n % 2][:],
                                  ALU.mult).then_inc(sem("u_free"), 1)
                if first_step and n == 1:
                    norm_scale(eng, 2 * f, 2)
                    norm_lo(eng, 2 * f, 2)
            for c in range(NC):
                for d in range(KT):
                    b = it * 24 + c * 8 + d
                    eng.wait_ge(sem("b_full"), b + 1)
                    add_gated(eng, ps[4 + d % 4], x, d, c, gate, "y_free", it * 8 + d + f * KT)

        body(0, True)
        with eng.Fori(1, FF_PAIRS) as i:
            body(i, False)

    def add_gated(eng, bank, xt, d, c, gate, done, step):
        cp = CH if c < NC - 1 else CP
        t0 = c * CH
        if c == NC - 1:
            eng.tensor_tensor(s_tmp[d % 2][:], bank[:, CP:CH].rearrange("p (s t) -> p s t", s=SB),
                              mods[:, gate, d, 1:NSEQ].unsqueeze(2).to_broadcast([128, SB, ST]),
                              ALU.mult).then_inc(sem("s_gated"), 1)
        last = eng.scalar_tensor_tensor(xt[:, d, t0:t0 + cp], bank[:, 0:cp], mods[:, gate, d, 0:1],
                                        xt[:, d, t0:t0 + cp], ALU.mult, ALU.add)
        if c == NC - 1:
            eng.wait_ge(sem("s_gated"), step + 1)
            xs_ = xt[:, d, TP:T].rearrange("p (s t) -> p s t", s=SB)
            last = eng.tensor_tensor(xs_, xs_, s_tmp[d % 2][:], ALU.add)
        last.then_inc(sem(done), 1)

    def final_tensor(eng):
        def turn(c):
            eng.wait_ge(sem("h_ready"), NC * NORMS_BEFORE + c + 1)
            eng.wait_ge(sem("h_modulated"), NC * NORMS_BEFORE + c + 1)
            for m in range(3):
                tile = 3 * c + m
                for half in range(2):
                    n = 2 * tile + half
                    if tile >= 2:
                        eng.wait_ge(sem(("y_even", "y_odd")[half]), tile - 1)
                    elif tile == 0 and half == 0:
                        eng.wait_ge(sem("y_free"), 2 * FF_PAIRS * 24 + CREDIT)
                    for k in range(4):
                        last = eng.transpose(ps[4 + n % 4][:, 128 * k:128 * k + 128],
                                             h_f[:, 4 * half + k, 128 * tile:128 * tile + 128], ident[:])
                    last.then_inc(sem("y_turned"), 1)

        norm_sum(eng, NORMS_BEFORE, NC - 1)
        for c in range(NC):
            turn(c)

    def final_scalar(eng):
        norm_scalar(eng, NORMS_BEFORE, x_after_ffn2)
        for tile in range(T // 128):
            n = 2 * tile + 1
            if tile == 3:
                norm_modulate(eng, NORMS_BEFORE, 2)
            eng.wait_ge(sem("y_turned"), n + 1)
            if tile >= 2:
                eng.wait_ge(sem(f"y_stored{tile % 2}"), 16 * (tile // 2))
            eng.activation(y_rows[tile % 2][:, 512:1024], ps[4 + n % 4][:], ACT.Copy).then_inc(sem("y_odd"), 1)

    def final_vector(eng):
        def copy_out(c):
            for tile in range(3 * c, 3 * c + 3):
                n = 2 * tile
                eng.wait_ge(sem("y_turned"), n + 1)
                if tile >= 2:
                    eng.wait_ge(sem(f"y_stored{tile % 2}"), 16 * (tile // 2))
                eng.tensor_copy(y_rows[tile % 2][:, 0:512], ps[4 + n % 4][:]).then_inc(sem("y_even"), 1)

        for c in range(NC):
            norm_inverse(eng, NORMS_BEFORE, c)
            norm_scale(eng, NORMS_BEFORE, c)
            if c >= 1:
                copy_out(c - 1)
        copy_out(NC - 1)

    def final_sync(eng):
        yp = o["y_prompt"][0].rearrange("(m p) d -> m p d", p=128)
        for tile in range(T // 128):
            eng.wait_ge(sem("y_even"), tile + 1)
            eng.wait_ge(sem("y_odd"), tile + 1)
            dst = yp[tile] if tile < TP // 128 else o["y_sample"].rearrange("s t d -> (s t) d")
            eng.dma_start(dst, y_rows[tile % 2][:]).then_inc(sem(f"y_stored{tile % 2}"), 16)
        eng.wait_ge(sem("y_stored0"), 16 * 5)
        eng.wait_ge(sem("y_stored1"), 16 * 4)

    N_IT = KT // 2
    COLS = (COL_XR, COL_GR, COL_Q, COL_K, COL_V, COL_GA, COL_GB)
    XR, GR, Q, K, V, GA, GB = range(7)
    ST_BEFORE = {Q: 0, K: 1, V: 2, GA: 2, GB: 3}
    TOK_BEFORE = (0, 0, 1, 1, 3, 2)
    FL_STEPS = LOG1P_STEPS + 5

    def x_samples(t):
        return xpad[t][:, XP:].rearrange("p (s j) -> p s j", s=SB)

    def proj_sync(eng):
        w_in_v = kview(a["w_in"][0])

        def load(i, j):
            load_block(eng, B_PROJ + i * 7 + j, PROJ_SLOTS[j], w_in_v[:, :, ds(i * 256 + COLS[j], 256)])

        def load_gates(i):
            for n, name in enumerate(("rg_wa", "rg_wx")):
                for half in range(2):
                    src = a[name][0].rearrange("(n two) i j -> two i n j", two=2)[half]
                    eng.dma_start(bd[64 * half:64 * half + 64, 2 * n:2 * n + 2, 64 * half:64 * half + 64],
                                  src[:, ds(i * 2, 2), :]).then_inc(sem("bd_loaded"), 16)

        load(0, 0)
        load(0, 1)
        eng.wait_ge(sem("y_free"), FF_PAIRS * 24 + CREDIT)
        eng.dma_start(x_dram, x[:].rearrange("p k t -> p (k t)")).then_inc(sem("x_spilled"), 16)
        eng.wait_ge(sem("bd_clear"), 1)
        load_gates(0)
        for j in range(2, 7):
            load(0, j)
        with eng.Fori(1, N_IT) as i:
            load(i, 0)
            eng.wait_ge(sem("ri_full"), i * 12)
            load_gates(i)
            for j in range(1, 7):
                load(i, j)

    def proj_tensor(eng):
        eng.wait_ge(sem("fl_w_lo"), 1)

        def forget(c):
            eng.wait_ge(sem("h_lo"), NC + c + 1)
            for k in range(KT):
                last = mm3(eng, ps[3 + c][0:H, 0:CH], wfl_hi[:, k, :], wfl_lo[:, k, :], acts_hi[:, k, tokens_of(c)],
                           acts_lo[:, k, tokens_of(c)], k == 0, k == KT - 1)
            last.then_inc(sem("fl_full"), 1)

        def body(i, first):
            for j in range(7):
                for n in range(6):
                    t, c = n // 3, n % 3
                    g = i * 42 + j * 6 + n
                    eng.wait_ge(sem("proj_free"), g + 1)
                    if first and j == XR and n < NC:
                        forget(n)
                    if first and (j, n) == (XR, 3):
                        eng.wait_ge(sem("fl_z"), 3)
                    if j in (V, GA):
                        e = i * 12 + (j - V) * 6 + n
                        if (j, n) == (V, 0):
                            eng.wait_ge(sem("ri_moved"), i * 12 + 12 + 2)
                        eng.wait_ge(sem("tok_moved"), e + 1)
                        for m in range(3):
                            last = eng.transpose(ps[6 + n % 2][:, 128 * m:128 * m + 128],
                                                 st[t][:, CH * c + 128 * m:CH * c + 128 * m + 128], ident[:])
                        last.then_inc(sem("tok_turned"), 1)
                    if n == 0:
                        wait_block(eng, B_PROJ + i * 7 + j)
                    whi, wlo = wcols(PROJ_SLOTS[j][2], t)
                    for k in range(KT):
                        last = mm3(eng, ps[n][:, 0:CH], whi[k], wlo[k], acts_hi[:, k, tokens_of(c)],
                                   acts_lo[:, k, tokens_of(c)], k == 0, k == KT - 1,
                                   sem("w_used") if (n, k) == (0, 0) else None)
                    last.then_inc(sem("proj_full"), 1)
                    if j == GR and first and n == 5:
                        logf_turn(eng)
                    if j == Q:
                        if n == 0:
                            eng.wait_ge(sem("bd_loaded"), i * 64 + 64)
                            if first:
                                eng.wait_ge(sem("lft_ready"), 1)
                            eng.wait_ge(sem("tok_moved"), i * 12 + 2)
                        if c == 0:
                            eng.wait_ge(sem("conv_ready"), i * 2 + t + 1)
                        for kind in range(2):
                            eng.wait_ge(sem("ri_moved"), i * 12 + 2 * n + kind + 1)
                            eng.matmul(ps[6 + kind][:, 0:CH], bd[:, 2 * kind + t, :], xc[t][:, tokens_of(c)],
                                       start=True, stop=True).then_inc(sem("ri_full"), 1)
        body(0, True)
        with eng.Fori(1, N_IT) as i:
            body(i, False)

    def logf_turn(eng):
        eng.wait_ge(sem("fl_done"), 1)
        eng.wait_ge(sem("fl_z"), 3)
        for m in range(T // 128):
            last = eng.transpose(ps[7][:, H * m:H * m + H], it[1][0:H, 128 * m:128 * m + 128], ident[0:H, 0:H])
        last.then_inc(sem("lf_turned"), 1)

    def proj_scalar(eng):
        eng.wait_ge(sem("x_spilled"), 16)
        eng.wait_ge(sem("h_lo"), 2 * NC)
        for c in range(NC):
            eng.wait_ge(sem("fl_full"), c + 1)
            eng.activation(it[1][0:H, tokens_of(c)], ps[3 + c][0:H, 0:CH], ACT.Identity,
                           bias=b_fgt_col[:]).then_inc(sem("fl_z"), 1)
        eng.wait_ge(sem("fl_z"), 3)
        eng.activation(rt[0][0:H, :], it[1][0:H, :], ACT.Abs).then_inc(sem("fl_act"), 1)
        eng.wait_ge(sem("fl_act"), 1)
        eng.activation(rt[0][0:H, :], rt[0][0:H, :], ACT.Exp, scale=-1.0).then_inc(sem("fl_act"), 1)
        log1p_scalar(eng, rt[1][0:H, :], "fl")

        def body(i, first):
            for j in range(7):
                for n in range(6):
                    t, c = n // 3, n % 3
                    g = i * 42 + j * 6 + n
                    tile = i * 2 + t
                    if j in (V, GA):
                        move_tokens(eng, i, j, n)
                    eng.wait_ge(sem("proj_full"), g + 1)
                    bank = ps[n][:, 0:CH]
                    if j == XR:
                        if c == 0:
                            eng.wait_ge(sem("rnn_done"), i * 2 + t + 1)
                        if c < NC - 1:
                            eng.activation(xpad[t][:, PAD + CH * c:PAD + CH * c + CH], bank, ACT.Copy).then_inc(sem("proj_free"), 1)
                        else:
                            eng.activation(xpad[t][:, PAD + CH * c:XP], bank[:, 0:CP], ACT.Copy)
                            eng.activation(x_samples(t)[:, :, PAD:], bank[:, CP:CH].rearrange("p (s q) -> p s q", s=SB),
                                           ACT.Copy).then_inc(sem("proj_free"), 1)
                    elif j == GR:
                        if c == 0:
                            eng.wait_ge(sem(f"a_stored{t}"), i * 16 + 16)
                        eng.activation(gl[t][:, tokens_of(c)], bank, ACT.Gelu_apprx_tanh).then_inc(sem("proj_free"), 1)
                    else:
                        if c == 0:
                            eng.wait_ge(sem(f"st_stored{t}"), (i * 4 + ST_BEFORE[j] + 1) * 16)
                        func = ACT.Sigmoid if j in (GA, GB) else ACT.Copy
                        eng.activation(st[t][:, tokens_of(c)], bank, func,
                                       scale=HD ** -0.5 if j == Q else 1.0).then_inc(sem("proj_free"), 1)
                        if c == NC - 1 and j != V:
                            eng.wait_ge(sem("proj_free"), g + 1 + 6)
                            dst = {Q: q_dram, K: k_dram, GA: ga_dram, GB: gb_dram}[j]
                            eng.dma_start(dst[ds(tile * 128, 128), :], st[t][:]).then_inc(sem(f"st_stored{t}"), 16)
                    if j == Q:
                        gates(eng, i, n, first)
                    if n == 2:
                        nj = (j + 1) % 7
                        raw = PROJ_SLOTS[nj][0]
                        split_hi(eng, B_PROJ + i * 7 + j + 1, PROJ_SLOTS[nj],
                                 (i * (4, 3)[raw] if j < 6 else i * 4 + 4) + nj // 2 + PROJ_RAWS[raw])
                    if first and (j, n) == (GR, 5):
                        forget_out(eng)
                    if (j, n) == (GA, 0):
                        for u in range(2):
                            eng.wait_ge(sem("rnn_done"), i * 2 + u + 1 + 2)
                            eng.dma_start(a_dram[ds(i * 256 + u * 128, 128), :], gl[u][:]).then_inc(sem(f"a_stored{u}"), 16)
        body(0, True)
        with eng.Fori(1, N_IT) as i:
            body(i, False)

    def move_tokens(eng, i, j, n):
        t, c = n // 3, n % 3
        which = j - V
        e = i * 12 + which * 6 + n
        slot = n % 2
        eng.wait_ge(sem("tok_turned"), e + 1)
        eng.wait_ge(sem(f"tok_stored{slot}"), ((i * 2 + which) * 4 + TOK_BEFORE[n] + 1) * 16)
        eng.activation(tok[slot][:], ps[6 + slot][:, 0:CH].rearrange("p (m d) -> p m d", m=3), ACT.Copy).then_inc(sem("tok_moved"), 1)
        eng.wait_ge(sem("tok_moved"), e + 1 + 2)
        name = ("k", "v")[which]
        prompt = o[name + "_prompt"][0, 0].rearrange("(m p) h d -> p m (h d)", p=128)
        cols = ds(i * 256 + t * 128, 128)
        m1 = 3 if c < NC - 1 else 2
        eng.dma_start(prompt[:, 3 * c:3 * c + m1, cols], tok[slot][:, 0:m1, :]).then_inc(sem(f"tok_stored{slot}"), 16)
        if c == NC - 1:
            sample = o[name + "_sample"][0].rearrange("s t h d -> (s t) (h d)")
            eng.dma_start(sample[:, cols], tok[slot][:, 2, :]).then_inc(sem(f"tok_stored{slot}"), 16)

    def gates(eng, i, n, first):
        t, c = n // 3, n % 3
        if first and n == 0:
            eng.wait_ge(sem("bias_stored"), 16)
            eng.wait_ge(sem("lf_turned"), 1)
        for kind, buf in ((0, rt), (1, it)):
            eng.wait_ge(sem("ri_full"), i * 12 + 2 * n + kind + 1)
            eng.activation(buf[t][:, tokens_of(c)], ps[6 + kind][:, 0:CH], ACT.Sigmoid,
                           bias=gate_p[:, t, kind:kind + 1]).then_inc(sem("ri_moved"), 1)
        if c == NC - 1:
            eng.wait_ge(sem("ri_moved"), i * 12 + 2 * n + 2 + 2)
            eng.activation(rt[t][:], rt[t][:], ACT.Tanh, scale=gate_p[:, t, 2:3]).then_inc(sem("rnn_act"), 1)
            eng.wait_ge(sem("rnn_act"), i * 4 + 2 * t + 1)
            eng.activation(xpad[t][:, 0:T], rt[t][:], ACT.Sqrt, scale=4.0, bias=tiny_col[:]).then_inc(sem("rnn_act"), 1)

    def forget_out(eng):
        eng.wait_ge(sem("bias_ready"), 1)
        eng.dma_start(bias_dram, rt[0][0:H, 0:TP]).then_inc(sem("bias_stored"), 16)
        eng.wait_ge(sem("lft_ready"), 1)
        eng.dma_start(o["logf_prompt"][0, 0].rearrange("(m p) h -> p m h", p=128), lft[:, 0:TP // 128, :]).then_inc(sem("logf_stored"), 16)
        eng.dma_start(o["logf_sample"][0].rearrange("s t h -> (s t) h"), lft[:, TP // 128, :]).then_inc(sem("logf_stored"), 16)

    def proj_gpsimd(eng):
        split_lo(eng, B_PROJ, PROJ_SLOTS[0])
        with eng.Fori(0, N_IT) as i:
            for j in range(7):
                split_lo(eng, B_PROJ + i * 7 + j + 1, PROJ_SLOTS[(j + 1) % 7])

    class Steps:

        def __init__(self, eng, name, base):
            self.eng, self.sem, self.base, self.n = eng, sem(name), base, 0

        def done(self, instruction):
            instruction.then_inc(self.sem, 1)
            self.n += 1

        def settle(self):
            self.eng.wait_ge(self.sem, self.base + self.n)

    RNN_STEPS = 2 * 21

    def proj_vector(eng):
        eng.sem_inc(sem("rnn_done"), 2)
        eng.wait_ge(sem("x_spilled"), 16)
        eng.wait_ge(sem("h_lo"), 2 * NC)
        eng.memset(bd[:], 0.0).then_inc(sem("bd_clear"), 1)
        log1p_vector(eng, [rt[0][0:H, :], rt[1][0:H, :], it[0][0:H, :], xc[0][0:H, :]], "fl", 2)
        eng.tensor_scalar(it[1][0:H, :], it[1][0:H, :], 0.0, None, ALU.min).then_inc(sem("fl_dve"), 1)
        eng.wait_ge(sem("fl_dve"), LOG1P_STEPS + 1)
        eng.tensor_tensor(it[1][0:H, :], it[1][0:H, :], rt[0][0:H, :], ALU.subtract).then_inc(sem("fl_done"), 1)
        eng.wait_ge(sem("fl_done"), 1)
        minus_sums(eng, rt[0][0:H, 0:TP], it[1][0:H, 0:TP], 0.0).then_inc(sem("bias_ready"), 1)

        def body(i, first):
            s = Steps(eng, "rnn_dve", i * RNN_STEPS)

            def channel(vec, t):
                return params[:, ds(i * 2 + (vec + t), 1)]

            for t in range(2):
                tile = i * 2 + t
                xs_, out_s = x_samples(t), xc[t][:, TP:T].rearrange("p (s q) -> p s q", s=SB)
                eng.wait_ge(sem("proj_free"), i * 42 + 3 * t + 3 + 6)
                s.done(eng.memset(xpad[t][:, 0:PAD], 0.0))
                for n, src in enumerate((channel(G_BA, t), channel(G_BX, t), sp4[:, ds(tile, 1)])):
                    eng.tensor_copy(gate_p[:, t, n:n + 1], src)
                cs = conv_state[:].rearrange("p (s j n) -> p s j n", s=SB, j=PAD)
                s.done(eng.tensor_copy(xs_[:, :, 0:PAD], cs[:, :, :, ds(tile, 1)].rearrange("p s j n -> p s (j n)")))
                s.settle()
                for j in range(CONV_W):
                    w = channel(G_CONVW + KT * j, t)
                    for out, src in ((xc[t][:, 0:TP], xpad[t][:, j:j + TP]), (out_s, xs_[:, :, j:j + ST])):
                        if j == 0:
                            s.done(eng.tensor_scalar(out, src, w, channel(G_CONVB, t), ALU.mult, ALU.add))
                        else:
                            s.done(eng.scalar_tensor_tensor(out, src, w, out, ALU.mult, ALU.add))
                    s.settle()
                eng.tensor_copy(states[:, ds(tile, 1), 0:PAD], xpad[t][:, TP:XP].unsqueeze(1))
                eng.tensor_copy(states[:, ds(tile, 1), PAD:PAD + SB * PAD].rearrange("p o (s j) -> p (o s) j", s=SB),
                                xs_[:, :, ST:ST + PAD]).then_inc(sem("conv_ready"), 1)
                if first and t == 1:
                    eng.wait_ge(sem("lf_turned"), 1)
                    eng.tensor_copy(lft[:], ps[7][:, 0:H * (T // 128)].rearrange("p (m h) -> p m h", h=H)).then_inc(sem("lft_ready"), 1)
            for t in range(2):
                tile = i * 2 + t
                root = xpad[t][:, 0:T]
                eng.wait_ge(sem("rnn_act"), i * 4 + 2 * t + 2)
                s.done(eng.tensor_tensor(it[t][:], it[t][:], xc[t][:], ALU.mult))
                s.settle()
                s.done(eng.tensor_scalar(xc[t][:], rt[t][:], 1.0, None, ALU.add))
                s.settle()
                s.done(eng.reciprocal(xc[t][:], xc[t][:]))
                s.done(eng.tensor_scalar(rt[t][:], rt[t][:], -1.0, 1.0, ALU.mult, ALU.add))
                s.settle()
                s.done(eng.tensor_tensor(root, root, xc[t][:], ALU.mult))
                s.done(eng.tensor_tensor(rt[t][:], rt[t][:], xc[t][:], ALU.mult))
                s.settle()
                s.done(eng.tensor_tensor(it[t][:], it[t][:], root, ALU.mult))
                first_a, first_u = rt[t][:, TP:T:ST], it[t][:, TP:T:ST]
                s.done(eng.tensor_tensor(tmp8[t][:], first_a, h0[:].rearrange("p (s n) -> p s n", s=SB)[:, :, ds(tile, 1)].rearrange("p s n -> p (s n)"), ALU.mult))
                s.settle()
                s.done(eng.tensor_tensor(first_u, first_u, tmp8[t][:], ALU.add))
                s.done(eng.memset(first_a, 0.0))
                s.settle()
                s.done(eng.tensor_tensor_scan(xc[t][:], rt[t][:], it[t][:], 0.0, ALU.mult, ALU.add))
                s.settle()
                eng.tensor_copy(states[:, ds(tile, 1), 27:28], xc[t][:, TP - 1:TP].unsqueeze(1))
                eng.tensor_copy(states[:, ds(tile, 1), 28:36], xc[t][:, TP + ST - 1:T:ST].unsqueeze(1)).then_inc(sem("states_ready"), 1)
                eng.wait_ge(sem("proj_free"), i * 42 + 6 + 3 * t + 3 + 6)
                eng.tensor_tensor(gl[t][:], gl[t][:], xc[t][:], ALU.mult).then_inc(sem("rnn_done"), 1)
            assert s.n == RNN_STEPS, s.n
        body(0, True)
        with eng.Fori(1, N_IT) as i:
            body(i, False)

    G_BRR = 42 * N_IT

    def brr_sync(eng):
        for t in range(2):
            eng.wait_ge(sem(f"a_stored{t}"), (N_IT + 1) * 16)
        eng.dma_start(a_stage[:], kview(a_dram)).then_inc(sem("a_loaded"), 16)
        w = kview(a["w_br_rnn"][0])

        def gate_in(j, t):
            if j == 0:
                eng.wait_ge(sem(f"st_stored{t}"), (4 * N_IT + 1) * 16)
            else:
                eng.wait_ge(sem(f"z1_stored{t}"), 16 * j)
            eng.dma_start(st[t][:], ga_dram[256 * j + 128 * t:256 * j + 128 * t + 128, :]).then_inc(sem(f"gate_loaded{t}"), 16)

        def out(j, t):
            eng.wait_ge(sem("br_free"), 6 * j + 3 * t + 3)
            eng.dma_start(z1_dram[256 * j + 128 * t:256 * j + 128 * t + 128, :], st[t][:]).then_inc(sem(f"z1_stored{t}"), 16)

        load_block(eng, B_BRR, BRR_SLOTS[0], w[:, :, 0:256])
        gate_in(0, 0)
        gate_in(0, 1)
        load_block(eng, B_BRR + 1, BRR_SLOTS[1], w[:, :, 256:512])
        for j in range(4):
            if j < 2:
                load_block(eng, B_BRR + j + 2, BRR_SLOTS[j + 2], w[:, :, 256 * j + 512:256 * j + 768])
            if j == 0:
                eng.wait_ge(sem("logf_stored"), 32)
                eng.dma_start(lf16[:].rearrange("t (s h) -> t s h", s=SB), o["logf_sample"][0].rearrange("s t h -> t s h")).then_inc(sem("lf16_loaded"), 16)
            if j == 1:
                eng.wait_ge(sem("w_used"), B_BRR + 1 + CREDIT)
                head_loads(eng, 0, 0)
            if j == 2:
                merge_loads_ahead(eng)
            for t in range(2):
                out(j, t)
                if j < 3:
                    gate_in(j + 1, t)
        eng.wait_ge(sem("new_f_ready"), 1)
        eng.dma_start(past_dram[:, PAST:PAST + ST], new_f[:]).then_inc(sem("past_stored"), 16)
        eng.wait_ge(sem("state_out_ready"), 2)
        cp = o["conv_prompt"][0, 0]
        cs = o["conv_sample"][0].rearrange("s j d -> (s j) d")
        for dst, r0, r1 in ((cp, 0, 3), (cs, 3, 27), (o["rglru_prompt"][0], 27, 28), (o["rglru_sample"][0], 28, 36)):
            eng.dma_start(dst, state_out[r0:r1, :]).then_inc(sem("states_stored"), 16)

    def brr_tensor(eng):
        for j in range(4):
            for n in range(6):
                t, c = n // 3, n % 3
                q = 6 * j + n
                if j == 0:
                    eng.wait_ge(sem("proj_free"), G_BRR - 6 + n + 1 + 6)
                    if t == 0:
                        eng.wait_ge(sem("a_lo"), c + 1)
                else:
                    eng.wait_ge(sem("br_free"), q - 6 + 1)
                if n == 0:
                    wait_block(eng, B_BRR + j)
                whi, wlo = wcols(BRR_SLOTS[j][2], t)
                for k in range(KT):
                    last = mm3(eng, ps[n][:, 0:CH], whi[k], wlo[k], acts_hi[:, k, tokens_of(c)],
                               acts_lo[:, k, tokens_of(c)], k == 0, k == KT - 1,
                               sem("w_used") if (n, k) == (0, 0) else None)
                last.then_inc(sem("br_full"), 1)
            if j == 1:
                eng.wait_ge(sem("states_ready"), 2 * N_IT)
                eng.wait_ge(sem("tok_moved"), 12 * N_IT + 2)
                for half in range(2):
                    for k in range(4):
                        last = eng.transpose(ps[6 + half][0:36, 128 * k:128 * k + 128], states[:, 4 * half + k, :], ident[:])
                last.then_inc(sem("state_rows_turned"), 1)
            if j == 2:
                eng.wait_ge(sem("lf16_loaded"), 16)
                eng.wait_ge(sem("state_out_ready"), 2)
                eng.transpose(ps[6][:, 0:ST], lf16[:], ident[0:ST, 0:ST]).then_inc(sem("lf16_turned"), 1)

    def brr_scalar(eng):
        eng.wait_ge(sem("a_loaded"), 16)
        eng.wait_ge(sem("proj_full"), G_BRR)
        for c in range(NC):
            eng.activation(acts_hi[:, :, tokens_of(c)], a_stage[:, :, tokens_of(c)], ACT.Copy).then_inc(sem("a_hi"), 1)
        for j in range(1, 4):
            raw = BRR_SLOTS[j][0]
            split_hi(eng, B_BRR + j, BRR_SLOTS[j], BRR_RAWS[raw] + j // 2)
        eng.wait_ge(sem("state_rows_turned"), 1)
        for half in range(2):
            eng.activation(state_out[:, 512 * half:512 * half + 512], ps[6 + half][0:36, :], ACT.Copy).then_inc(sem("state_out_ready"), 1)

    def brr_gpsimd(eng):
        for j in range(1, 4):
            split_lo(eng, B_BRR + j, BRR_SLOTS[j])

    def brr_vector(eng):
        for c in range(NC):
            eng.wait_ge(sem("a_hi"), c + 1)
            eng.tensor_tensor(acts_lo[:, :, tokens_of(c)], a_stage[:, :, tokens_of(c)],
                              acts_hi[:, :, tokens_of(c)].bitcast(F32), ALU.subtract).then_inc(sem("a_lo"), 1)
        for j in range(4):
            for n in range(6):
                t, c = n // 3, n % 3
                eng.wait_ge(sem("br_full"), 6 * j + n + 1)
                if c == 0:
                    eng.wait_ge(sem(f"gate_loaded{t}"), 16 * (j + 1))
                eng.tensor_tensor(st[t][:, tokens_of(c)], ps[n][:, 0:CH], st[t][:, tokens_of(c)], ALU.mult).then_inc(sem("br_free"), 1)
            if j == 3:
                eng.wait_ge(sem("lf16_turned"), 1)
                eng.tensor_copy(new_logf[:], ps[6][:, 0:ST]).then_inc(sem("lf16_moved"), 1)
                eng.wait_ge(sem("lf16_moved"), 1)
                minus_sums(eng, new_f[:], new_logf[:], past_last[:]).then_inc(sem("new_f_ready"), 1)

    PAIRS = H // 2
    STEPS = 16

    def att_sync(eng):
        for t in range(2):
            eng.wait_ge(sem(f"z1_stored{t}"), 64)
            eng.wait_ge(sem(f"tok_stored{t}"), 16 * (8 * N_IT + 1))
        eng.wait_ge(sem("states_stored"), 64)
        eng.wait_ge(sem("past_stored"), 32)
        v_rows = o["v_prompt"][0, 0].rearrange("(m p) h d -> p m (h d)", p=128)

        def body(i, last):
            for hh in range(2):
                hd = i * 2 + hh
                eng.wait_ge(sem("pa_max"), i * 16 + 8 * hh + 8)
                eng.dma_start(kbias[hh][:], bias_dram[ds(hd, 1), :].to_broadcast([128, TP])).then_inc(sem(f"kbias_loaded{hh}"), 16)
                eng.wait_ge(sem("pa_pv"), i * 16 + 8 * hh + 8)
                eng.dma_start(vh[hh][:], v_rows[:, :, ds(hd * 64, 64)]).then_inc(sem(f"vh_loaded{hh}"), 16)
                if not (last and hh == 1):
                    eng.wait_ge(sem("pa_split"), hd + 2)
                    head_loads(eng, i, hh + 1)
        with eng.Fori(0, PAIRS - 1) as i:
            body(i, False)
        body(PAIRS - 1, True)

    def head_loads(eng, i, ahead):
        for half in range(2):
            rows = slice(64 * half, 64 * half + 64)
            eng.dma_start(kf[rows, :], k_dram[ds(i * 128 + ahead * 64, 64), 0:TP]).then_inc(sem("kq_loaded"), 16)
            eng.dma_start(qf[rows, :], q_dram[ds(i * 128 + ahead * 64, 64), 0:TP]).then_inc(sem("kq_loaded"), 16)

    def att_tensor(eng):
        eng.wait_ge(sem("br_free"), 24)
        eng.wait_ge(sem("state_out_ready"), 2)
        eng.wait_ge(sem("lf16_moved"), 1)
        def scores(i, k):
            hh, qi = k // 8, k % 8
            keys = 128 * (qi + 1)
            if qi == 0:
                eng.wait_ge(sem("pa_split"), i * 2 + hh + 2)
            eng.wait_ge(sem("pa_max"), i * 16 + k - 2 + 1 + 16)
            lhs = q_hl[hh][:, 128 * qi:128 * qi + 128]
            for c0 in range(0, keys, 512):
                c1 = min(c0 + 512, keys)
                out = psum[:, 1024 * (k % 2) + c0:1024 * (k % 2) + c1]
                eng.matmul(out, lhs, k_hi[hh][:, c0:c1], start=True, stop=False)
                last = eng.matmul(out, lhs, k_lo[hh][:, c0:c1], start=False, stop=c1 < keys)
            last = eng.matmul(psum[:, 1024 * (k % 2) + keys - 128:1024 * (k % 2) + keys], ident_r[:], causal_r[:],
                              start=False, stop=True)
            last.then_inc(sem("pa_s"), 1)

        def turn(i, k):
            hh, qi = k // 8, k % 8
            eng.wait_ge(sem("pa_exp"), i * 16 + k + 1)
            eng.wait_ge(sem("pa_c4"), i * 16 + k + 1)
            for kb in range(qi + 1):
                if kb == 4:
                    eng.wait_ge(sem("pa_c5"), i * 8 + 4 * hh + qi - 4 + 1)
                last = eng.transpose(ps[4 + kb // 4][:, 128 * (kb % 4):128 * (kb % 4) + 128],
                                     pr[k % 4][:, 128 * kb:128 * kb + 128], ident[:])
                if kb == min(3, qi):
                    last.then_inc(sem("pa_t4"), 1)
            if qi >= 4:
                last.then_inc(sem("pa_t5"), 1)

        def values(i, k):
            hh, qi = k // 8, k % 8
            if qi == 0:
                eng.wait_ge(sem(f"vh_loaded{hh}"), i * 16 + 16)
            eng.wait_ge(sem("pa_out"), i * 16 + k + 1)
            if k <= 1:
                eng.wait_ge(sem("pa_turned_in"), i * 8 + 7 + k)
            elif k >= 10:
                eng.wait_ge(sem("pa_turned_in"), i * 8 + k - 1)
            eng.wait_ge(sem("pa_c4"), i * 16 + k + 2)
            for kb in range(qi + 1):
                if kb == 4:
                    eng.wait_ge(sem("pa_c5"), i * 8 + 4 * hh + qi - 4 + 2)
                last = eng.matmul(ps[6 + k % 2][:, 0:HD], pT[k % 2][:, 128 * kb:128 * kb + 128], vh[hh][:, kb, :],
                                  start=(kb == 0), stop=(kb == qi))
            last.then_inc(sem("pa_pv"), 1)

        def turn_att(i, m):
            eng.wait_ge(sem("pa_out"), i * 16 + 8 + m + 1 + 2)
            eng.transpose(ps[6 + m % 2][:, 128:256], att[:, m, :], ident[:]).then_inc(sem("pa_at"), 1)

        def body(i, first=False, last=False):
            for k in range(STEPS):
                if k + 2 < STEPS:
                    scores(i, k + 2)
                elif not last:
                    scores(i + 1, k + 2 - STEPS)
                turn(i, k)
                if k >= 1:
                    values(i, k - 1)
                if k >= 10:
                    turn_att(i, k - 10)
                if k == 0 and not first:
                    turn_att(i - 1, 7)
            values(i, STEPS - 1)
            turn_att(i, 6)

        scores(0, 0)
        scores(0, 1)
        body(0, first=True)
        with eng.Fori(1, PAIRS - 1) as i:
            body(i)
        body(PAIRS - 1, last=True)
        turn_att(PAIRS - 1, 7)

    def split_head_hi(eng, i, hd, hh):
        eng.wait_ge(sem("kq_loaded"), hd * 64 + 64)
        eng.wait_ge(sem("pa_s"), hd * 8 + 8)
        eng.activation(k_hi[hh][:], kf[:], ACT.Copy)
        eng.activation(q_hl[hh][:], qf[:], ACT.Copy).then_inc(sem("pa_hi"), 1)

    def att_scalar(eng):
        eng.sem_inc(sem("pa_c4"), 1)

        def body(i, first=False, last=False):
            def exp(i, k):
                keys = 128 * (k % 8 + 1)
                eng.wait_ge(sem("pa_neg"), i * 16 + k + 1)
                eng.activation(pr[k % 4][:, 0:keys], pr[k % 4][:, 0:keys], ACT.Exp, bias=stat[:, k % 4, 1:2],
                               accum_out=stat[:, k % 4, 2:3]).then_inc(sem("pa_exp"), 1)

            if first:
                exp(i, 0)
            for k in range(STEPS):
                if k + 1 < STEPS:
                    exp(i, k + 1)
                elif not last:
                    exp(i + 1, 0)
                cols = 128 * min(4, k % 8 + 1)
                eng.wait_ge(sem("pa_t4"), i * 16 + k + 1)
                eng.wait_ge(sem("pa_pv"), i * 16 + k - 1 + 16)
                eng.activation(pT[k % 2][:, 0:cols], ps[4][:, 0:cols], ACT.Copy).then_inc(sem("pa_c4"), 1)
                if k == 1:
                    split_head_hi(eng, i, i * 2 + 1, 1)
                if k == 9 and not last:
                    split_head_hi(eng, i, i * 2 + 2, 0)
        body(0, first=True)
        with eng.Fori(1, PAIRS - 1) as i:
            body(i)
        body(PAIRS - 1, last=True)

    def att_gpsimd(eng):
        eng.sem_inc(sem("pa_split"), 1)

        def body(i, hh):
            hd = i * 2 + hh
            eng.wait_ge(sem("pa_hi"), hd + 1)
            eng.tensor_tensor(k_lo[hh][:], kf[:], k_hi[hh][:].bitcast(F32), ALU.subtract).then_inc(sem("pa_k_lo"), 1)
            eng.wait_ge(sem("pa_k_lo"), hd + 1)
            low = slice(64, 128)
            eng.tensor_tensor(q_hl[hh][low, :], qf[low, :], q_hl[hh][low, :].bitcast(F32), ALU.subtract).then_inc(sem("pa_split"), 1)
        with eng.Fori(0, PAIRS) as i:
            body(i, 0)
            body(i, 1)

    def att_vector(eng):
        eng.sem_inc(sem("pa_max"), 16)
        eng.sem_inc(sem("pa_c5"), 1)
        eng.sem_inc(sem("pa_out"), 2)
        eng.sem_inc(sem("pa_turned_in"), 8)

        def maxima(i, k):
            hh, qi = k // 8, k % 8
            keys = 128 * (qi + 1)
            st_ = stat[:, k % 4, :]
            eng.wait_ge(sem("pa_s"), i * 16 + k + 1 + 16)
            if qi == 0:
                eng.wait_ge(sem(f"kbias_loaded{hh}"), i * 16 + 16)
            eng.memset(wait_mark[:, 0:1], 0.0)
            eng.tensor_tensor_reduce(pr[k % 4][:, 0:keys], psum[:, 1024 * (k % 2):1024 * (k % 2) + keys],
                                     kbias[hh][:, 0:keys], 1.0, -3e38, ALU.add, ALU.max, st_[:, 0:1]).then_inc(sem("pa_max"), 1)
            eng.wait_ge(sem("pa_max"), i * 16 + k + 1 + 16)
            eng.tensor_scalar(st_[:, 1:2], st_[:, 0:1], -1.0, None, ALU.mult).then_inc(sem("pa_neg"), 1)

        def output(i, k):
            hh, qi = k // 8, k % 8
            st_ = stat[:, k % 4, :]
            eng.wait_ge(sem("pa_exp"), i * 16 + k + 1)
            eng.reciprocal(st_[:, 3:4], st_[:, 2:3]).then_inc(sem("pa_rec"), 1)
            eng.wait_ge(sem("pa_rec"), i * 16 + k + 1)
            eng.wait_ge(sem("pa_pv"), i * 16 + k + 1 + 16)
            eng.tensor_scalar(att[:, qi, HD * hh:HD * hh + HD], ps[6 + k % 2][:, 0:HD], st_[:, 3:4], None,
                              ALU.mult).then_inc(sem("pa_out"), 1)

        def split_att(i, m):
            src = ps[6 + m % 2][:, 128:256]
            hi = acts_hi[:, ds(i, 1), 128 * m:128 * m + 128].rearrange("p o t -> p (o t)")
            lo = acts_lo[:, ds(i, 1), 128 * m:128 * m + 128].rearrange("p o t -> p (o t)")
            eng.wait_ge(sem("pa_at"), i * 8 + m + 1)
            eng.tensor_scalar(hi, src, 1.0, None, ALU.mult).then_inc(sem("pa_att_hi"), 1)
            eng.wait_ge(sem("pa_att_hi"), i * 8 + m + 1)
            eng.tensor_tensor(lo, src, hi.bitcast(F32), ALU.subtract).then_inc(sem("pa_turned_in"), 1)

        def body(i, first=False, last=False):
            for k in range(STEPS):
                hh, qi = k // 8, k % 8
                if k + 2 < STEPS:
                    maxima(i, k + 2)
                elif not last:
                    maxima(i + 1, k + 2 - STEPS)
                if qi >= 4:
                    cols = 128 * (qi - 3)
                    eng.wait_ge(sem("pa_t5"), i * 8 + 4 * hh + qi - 4 + 1)
                    eng.wait_ge(sem("pa_pv"), i * 16 + k - 1 + 16)
                    eng.tensor_copy(pT[k % 2][:, 512:512 + cols], ps[5][:, 0:cols]).then_inc(sem("pa_c5"), 1)
                if k >= 1:
                    output(i, k - 1)
                if k >= 10:
                    split_att(i, k - 10)
                if k == 0 and not first:
                    split_att(i - 1, 7)
            output(i, STEPS - 1)
            split_att(i, 6)

        maxima(0, 0)
        maxima(0, 1)
        body(0, first=True)
        with eng.Fori(1, PAIRS - 1) as i:
            body(i)
        body(PAIRS - 1, last=True)
        split_att(PAIRS - 1, 7)

    UNITS = 2 * SB

    def sat_sync(eng):
        eng.wait_ge(sem("pa_s"), (PAIRS - 1) * 16 + 8 + 16)
        eng.wait_ge(sem("pa_split"), 2 * PAIRS + 1)
        k_rows = a["cache_k"][0].rearrange("b (m p) h d -> b p m (h d)", p=128)
        v_rows = a["cache_v"][0].rearrange("b (m p) h d -> p (b m) (h d)", p=128)

        def keys(b, g, first=False):
            u = b * 2 + g
            eng.wait_ge(sem("sa_sc"), u * 4 + 1)
            eng.dma_start(kc[g][:], k_rows[b][:, :, 512 * g:512 * g + 512]).then_inc(sem(f"kc_loaded{g}"), 16)
            if first:
                eng.wait_ge(sem("pa_turned_in"), 8 * PAIRS + 8)
                eng.wait_ge(sem("qd_clear"), 1)
            toks = ds(b * ST + TP, ST)
            for half in range(2):
                src = q_dram[512 * g:512 * g + 512, :].rearrange("(p two d) t -> two d p t", two=2, d=HD)[half]
                eng.dma_start(qd[g][64 * half:64 * half + 64, :, ST * half:ST * half + ST], src[:, :, toks]).then_inc(sem(f"kc_loaded{g}"), 16)
            eng.dma_start(kn[g][:], k_dram[512 * g:512 * g + 512, :].rearrange("(p c) t -> c p t", c=128)[:, :, toks]).then_inc(sem(f"kc_loaded{g}"), 16)

        def late(b, g):
            eng.wait_ge(sem("sa_pv"), b * 2 + g + 1)
            eng.dma_start(vn[g][:], o["v_sample"][0][b, :, 8 * g:8 * g + 8, :].rearrange("t h d -> t (h d)")).then_inc(sem(f"sa_small{g}"), 16)
            for h in range(8):
                eng.dma_start(sp[g][ST * h:ST * h + ST, :],
                              past_dram[ds(b * H + 8 * g + h, 1), :].to_broadcast([ST, PAST + ST])).then_inc(sem(f"sa_small{g}"), 16)

        def values(b, g):
            eng.wait_ge(sem("sa_pv"), b * 2 + g + 2)
            eng.dma_start(vc[:], v_rows[:, ds(b * 8, 8), 512 * g:512 * g + 512]).then_inc(sem("vc_loaded"), 16)

        keys(0, 0, first=True)
        late(0, 0)
        with eng.Fori(0, SB - 1) as b:
            keys(b, 1)
            values(b, 0)
            late(b, 1)
            keys(b + 1, 0)
            values(b, 1)
            late(b + 1, 0)
        keys(SB - 1, 1)
        values(SB - 1, 0)
        late(SB - 1, 1)
        values(SB - 1, 1)

    def sat_tensor(eng):
        eng.sem_inc(sem("sa_pv"), 2)
        eng.wait_ge(sem("pa_turned_in"), 8 * PAIRS + 8)

        def scores(b, g, turn_last):
            u = b * 2 + g
            base = 1536 * g

            def turn(p):
                for bk, name in enumerate(("sa_kev6", "sa_kev7")):
                    eng.wait_ge(sem(name), u * 4 + p + 1)
                    for m in range(4):
                        last = eng.transpose(ps[6 + bk][:, 128 * m:128 * m + 128],
                                             kc[g][:, 4 * bk + m, 128 * p:128 * p + 128], ident[:])
                    last.then_inc(sem(("sa_kt6", "sa_kt7")[bk]), 1)

            eng.wait_ge(sem(f"kc_loaded{g}"), b * 64 + 64)
            turn(0)
            for p in range(4):
                if p < 3:
                    turn(p + 1)
                rows = slice(32 * p, 32 * p + 32)
                for bk, name in enumerate(("sa_kev6", "sa_kev7")):
                    eng.wait_ge(sem(name), u * 4 + p + 2)
                    last = eng.matmul(psum[rows, base + 512 * bk:base + 512 * bk + 512], qd[g][:, p, :],
                                      kTs[p % 2][:, 512 * bk:512 * bk + 512], start=True, stop=True)
                if p < 3:
                    last.then_inc(sem("sa_sc"), 1)
                if p == 0 and turn_last:
                    turn_out(b - 1, g)
            eng.wait_ge(sem("sa_out"), u + 1)
            new = slice(base + PAST, base + PAST + ST)
            eng.matmul(psum[:, new], pick_r[:], causal_r[0:ST, 0:ST], start=True, stop=False, skip_group_check=True)
            for p in range(4):
                last = eng.matmul(psum[32 * p:32 * p + 32, new], qd[g][:, p, :], kn[g][:, p, :], start=False, stop=True,
                                  skip_group_check=True)
            last.then_inc(sem("sa_sc"), 1)

        def finish(b, g):
            u = b * 2 + g
            base = 1536 * g
            eng.wait_ge(sem("sa_exp"), u + 1)
            for kb in range(NEWK + 1):
                n = 128 if kb < NEWK else ST
                last = eng.transpose(psum[0:n, base + 128 * kb:base + 128 * kb + 128], sp[g][:, 128 * kb:128 * kb + n], ident[:])
                if kb in (3, 7, 8):
                    last.then_inc(sem(f"sa_pt{kb // 4}"), 1)
            eng.wait_ge(sem("sa_pe2"), u + 1)
            eng.wait_ge(sem("sa_pe1"), u + 1)
            eng.wait_ge(sem("vc_loaded"), u * 16 + 16)
            eng.wait_ge(sem(f"sa_small{g}"), b * 144 + 144)
            for kb in range(NEWK + 1):
                for p in range(4):
                    probs, v = ((spT[:, kb, 32 * p:32 * p + 32], vc[:, kb, 128 * p:128 * p + 128]) if kb < NEWK else
                                (spT[0:ST, kb, 32 * p:32 * p + 32], vn[g][:, 128 * p:128 * p + 128]))
                    last = eng.matmul(psum[32 * p:32 * p + 32, base + 1280:base + 1408], probs, v,
                                      start=(kb == 0), stop=(kb == NEWK), skip_group_check=True)
            last.then_inc(sem("sa_pv"), 1)

        def turn_out(b, g):
            eng.wait_ge(sem("sa_o_rows"), b * 2 + g + 1)
            eng.transpose(psum[:, 1536 * g + 1408:1536 * g + 1536], o_rows[:], ident[:]).then_inc(sem("sa_o_turned"), 1)

        scores(0, 0, False)
        scores(0, 1, False)
        finish(0, 0)
        with eng.Fori(0, SB - 1) as b:
            scores(b + 1, 0, True)
            finish(b, 1)
            scores(b + 1, 1, True)
            finish(b + 1, 0)
        turn_out(SB - 1, 0)
        finish(SB - 1, 1)
        turn_out(SB - 1, 1)

    def sat_scalar(eng):
        eng.sem_inc(sem("sa_kev6"), 1)

        def stage(vb, vg, ub, ug):
            for p in range(4):
                if vb is not None:
                    v = vb * 2 + vg
                    eng.wait_ge(sem("sa_kt6"), v * 4 + p + 1)
                    eng.wait_ge(sem("sa_sc"), v * 4 + p + 4)
                    eng.activation(kTs[p % 2][:, 0:512], ps[6], ACT.Copy).then_inc(sem("sa_kev6"), 1)
                if p == 1 and ub is not None:
                    u = ub * 2 + ug
                    eng.wait_ge(sem("sa_neg"), u + 1)
                    eng.activation(sp[ug][:], sp[ug][:], ACT.Exp, bias=sstat[:, ug, 1:2],
                                   accum_out=sstat[:, ug, 2:3]).then_inc(sem("sa_exp"), 1)
            if ub is not None:
                u = ub * 2 + ug
                base = 1536 * ug
                eng.wait_ge(sem("sa_pt0"), u + 1)
                eng.wait_ge(sem("sa_pv"), u + 2)
                eng.activation(spT[:, 0:4, :], psum[:, base:base + 512].rearrange("p (k n) -> p k n", k=4), ACT.Copy)
                eng.wait_ge(sem("sa_pt2"), u + 1)
                eng.activation(spT[0:ST, NEWK, :], psum[0:ST, base + 1024:base + 1152], ACT.Copy).then_inc(sem("sa_pe2"), 1)

        stage(0, 0, None, None)
        stage(0, 1, 0, 0)
        with eng.Fori(0, SB - 1) as b:
            stage(b + 1, 0, b, 1)
            stage(b + 1, 1, b + 1, 0)
        stage(None, None, SB - 1, 1)

    def sat_vector(eng):
        eng.sem_inc(sem("sa_kev7"), 1)
        eng.sem_inc(sem("sa_out"), 2)
        for g in range(2):
            last = eng.memset(qd[g][:], 0.0)
        last.then_inc(sem("qd_clear"), 1)

        def stage(vb, vg, ub, ug, wb):
            s_ = None if ub is None else sstat[:, ug, :]
            for p in range(4):
                if vb is not None:
                    v = vb * 2 + vg
                    eng.wait_ge(sem("sa_kt7"), v * 4 + p + 1)
                    eng.wait_ge(sem("sa_sc"), v * 4 + p + 4)
                    eng.tensor_copy(kTs[p % 2][:, 512:1024], ps[7]).then_inc(sem("sa_kev7"), 1)
                if p == 0 and ub is not None:
                    u = ub * 2 + ug
                    eng.wait_ge(sem(f"sa_small{ug}"), ub * 144 + 144)
                    eng.wait_ge(sem("sa_sc"), u * 4 + 4 + 5)
                    eng.memset(wait_mark[:, 1:2], 0.0)
                    eng.tensor_tensor_reduce(sp[ug][:], psum[:, 1536 * ug:1536 * ug + PAST + ST], sp[ug][:], 1.0, -3e38,
                                             ALU.add, ALU.max, s_[:, 0:1]).then_inc(sem("sa_stat"), 1)
                    eng.wait_ge(sem("sa_stat"), u * 2 + 1)
                    eng.tensor_scalar(s_[:, 1:2], s_[:, 0:1], -1.0, None, ALU.mult).then_inc(sem("sa_neg"), 1)
                if p == 1 and wb is not None:
                    output(wb, 1 - ug)
                if p == 2 and ub is not None:
                    eng.wait_ge(sem("sa_exp"), u + 1)
                    eng.reciprocal(s_[:, 3:4], s_[:, 2:3]).then_inc(sem("sa_stat"), 1)
            if ub is not None:
                base = 1536 * ug
                eng.wait_ge(sem("sa_pt1"), u + 1)
                eng.wait_ge(sem("sa_pv"), u + 2)
                eng.tensor_copy(spT[:, 4:8, :], psum[:, base + 512:base + 1024].rearrange("p (k n) -> p k n", k=4)).then_inc(sem("sa_pe1"), 1)
                eng.wait_ge(sem("sa_stat"), u * 2 + 2)
                eng.wait_ge(sem("sa_pv"), u + 1 + 2)
                eng.tensor_scalar(o_rows[:], psum[:, base + 1280:base + 1408], s_[:, 3:4], None,
                                  ALU.mult).then_inc(sem("sa_o_rows"), 1)

        def output(b, g):
            u = b * 2 + g
            eng.wait_ge(sem("sa_o_turned"), u + 1)
            out = psum[:, 1536 * g + 1408:1536 * g + 1536].rearrange("p (k n) -> p k n", k=4)
            toks = ds(b * ST + TP, ST)
            blocks = [(out[64 * half:64 * half + 64, :, ST * half:ST * half + ST],
                       acts_hi[64 * half:64 * half + 64, 4 * g:4 * g + 4, toks],
                       acts_lo[64 * half:64 * half + 64, 4 * g:4 * g + 4, toks]) for half in range(2)]
            for src, hi, lo in blocks:
                last = eng.tensor_scalar(hi, src, 1.0, None, ALU.mult)
            last.then_inc(sem("sa_hi"), 1)
            eng.wait_ge(sem("sa_hi"), u + 1)
            for src, hi, lo in blocks:
                last = eng.tensor_tensor(lo, src, hi.bitcast(F32), ALU.subtract)
            last.then_inc(sem("sa_out"), 1)

        stage(0, 0, None, None, None)
        stage(0, 1, 0, 0, None)
        with eng.Fori(0, SB - 1) as b:
            stage(b + 1, 0, b, 1, b)
            stage(b + 1, 1, b + 1, 0, b)
        stage(None, None, SB - 1, 1, SB - 1)
        output(SB - 1, 1)

    def pair_block(name):
        w = kview(a[name][0])
        return lambda j: w[:, :, 256 * j:256 * j + 256]

    def merge_loads_ahead(eng):
        for j in range(2):
            load_block(eng, B_BRA + j, PAIR_SLOTS[j], pair_block("w_br_att")(j))

    def merge_sync(eng):
        eng.wait_ge(sem("sa_out"), UNITS + 2)

        def gate(q):
            tile, c = q // 3, q % 3
            if q >= 2:
                eng.wait_ge(sem("m_free"), q - 1)
            eng.dma_start(gb_t[q % 2][:], gb_dram[128 * tile:128 * tile + 128, tokens_of(c)]).then_inc(sem(f"gate_loaded{q % 2}"), 16)
        gate(0)
        gate(1)
        for d in range(KT):
            eng.dma_start(zt[d][:], z1_dram[128 * d:128 * d + 128, :]).then_inc(sem("z1_loaded"), 16)
        load_block(eng, B_BRA + 2, PAIR_SLOTS[0], pair_block("w_br_att")(2))
        eng.dma_start(x[:].rearrange("p k t -> p (k t)"), x_dram).then_inc(sem("x_again"), 16)
        for q in range(2, 24):
            gate(q)
            if q == 6:
                load_block(eng, B_BRA + 3, PAIR_SLOTS[1], pair_block("w_br_att")(3))
            if q in (12, 18):
                j = q // 6 - 2
                load_block(eng, B_OUT + j, PAIR_SLOTS[j], pair_block("w_out")(j))
        for j in (2, 3):
            load_block(eng, B_OUT + j, PAIR_SLOTS[j % 2], pair_block("w_out")(j))

    def out_bank(at):
        return at % 2 * 3 + at // 2

    def merge_tensor(eng):
        for block0, done in ((B_BRA, "m_free"), (B_OUT, "o_free")):
            for j in range(4):
                for at in range(6):
                    n = out_bank(at) if (block0, j) == (B_OUT, 3) else at
                    t, c = n // 3, n % 3
                    q = 6 * j + n
                    if block0 == B_OUT and j == 0:
                        eng.wait_ge(sem("m_free"), 24)
                        if t == 0:
                            eng.wait_ge(sem("z_lo"), 8 * c + 8)
                    elif j == 0:
                        eng.wait_ge(sem("sa_out"), UNITS + 2)
                    else:
                        eng.wait_ge(sem(done), q - 6 + 1)
                    if at == 0:
                        wait_block(eng, block0 + j)
                    whi, wlo = wcols(PAIR_SLOTS[j % 2][2], t)
                    for k in range(KT):
                        last = mm3(eng, ps[n][:, 0:CH], whi[k], wlo[k], acts_hi[:, k, tokens_of(c)],
                                   acts_lo[:, k, tokens_of(c)], k == 0, k == KT - 1,
                                   sem("w_used") if (at, k) == (0, 0) else None)
                    last.then_inc(sem("m_full"), 1)
                    if (block0, j) == (B_OUT, 3) and at in (3, 5):
                        norm_sum(eng, 2, at // 2 - 1)
        eng.wait_ge(sem("o_free"), 23)
        norm_sum(eng, 2, 2)

    def pair_split(eng, block0, j):
        raw = PAIR_SLOTS[j % 2][0]
        split_hi(eng, block0 + j, PAIR_SLOTS[j % 2], {B_BRA: BRA_RAWS, B_OUT: OUT_RAWS}[block0][raw] + j // 2)

    def merge_scalar(eng):
        for j in range(1, 4):
            pair_split(eng, B_BRA, j)
        pair_split(eng, B_OUT, 0)
        eng.wait_ge(sem("m_free"), 24)
        eng.wait_ge(sem("m_full"), 24)
        for c in range(NC):
            for d in range(KT):
                eng.activation(acts_hi[:, d, tokens_of(c)], zt[d][:, tokens_of(c)], ACT.Copy).then_inc(sem("z_hi"), 1)
        for j in range(1, 4):
            pair_split(eng, B_OUT, j)

    def merge_gpsimd(eng):
        for j in range(1, 4):
            split_lo(eng, B_BRA + j, PAIR_SLOTS[j % 2])
        for j in range(4):
            split_lo(eng, B_OUT + j, PAIR_SLOTS[j % 2])

    def merge_vector(eng):
        for q in range(24):
            j, n = q // 6, q % 6
            tile, c = q // 3, q % 3
            eng.wait_ge(sem("m_full"), q + 1)
            eng.wait_ge(sem(f"gate_loaded{q % 2}"), 16 * (q // 2 + 1 + 4))
            if q == 0:
                eng.wait_ge(sem("z1_loaded"), 16 * KT)
            eng.tensor_tensor(gb_t[q % 2][:], ps[n][:, 0:CH], gb_t[q % 2][:], ALU.mult).then_inc(sem("m_step"), 1)
            eng.wait_ge(sem("m_step"), q + 1)
            z_ = zt[tile][:, tokens_of(c)]
            eng.tensor_tensor(z_, z_, gb_t[q % 2][:], ALU.add).then_inc(sem("m_free"), 1)
        for c in range(NC):
            for d in range(KT):
                eng.wait_ge(sem("z_hi"), 8 * c + d + 1)
                eng.tensor_tensor(acts_lo[:, d, tokens_of(c)], zt[d][:, tokens_of(c)],
                                  acts_hi[:, d, tokens_of(c)].bitcast(F32), ALU.subtract).then_inc(sem("z_lo"), 1)
        eng.wait_ge(sem("x_again"), 16)
        for q in range(24):
            n = out_bank(q % 6) if q >= 18 else q % 6
            d, c = q // 6 * 2 + n // 3, n % 3
            eng.wait_ge(sem("m_full"), 24 + q + 1)
            add_gated(eng, ps[n], x, d, c, 5, "o_free", FF_PAIRS * KT + d)

    def x_set_up(eng, c):
        if c == 0:
            eng.wait_ge(sem("x_moved"), 2 * (T // 128) + CREDIT)
            eng.wait_ge(sem("mod_final"), 7)
            eng.wait_ge(sem("past_stored"), 16)

    def x_after_ffn(f, c):
        return ((f + 1) * FF_PAIRS - 1) * 24 + (c + 1) * 8 + CREDIT

    def x_after_ffn1(eng, c):
        eng.wait_ge(sem("y_free"), x_after_ffn(0, c))

    def x_after_mixer(eng, c):
        eng.wait_ge(sem("o_free"), 18 + 2 * (c + 1))

    def x_after_ffn2(eng, c):
        eng.wait_ge(sem("y_free"), x_after_ffn(1, c))

    def ffn_blocks_ahead(eng, f):
        if f == 1:
            eng.wait_ge(sem("z_lo"), NC * KT)
        ffn_split_hi(eng, f, 0, 0)
        ffn_split_hi(eng, f, 0, 1)

    block = ctx.enter_context(nc.Block())

    @block.sync
    def _(eng):
        setup_sync(eng)
        ffn_sync(eng, 0)
        proj_sync(eng)
        brr_sync(eng)
        att_sync(eng)
        sat_sync(eng)
        merge_sync(eng)
        ffn_sync(eng, 1)
        final_sync(eng)

    @block.scalar
    def _(eng):
        setup_scalar(eng)
        ffn_blocks_ahead(eng, 0)
        norm_scalar(eng, 0, x_set_up)
        ffn_scalar(eng, 0)
        split_hi(eng, B_PROJ, PROJ_SLOTS[0], PROJ_RAWS[0])
        norm_scalar(eng, 1, x_after_ffn1)
        proj_scalar(eng)
        brr_scalar(eng)
        split_head_hi(eng, 0, 0, 0)
        pair_split(eng, B_BRA, 0)
        att_scalar(eng)
        sat_scalar(eng)
        merge_scalar(eng)
        ffn_blocks_ahead(eng, 1)
        norm_scalar(eng, 2, x_after_mixer)
        ffn_scalar(eng, 1)
        final_scalar(eng)

    @block.gpsimd
    def _(eng):
        setup_gpsimd(eng)
        ffn_gpsimd(eng, 0)
        proj_gpsimd(eng)
        brr_gpsimd(eng)
        split_lo(eng, B_BRA, PAIR_SLOTS[0])
        att_gpsimd(eng)
        merge_gpsimd(eng)
        ffn_gpsimd(eng, 1)

    @block.tensor
    def _(eng):
        setup_tensor(eng)
        for c in range(NC):
            norm_sum(eng, 0, c)
        ffn_tensor(eng, 0)
        proj_tensor(eng)
        brr_tensor(eng)
        att_tensor(eng)
        sat_tensor(eng)
        merge_tensor(eng)
        ffn_tensor(eng, 1)
        final_tensor(eng)

    @block.vector
    def _(eng):
        setup_vector(eng)
        norm_vector(eng, 0)
        ffn_vector(eng, 0)
        norm_vector(eng, 1)
        proj_vector(eng)
        brr_vector(eng)
        att_vector(eng)
        sat_vector(eng)
        merge_vector(eng)
        norm_vector(eng, 2)
        ffn_vector(eng, 1)
        final_vector(eng)


_INS = ['x_prompt', 'x_sample', 'cache_k', 'cache_v', 'cache_logf', 'state_conv', 'state_rglru', 'c_prompt',
        'c_sample', 'w_ada', 'b_ada', 'ffn1_norm', 'ffn1_w1', 'ffn1_w3', 'ffn1_w2', 'mix_norm', 'w_in', 'b_fgt',
        'conv_w', 'conv_b', 'rg_wa', 'rg_ba', 'rg_wx', 'rg_bx', 'rg_lam', 'w_br_rnn', 'w_br_att', 'w_out',
        'ffn2_norm', 'ffn2_w1', 'ffn2_w3', 'ffn2_w2', 'final_norm', 'w_ada_f', 'b_ada_f']
_OUTS = [('y_prompt', (1, TP, D)), ('y_sample', (SB, ST, D)),
         ('k_prompt', (1, 1, TP, H, HD)), ('v_prompt', (1, 1, TP, H, HD)), ('logf_prompt', (1, 1, TP, H)),
         ('conv_prompt', (1, 1, CONV_W - 1, D)), ('rglru_prompt', (1, 1, D)),
         ('k_sample', (1, SB, ST, H, HD)), ('v_sample', (1, SB, ST, H, HD)), ('logf_sample', (1, SB, ST, H)),
         ('conv_sample', (1, SB, CONV_W - 1, D)), ('rglru_sample', (1, SB, D))]


def kernel(**inputs):
    import concourse.bacc as bacc
    from concourse.bass_utils import run_bass_kernel_spmd

    nc = bacc.Bacc("TRN2", target_bir_lowering=False, num_devices=1)
    arrays, ins, outs = {}, {}, {}
    for name in _INS:
        arrays[f"in_{name}"] = np.ascontiguousarray(inputs[name])
        ins[name] = nc.dram_tensor(f"in_{name}", arrays[f"in_{name}"].shape, F32, kind="ExternalInput").ap()
    for name, shape in _OUTS:
        outs[name] = nc.dram_tensor(f"out_{name}", shape, F32, kind="ExternalOutput").ap()
    build(nc, ins, outs)
    got = run_bass_kernel_spmd(nc, [arrays], core_ids=[0]).results[0]
    return tuple(got[f"out_{name}"] for name, _ in _OUTS)
```
